# Optimizing a Trainium2 kernel written in Bass

```python
import jax, jax.numpy as jnp
from jax import lax
import numpy as np

D_MODEL = 1024
BATCH = 1
SEQ = 256
DEPTH = 2

CHUNK = 64
Q_BLOCK = 128
ROPE_THETA = 500000.0
EPS = 1e-6

A_HEADS = 4
A_HEAD_DIM = 128
A_ROT = A_HEAD_DIM // 4
IDX_HEADS = 8
IDX_DIM = 64
IDX_ROT = IDX_DIM // 4
TOPK_MAX = 256
B_HEADS = 4
B_NOPE = 128
B_ROPE = 64
B_V = 128
B_Q_RANK = 256
B_KV_RANK = 128
C_HEADS = 4
C_HEAD_DIM = 128
C_LEFT_CHUNKS = 8
C_BAND = (C_LEFT_CHUNKS + 1) * CHUNK
REL_CLIP = 128
N_BRANCH = 3
A_QW = A_HEADS * A_HEAD_DIM
B_OUT = B_HEADS * B_V
C_W = C_HEADS * C_HEAD_DIM
IN_SIZES = (A_QW, A_HEAD_DIM, A_HEAD_DIM, IDX_HEADS * IDX_DIM, IDX_DIM, IDX_HEADS,
            B_Q_RANK, B_KV_RANK, B_ROPE, C_W, C_W, C_W, N_BRANCH * D_MODEL)
N_IN = (A_QW + 2 * A_HEAD_DIM + IDX_HEADS * IDX_DIM + IDX_DIM + IDX_HEADS
        + B_Q_RANK + B_KV_RANK + B_ROPE + 3 * C_W + N_BRANCH * D_MODEL)
N_GROUPS = 4
EXPERTS_PER_GROUP = 8
N_EXPERTS = N_GROUPS * EXPERTS_PER_GROUP
TOP_K_EXPERT = 2
D_EXPERT = 256

kernel_name = "hybrid_chunk_causal_dsa_mla_chunkattn_hmoe"

def rmsnorm(x, g):
    xf = x.astype(jnp.float32)
    y = xf * lax.rsqrt(jnp.mean(xf * xf, axis=-1, keepdims=True) + EPS)
    return (y * g.astype(jnp.float32)).astype(x.dtype)

def rope_tables(seq, rot):
    pos = jnp.arange(seq, dtype=jnp.float32)
    inv = ROPE_THETA ** (-jnp.arange(0, rot, 2, dtype=jnp.float32) / rot)
    ang = pos[:, None] * inv[None, :]
    return jnp.cos(ang), jnp.sin(ang)

def apply_rope(x, cos, sin):
    if x.ndim == 4:
        cos, sin = cos[:, None, :], sin[:, None, :]
    xf = x.astype(jnp.float32)
    x1, x2 = jnp.split(xf, 2, axis=-1)
    out = jnp.concatenate([x1 * cos - x2 * sin, x1 * sin + x2 * cos], axis=-1)
    return out.astype(x.dtype)

def partial_rope(x, cos, sin, rot):
    return jnp.concatenate([apply_rope(x[..., :rot], cos, sin), x[..., rot:]], axis=-1)

def split_cols(z, sizes):
    outs, off = [], 0
    for s in sizes:
        outs.append(z[..., off:off + s])
        off += s
    return outs

def to_blocks(t, nb):
    b = t.shape[0]
    return jnp.moveaxis(t.reshape((b, nb, Q_BLOCK) + t.shape[2:]), 1, 0)

def from_blocks(t):
    t = jnp.moveaxis(t, 0, 1)
    return t.reshape(t.shape[0], t.shape[1] * t.shape[2], -1)

def dsa_mixer(q, k, v, iq, ik, iw):
    bsz, seq = q.shape[0], q.shape[1]
    topk = min(TOPK_MAX, seq // 4)
    nb = seq // Q_BLOCK
    kchunk = jnp.arange(seq) // CHUNK
    qchunk = kchunk.reshape(nb, Q_BLOCK)
    iw = iw.astype(jnp.float32) * (IDX_HEADS ** -0.5)

    def one_block(args):
        qb, iqb, iwb, qc = args
        rel = jax.nn.relu(jnp.einsum('bqhd,bkd->bqhk', iqb, ik).astype(jnp.float32) * (IDX_DIM ** -0.5))
        score = jnp.einsum('bqhk,bqh->bqk', rel, iwb)
        allowed = kchunk[None, :] <= qc[:, None]
        score = jnp.where(allowed[None], score, -jnp.inf)
        _, idx = lax.top_k(score, topk)
        sel_ok = kchunk[idx] <= qc[None, :, None]
        kg = jax.vmap(lambda kk, ii: kk[ii])(k, idx)
        vg = jax.vmap(lambda vv, ii: vv[ii])(v, idx)
        logits = jnp.einsum('bqhd,bqkd->bqhk', qb, kg).astype(jnp.float32) * (A_HEAD_DIM ** -0.5)
        logits = jnp.where(sel_ok[:, :, None, :], logits, -jnp.inf)
        p = jax.nn.softmax(logits, axis=-1).astype(vg.dtype)
        return jnp.einsum('bqhk,bqkd->bqhd', p, vg)

    out = lax.map(one_block, (to_blocks(q, nb), to_blocks(iq, nb), to_blocks(iw, nb), qchunk))
    return from_blocks(out)

def mla_mixer(q_nope, q_rope, k_nope, k_rope, v):
    seq = q_nope.shape[1]
    nb = seq // Q_BLOCK
    kchunk = jnp.arange(seq) // CHUNK
    qchunk = kchunk.reshape(nb, Q_BLOCK)
    scale = (B_NOPE + B_ROPE) ** -0.5

    def one_block(args):
        qn, qr, qc = args
        s = (jnp.einsum('bqhd,bkhd->bhqk', qn, k_nope)
             + jnp.einsum('bqhr,bkr->bhqk', qr, k_rope)).astype(jnp.float32) * scale
        mask = kchunk[None, :] <= qc[:, None]
        s = jnp.where(mask[None, None], s, -jnp.inf)
        p = jax.nn.softmax(s, axis=-1).astype(v.dtype)
        return jnp.einsum('bhqk,bkhd->bqhd', p, v)

    out = lax.map(one_block, (to_blocks(q_nope, nb), to_blocks(q_rope, nb), qchunk))
    return from_blocks(out)

def chunk_band_mixer(q, k, v, rel_table):
    bsz, seq = q.shape[0], q.shape[1]
    n_chunks = seq // CHUNK
    shp = (bsz, n_chunks, CHUNK, C_HEADS, C_HEAD_DIM)
    qc, kc, vc = q.reshape(shp), k.reshape(shp), v.reshape(shp)
    pad = ((0, 0), (C_LEFT_CHUNKS, 0), (0, 0), (0, 0), (0, 0))
    kp, vp = jnp.pad(kc, pad), jnp.pad(vc, pad)
    band_idx = jnp.arange(n_chunks)[:, None] + jnp.arange(C_LEFT_CHUNKS + 1)[None, :]
    kb = kp[:, band_idx].reshape(bsz, n_chunks, C_BAND, C_HEADS, C_HEAD_DIM)
    vb = vp[:, band_idx].reshape(bsz, n_chunks, C_BAND, C_HEADS, C_HEAD_DIM)
    valid = jnp.repeat(band_idx >= C_LEFT_CHUNKS, CHUNK, axis=1)
    qi = jnp.arange(CHUNK)
    kj = jnp.arange(C_BAND)
    dist = C_LEFT_CHUNKS * CHUNK + qi[:, None] - kj[None, :]
    bias = rel_table[:, jnp.clip(dist, -REL_CLIP, REL_CLIP) + REL_CLIP].astype(jnp.float32)
    s = jnp.einsum('bcqhd,bckhd->bchqk', qc, kb).astype(jnp.float32) * (C_HEAD_DIM ** -0.5) + bias[None, None]
    s = jnp.where(valid[None, :, None, None, :], s, -jnp.inf)
    p = jax.nn.softmax(s, axis=-1).astype(vb.dtype)
    out = jnp.einsum('bchqk,bckhd->bcqhd', p, vb)
    return out.reshape(bsz, seq, C_W)

def hier_moe(h, w_group, b_group, w_router, b_router, w_gate, w_up, w_down):
    bsz, seq, d = h.shape
    t = h.reshape(-1, d)
    p_grp = jax.nn.softmax((t @ w_group).astype(jnp.float32) + b_group.astype(jnp.float32), axis=-1)
    pg, gsel = lax.top_k(p_grp, 1)
    e_logits = ((t @ w_router).astype(jnp.float32) + b_router.astype(jnp.float32)).reshape(-1, N_GROUPS, EXPERTS_PER_GROUP)
    e_in = jnp.take_along_axis(e_logits, gsel[:, :, None], axis=1)[:, 0]
    pe, esel = lax.top_k(jax.nn.softmax(e_in, axis=-1), TOP_K_EXPERT)
    wts = pg * pe / jnp.sum(pe, axis=-1, keepdims=True)
    gidx = gsel * EXPERTS_PER_GROUP + esel
    combine = jnp.sum(jax.nn.one_hot(gidx, N_EXPERTS, dtype=jnp.float32) * wts[..., None], axis=1)
    a = jnp.einsum('td,edf->tef', t, w_gate)
    u = jnp.einsum('td,edf->tef', t, w_up)
    hh = jax.nn.silu(a) * u * combine[:, :, None].astype(t.dtype)
    y = jnp.einsum('tef,efd->td', hh, w_down)
    return y.reshape(bsz, seq, d)

def setup_inputs(seed: int = 0) -> dict:
    key = jax.random.key(seed)
    ks = jax.random.split(key, 24)
    L = DEPTH
    f32 = jnp.float32

    def nrm(k, shape, fan):
        return jax.random.normal(k, shape, f32) * (fan ** -0.5)

    def gain(k, shape):
        return 1.0 + 0.05 * jax.random.normal(k, shape, f32)

    return {
        "x": jax.random.normal(ks[0], (BATCH, SEQ, D_MODEL), f32),
        "attn_norm_g": gain(ks[1], (L, D_MODEL)),
        "w_in": nrm(ks[2], (L, D_MODEL, N_IN), D_MODEL),
        "b_q_norm_g": gain(ks[3], (L, B_Q_RANK)),
        "b_w_uq": nrm(ks[4], (L, B_Q_RANK, B_HEADS * (B_NOPE + B_ROPE)), B_Q_RANK),
        "b_kv_norm_g": gain(ks[5], (L, B_KV_RANK)),
        "b_w_ukv": nrm(ks[6], (L, B_KV_RANK, B_HEADS * (B_NOPE + B_V)), B_KV_RANK),
        "c_rel_bias": 0.2 * jax.random.normal(ks[7], (L, C_HEADS, 2 * REL_CLIP + 1), f32),
        "w_proj_a": nrm(ks[8], (L, A_QW, D_MODEL), A_QW),
        "w_proj_b": nrm(ks[9], (L, B_OUT, D_MODEL), B_OUT),
        "w_proj_c": nrm(ks[10], (L, C_W, D_MODEL), C_W),
        "w_out": nrm(ks[11], (L, D_MODEL, D_MODEL), D_MODEL),
        "ffn_norm_g": gain(ks[12], (L, D_MODEL)),
        "w_group": nrm(ks[13], (L, D_MODEL, N_GROUPS), D_MODEL),
        "b_group": 0.01 * jax.random.normal(ks[14], (L, N_GROUPS), f32),
        "w_router": nrm(ks[15], (L, D_MODEL, N_EXPERTS), D_MODEL),
        "b_router": 0.01 * jax.random.normal(ks[16], (L, N_EXPERTS), f32),
        "w_gate": nrm(ks[17], (L, N_EXPERTS, D_MODEL, D_EXPERT), D_MODEL),
        "w_up": nrm(ks[18], (L, N_EXPERTS, D_MODEL, D_EXPERT), D_MODEL),
        "w_down": nrm(ks[19], (L, N_EXPERTS, D_EXPERT, D_MODEL), D_EXPERT),
        "final_norm_g": gain(ks[20], (D_MODEL,)),
    }

def reference(x, attn_norm_g, w_in, b_q_norm_g, b_w_uq, b_kv_norm_g, b_w_ukv, c_rel_bias,
              w_proj_a, w_proj_b, w_proj_c, w_out, ffn_norm_g, w_group, b_group,
              w_router, b_router, w_gate, w_up, w_down, final_norm_g):
    bsz, seq, d = x.shape
    cos_a, sin_a = rope_tables(seq, A_ROT)
    cos_i, sin_i = rope_tables(seq, IDX_ROT)
    cos_b, sin_b = rope_tables(seq, B_ROPE)
    for l in range(DEPTH):
        h = rmsnorm(x, attn_norm_g[l])
        z = h @ w_in[l]
        (aq, ak, av, aiq, aik, aiw, bcq, bckv, bkr, cq, ck, cv, gl) = split_cols(z, IN_SIZES)
        aq = partial_rope(aq.reshape(bsz, seq, A_HEADS, A_HEAD_DIM), cos_a, sin_a, A_ROT)
        ak = partial_rope(ak, cos_a, sin_a, A_ROT)
        aiq = partial_rope(aiq.reshape(bsz, seq, IDX_HEADS, IDX_DIM), cos_i, sin_i, IDX_ROT)
        aik = partial_rope(aik, cos_i, sin_i, IDX_ROT)
        o_a = dsa_mixer(aq, ak, av, aiq, aik, aiw)
        qb = (rmsnorm(bcq, b_q_norm_g[l]) @ b_w_uq[l]).reshape(bsz, seq, B_HEADS, B_NOPE + B_ROPE)
        q_nope = qb[..., :B_NOPE]
        q_rope = apply_rope(qb[..., B_NOPE:], cos_b, sin_b)
        kvb = (rmsnorm(bckv, b_kv_norm_g[l]) @ b_w_ukv[l]).reshape(bsz, seq, B_HEADS, B_NOPE + B_V)
        k_nope, vb = kvb[..., :B_NOPE], kvb[..., B_NOPE:]
        k_rope = apply_rope(bkr, cos_b, sin_b)
        o_b = mla_mixer(q_nope, q_rope, k_nope, k_rope, vb)
        hs = (bsz, seq, C_HEADS, C_HEAD_DIM)
        o_c = chunk_band_mixer(cq.reshape(hs), ck.reshape(hs), cv.reshape(hs), c_rel_bias[l])
        g = jax.nn.sigmoid(gl.astype(jnp.float32)).reshape(bsz, seq, N_BRANCH, d).astype(x.dtype)
        mix = (g[:, :, 0] * (o_a @ w_proj_a[l]) + g[:, :, 1] * (o_b @ w_proj_b[l])
               + g[:, :, 2] * (o_c @ w_proj_c[l]))
        x = x + mix @ w_out[l]
        x = x + hier_moe(rmsnorm(x, ffn_norm_g[l]), w_group[l], b_group[l], w_router[l], b_router[l],
                         w_gate[l], w_up[l], w_down[l])
    return rmsnorm(x, final_norm_g)


_drawn_inputs = setup_inputs


def setup_inputs(seed=0):
    import zlib

    import numpy as np

    out = dict(_drawn_inputs(seed))
    spreads = {}
    factors = {'b_q_norm_g': 4.706, 'b_group': 2.835}
    for name, (base, spread) in spreads.items():
        noise = np.random.default_rng([zlib.crc32(name.encode()), seed]).standard_normal(out[name].shape)
        drawn = base * np.exp(spread * noise) if base else spread * noise
        out[name] = __import__('jax').numpy.asarray(drawn.astype(out[name].dtype))
    for name, factor in factors.items():
        out[name] = (out[name] * factor).astype(out[name].dtype)
    return out
```

```python
from contextlib import ExitStack

import numpy as np
import concourse.bass as bass
from concourse import mybir

F32 = mybir.dt.float32
U32 = mybir.dt.uint32
I32 = mybir.dt.int32
ALU = mybir.AluOpType
ACT = mybir.ActivationFunctionType
AX_X = mybir.AxisListType.X

P = 128
L = 2
D = 1024
T = 256
TT = T // P
KC = D // P
CHUNK = 64
EPS = 1e-6
H = 4
HD = 128
IH, ID = 8, 64
TOPK = 64
BQ, BKV, BR = 256, 128, 64
A_ROT, I_ROT = HD // 4, ID // 4
N_IN = 6408
REL = 128
G, EPG = 4, 8
E = G * EPG
FE = 256
SLOTS = 32
XG = P // SLOTS
NG = E // XG
LATE_FROM = SLOTS
SCORE_GATE = 9
NEG = -1.0e30
REPL = -3.0e38

O_AQ, O_KV, O_IQ, O_IK, O_IW = 0, 512, 768, 1280, 1344
O_BQ, O_BKV, O_BKR = 1352, 1608, 1736
O_CQ, O_CK, O_CV, O_GL = 1800, 2312, 2824, 3336

RING = 6
BLK = 4096
NT = 18
PER_SET = 6
PER_LAYER = NT + PER_SET * NG
TOKEN_BLOCKS = [(0, 512), (512, 1024), (1024, 1352), (1352, 1800)]
B_CQ, B_CK, B_CV, B_GL, B_PROJ, B_WO = 4, 5, 6, 7, 13, 16
PROJ_ORDER = "cba"
SET_ORDER = [("gu", 0), ("gu", 1), ("gu", 2), ("gu", 3), ("d", 0), ("d", 2)]
GU_SLOT = [0, 1, 2, 3]
D_SLOT = [4, 4, 5, 5]

C_ID, C_U, C_ONE, C_M = 0, 128, 256, 384
C_CA, C_SA = 640, 640 + 2 * A_ROT
C_CI, C_SI = C_SA + 2 * A_ROT, C_SA + 2 * A_ROT + 2 * I_ROT
C_CB, C_SB = C_SI + 2 * I_ROT, C_SI + 2 * I_ROT + 2 * BR
C_IOTA = C_SB + 2 * BR
NCONST = C_IOTA + SLOTS
S_GA, S_GF, S_GQ, S_GKV, S_R = 0, KC, 2 * KC, 2 * KC + 2, 2 * KC + 3
NSMALL = S_R + KC * (G + E)
NUP = 2 * H * (HD + BR) + H * 2 * HD


def shape_constants():
    c = np.zeros((P, NCONST), np.float32)
    c[:, C_ID:C_ID + P] = np.eye(P)
    c[:, C_U:C_U + P] = np.triu(np.ones((P, P)), 1)
    c[:, C_ONE:C_ONE + P] = 1.0
    c[:CHUNK, C_M + 3 * CHUNK:C_M + 4 * CHUNK] = NEG
    for rot, oc, os in ((A_ROT, C_CA, C_SA), (I_ROT, C_CI, C_SI), (BR, C_CB, C_SB)):
        pos = np.arange(T, dtype=np.float32)
        inv = np.float32(500000.0) ** (-np.arange(0, rot, 2, dtype=np.float32) / np.float32(rot))
        ang = pos[:, None] * inv[None, :].astype(np.float32)
        cos, sin = np.cos(ang), np.sin(ang)
        for tt in range(TT):
            r = slice(tt * P, tt * P + P)
            c[:, oc + tt * rot:oc + (tt + 1) * rot] = np.concatenate([cos[r], cos[r]], 1)
            c[:, os + tt * rot:os + (tt + 1) * rot] = np.concatenate([-sin[r], sin[r]], 1)
    c[:, C_IOTA:C_IOTA + SLOTS] = np.arange(SLOTS)
    c[:, C_IOTA + LATE_FROM:C_IOTA + SLOTS] = -5.0
    return c


def build(nc, a):
    ctx = ExitStack()
    with ctx:
        def sb(name, shape, dt=F32):
            return ctx.enter_context(nc.sbuf_tensor(name, shape, dt))

        counts = {}

        def sig(name, per, unit=1):
            handle = ctx.enter_context(nc.semaphore(name))
            counts[handle.name] = per, unit
            return handle

        def at(signal, l, n=None):
            per, unit = counts[signal.name]
            return (l * per + (per if n is None else n)) * unit

        ps = ctx.enter_context(nc.psum_tensor("ps", [P, 8, 512], F32))

        ring = sb("ring", [P, RING, BLK])
        x = sb("x", [P, TT, D])
        xn = sb("xn", [P, TT, D])
        hT = sb("hT", [P, KC, T])
        cst = sb("cst", [P, NCONST])
        small = sb("small", [P, L, NSMALL])
        rbias = sb("rbias", [P, L, G + E])
        wup = sb("wup", [P, NUP])
        cbias = sb("cbias", [P, H, T])
        gates = sb("gates", [P, 3 * KC, T])
        aqT = sb("aqT", [P, H, T])
        keysT = sb("keysT", [P, 2, T])
        iqT = sb("iqT", [P, IH // 2, T])
        bcqT = sb("bcqT", [P, 2, T])
        bckvT = sb("bckvT", [P, T])
        qnT = sb("qnT", [P, H, T])
        knT = sb("knT", [P, H, T])
        qrT = sb("qrT", [P, 2, T])
        krT = sb("krT", [P, T])
        vB = sb("vB", [P, TT, H * HD])
        cqT = sb("cqT", [P, H, T])
        ckT = sb("ckT", [P, H, T])
        cv = sb("cv", [P, TT, H * HD])
        zkv = sb("zkv", [P, TT, 2 * HD])
        st = sb("st", [P, 64])
        st8 = sb("st8", [P, 8])
        flag = sb("flag", [P, 1], I32)

        gf = gates[:].rearrange("p c t -> p (c t)")
        zaq = gf[:, 0:1024].rearrange("p (a n) -> p a n", a=TT)
        ziq = gf[:, 1024:2048].rearrange("p (a n) -> p a n", a=TT)
        zb = gf[:, 2048:2816].rearrange("p (a n) -> p a n", a=TT)
        zik = gf[:, 2816:3072].rearrange("p (a s n) -> p a s n", a=TT, s=2)
        zkr = gf[:, 3072:3328].rearrange("p (a s n) -> p a s n", a=TT, s=2)
        ziw = gf[:, 3328:3344].rearrange("p (a n) -> p a n", a=TT)
        score = gf[:, SCORE_GATE * 512:SCORE_GATE * 512 + 512].rearrange("p (a n) -> p a n", a=TT)
        logits = iqT[:].rearrange("p s t -> p s t")
        xnf = xn[:].rearrange("p a d -> p (a d)")
        probsT = xnf[:, 0:1024].rearrange("p (k h q) -> p k h q", k=2, h=H)
        rope1 = xnf[:, 1024:1536]
        rope2 = xnf[:, 1536:2048]
        probs = xnf[:, 1024:2048].rearrange("p (h k) -> p h k", h=H)
        relu = xnf[:, 1024:2048].rearrange("p (b n) -> p b n", b=2)
        zqr = xnf[:, 0:512].rearrange("p (a n) -> p a n", a=TT)
        mixT = xnf.rearrange("p (c t) -> p c t", c=KC)
        sel = gf[:, 0:2048].rearrange("p (a n) -> p a n", a=TT)
        selwT = gf[:, 2048:4096].rearrange("p (g t) -> p g t", g=NG)
        xg = gf[:, 4096:5120].rearrange("p (k s) -> p k s", k=KC)
        yg = gf[:, 5120:6144].rearrange("p d -> p d")
        cf = ckT[:].rearrange("p h t -> p (h t)")
        selw = vB[:].rearrange("p a n -> p (a n)")
        selw1 = knT[:].rearrange("p h t -> p (h t)")
        selws = [selw, selw1]
        sw = cf[:, 0:256]
        hid = cf[:, 256:512]
        th = cf[:, 512:768]
        hidT = cf[:, 768:1024].rearrange("p (f s) -> p f s", f=2)
        cvf = cv[:].rearrange("p a n -> p (a n)")
        lg = cvf[:, 0:72].rearrange("p (a n) -> p a n", a=TT)
        g8 = cvf[:, 72:88].rearrange("p (a n) -> p a n", a=TT)
        m8 = cvf[:, 88:104].rearrange("p (a n) -> p a n", a=TT)
        i8 = cvf[:, 104:120].rearrange("p (a n) -> p a n", a=TT).bitcast(U32)
        prod = cvf[:, 120:184].rearrange("p (a n) -> p a n", a=TT)
        ein = cvf[:, 184:200].rearrange("p (a n) -> p a n", a=TT)
        e8 = cvf[:, 200:216].rearrange("p (a n) -> p a n", a=TT)
        j8 = cvf[:, 216:232].rearrange("p (a n) -> p a n", a=TT).bitcast(U32)
        fi = cvf[:, 232:240].rearrange("p (a n) -> p a n", a=TT)
        ohg = cvf[:, 240:248].rearrange("p (a n) -> p a n", a=TT)
        eg = cvf[:, 248:256].rearrange("p (a n) -> p a n", a=TT)
        rw = cvf[:, 256:272].rearrange("p (n a) -> p n a", a=TT)
        oh1 = cvf[:, 272:288].rearrange("p (a n) -> p a n", a=TT)
        oh2 = cvf[:, 288:304].rearrange("p (a n) -> p a n", a=TT)
        ce = cvf[:, 304:320].rearrange("p (a n) -> p a n", a=TT)
        comb = cvf[:, 320:384].rearrange("p (a n) -> p a n", a=TT)
        asg = cvf[:, 384:448].rearrange("p (a n) -> p a n", a=TT)
        rk = cvf[:, 448:512].rearrange("p (a n) -> p a n", a=TT)
        late = cvf[:, 512:576].rearrange("p (a n) -> p a n", a=TT)
        cnt = cvf[:, 576:577]
        thl = aqT[:].rearrange("p h t -> p (h t)")[:, 0:512].rearrange("p (a n) -> p a n", a=TT)
        hidl = cqT[:].rearrange("p h t -> p (h t)")[:, 0:512].rearrange("p (a n) -> p a n", a=TT)
        hidTl = cqT[:].rearrange("p h t -> p (h t)")[:, 512:1024].rearrange("p (f t) -> p f t", f=2)

        ident = cst[:, C_ID:C_ID + P]
        tri = cst[:, C_U:C_U + P]
        ones = cst[:, C_ONE:C_ONE + P]
        iota = cst[:, C_IOTA:C_IOTA + SLOTS]

        def mask_of(qt):
            return cst[:, C_M + P:C_M + 2 * P] if qt == 0 else cst[:, C_M:C_M + T]

        def keys(qt):
            return (qt + 1) * P

        consts_in = sig("consts_in", 0, 16)
        rbias_in = sig("rbias_in", 0, 16)
        fgain_in = sig("fgain_in", 0, 16)
        up_in = sig("up_in", 1, 16)
        cb_in = sig("cb_in", 1, 16)
        slot_in = [sig(f"slot_in{s}", PER_LAYER // RING, 16) for s in range(RING)]
        xn_ready = sig("xn_ready", 4)
        xnT_ps = sig("xnT_ps", 8)
        hT_dve = sig("hT_dve", 8)
        hT_act = sig("hT_act", 8)
        var_ready = sig("var_ready", 3)
        rstd_ready = sig("rstd_ready", 3)
        tok_ps = sig("tok_ps", 8)
        z_act = sig("z_act", 10)
        z_dve = sig("z_dve", 10)
        ckq_ps = sig("ckq_ps", 4)
        cv_ps = sig("cv_ps", 2)
        c_sb = sig("c_sb", 6)
        roped = sig("roped", 6)
        bn_ready = sig("bn_ready", 4)
        turn_ps = sig("turn_ps", 9)
        turn_act = sig("turn_act", 5)
        turn_dve = sig("turn_dve", 5)
        idx_ps = sig("idx_ps", 6)
        relu_sb = sig("relu_sb", 6)
        idx_used = sig("idx_used", 6)
        b_ps = sig("b_ps", 7)
        b_sb = sig("b_sb", 7)
        score_ps = sig("score_ps", 6)
        logit_sb = sig("logit_sb", 6)
        nmax_sb = sig("nmax_sb", 6)
        exp_sb = sig("exp_sb", 24)
        probs_sb = sig("probs_sb", 6)
        probsT_ps = sig("probsT_ps", 9)
        probsT_sb = sig("probsT_sb", 9)
        o_ps = sig("o_ps", 6)
        o_sb = sig("o_sb", 6)
        gate_ps = sig("gate_ps", 12)
        gate_sb = sig("gate_sb", 12)
        proj_ps = sig("proj_ps", 12)
        proj_used = sig("proj_used", 12)
        wo_half = sig("wo_half", 1)
        wo_ps = sig("wo_ps", 4)
        cb_masked = sig("cb_masked", 1)
        route_ps = sig("route_ps", 1)
        gdiff_sb = sig("gdiff_sb", 2)
        gexp_sb = sig("gexp_sb", 2)
        asg_sb = sig("asg_sb", 1)
        rank_ps = sig("rank_ps", 1)
        flag_sb = sig("flag_sb", 1)
        sel_sb = sig("sel_sb", 2)
        selw_sb = sig("selw_sb", 2)
        selwT_ps = sig("selwT_ps", 4)
        selwT_sb = sig("selwT_sb", 4)
        gath_ps = sig("gath_ps", 2 * NG)
        xg_sb = sig("xg_sb", 2 * NG)
        gu_ps = sig("gu_ps", NG)
        tanh_sb = sig("tanh_sb", NG)
        silu_sb = sig("silu_sb", NG)
        hid_sb = sig("hid_sb", NG)
        hidT_ps = sig("hidT_ps", NG)
        hidT_sb = sig("hidT_sb", NG)
        down_ps = sig("down_ps", NG)
        yg_sb = sig("yg_sb", 2 * NG)
        sw_sb = sig("sw_sb", NG)
        comb_ps = sig("comb_ps", 2 * NG)
        x_added = sig("x_added", 4 + 4 * NG)
        late_gu_in = [sig(f"late_gu_in{l}", 0, 16) for l in range(L)]
        late_d_in = [sig(f"late_d_in{l}", 0, 16) for l in range(L)]
        late_gu_ps = [sig(f"late_gu_ps{l}", 0) for l in range(L)]
        late_tanh = [sig(f"late_tanh{l}", 0) for l in range(L)]
        late_silu = [sig(f"late_silu{l}", 0) for l in range(L)]
        late_hid = [sig(f"late_hid{l}", 0) for l in range(L)]
        late_hidT_ps = [sig(f"late_hidT_ps{l}", 0) for l in range(L)]
        late_hidT_sb = [sig(f"late_hidT_sb{l}", 0) for l in range(L)]
        late_added = [sig(f"late_added{l}", 0) for l in range(L)]
        late_done = [sig(f"late_done{l}", 0) for l in range(L)]
        out_ready = sig("out_ready", 0)
        out_done = sig("out_done", 0, 16)

        def slot(s):
            return ring[:, s, :]

        def slot_k(s, n, k=KC):
            return ring[:, s, 0:k * n].rearrange("p (k n) -> p k n", k=k)

        def freed(l, i):
            if i < 4:
                return tok_ps, l, 2 * i + 2
            if i in (B_CQ, B_CK):
                return ckq_ps, l, 2 * (i - B_CQ) + 2
            if i == B_CV:
                return cv_ps, l, 2
            if i < B_PROJ:
                return gate_ps, l, 2 * (i - B_GL) + 2
            if i < B_WO:
                return proj_ps, l, 4 * (i - B_PROJ) + 4
            if i == B_WO:
                return wo_half, l, 1
            if i == B_WO + 1:
                return wo_ps, l, 4
            g, s = divmod(i - NT, PER_SET)
            return (gu_ps if SET_ORDER[s][0] == "gu" else down_ps), l, g + 1

        def loop_sets(eng, body):
            body(0, True, False)
            with eng.Fori(1, NG - 1) as g:
                body(g, False, False)
            body(NG - 1, False, True)

        pool_const = sig("pool_const", 0)
        step = ctx.enter_context(nc.semaphore("step"))
        taken = [0]

        def steps(n):
            taken[0] += n
            return taken[0]

        fgain = gf[:, 0:D]
        UNITS = [("c", 0), ("c", 1), ("b", 0), ("b", 1), ("a", 0), ("a", 1)]
        HEAD_AT = {"a": [0, 1, 2, 3], "b": [0, 2, 1, 3], "c": [0, 1, 2, 3]}
        PT_COUNT = [1, 3, 4, 6, 7, 9]
        SELW_BANKS = [2, 3, 6, 7]

        def copy_tokens(eng, l, tt, signal, copy):
            for i in range(4):
                eng.wait_ge(tok_ps, at(tok_ps, l, 2 * i + tt + 1))
                b = ps[:, (4 + 2 * i + tt) % 8, :]
                if i == 0:
                    moves = [(zaq[:, tt, :], b)]
                elif i == 1:
                    moves = [(zkv[:, tt, :], b[:, 0:256]), (ziq[:, tt, 0:256], b[:, 256:512])]
                elif i == 2:
                    moves = [(ziq[:, tt, 256:512], b[:, 0:256]), (zik[:, tt, 0, :], b[:, 256:320]),
                             (zik[:, tt, 1, :], b[:, 256:320]), (ziw[:, tt, :], b[:, 320:328])]
                else:
                    moves = [(zb[:, tt, :], b[:, 0:384]), (zkr[:, tt, 0, :], b[:, 384:448]),
                             (zkr[:, tt, 1, :], b[:, 384:448])]
                for dst, src in moves:
                    copy(dst, src).then_inc(signal, 1)

        def any_late(eng, l):
            eng.wait_ge(flag_sb, at(flag_sb, l))
            return eng.value_load(flag[0:1, 0:1], min_val=0, max_val=1) > 0

        block = ctx.enter_context(nc.Block())

        @block.sync
        def _(sp):
            sp.dma_start(x[:], a["x"].rearrange("b (t p) d -> p (b t) d", p=P)).then_inc(consts_in, 16)
            sp.dma_start(cst[:], a["consts"]).then_inc(consts_in, 16)
            sp.dma_start(small[:], a["small"].rearrange("l p n -> p l n")).then_inc(consts_in, 16)
            stream = a["stream"]

            def late_stream(l):
                with sp.If(any_late(sp, l)):
                    sp.wait_ge(gu_ps, at(gu_ps, l))
                    sp.wait_ge(down_ps, at(down_ps, l))

                    with sp.Fori(0, NG) as g:
                        for j in range(XG):
                            sp.wait_ge(late_done[l], at(late_done[l], 0, XG * g + (j + 1)))
                            i = g * PER_SET + (l * PER_LAYER + NT)
                            src = a["stream"][bass.ds(i + GU_SLOT[j], 1)].rearrange("b p n -> p (b n)")
                            sp.dma_start(ring[:, 0, :], src).then_inc(late_gu_in[l], 16)
                            src = a["stream"][bass.ds(i + D_SLOT[j], 1)].rearrange("b p n -> p (b n)")
                            h = (j % 2) * BLK // 2
                            sp.dma_start(ring[:, 1, 0:BLK // 2], src[:, h:h + BLK // 2]).then_inc(late_d_in[l], 16)
                    sp.wait_ge(late_done[l], at(late_done[l], 0, E + 1))

            for l in range(L):
                for i in range(NT):
                    s = i % RING
                    if l or i >= RING:
                        j = l * PER_LAYER + i - RING
                        f, fl, fn = freed(j // PER_LAYER, j % PER_LAYER)
                        sp.wait_ge(f, at(f, fl, fn))
                    n = BLK
                    if i < len(TOKEN_BLOCKS):
                        n = KC * (TOKEN_BLOCKS[i][1] - TOKEN_BLOCKS[i][0])
                    sp.dma_start(ring[:, s, 0:n], stream[l * PER_LAYER + i, :, 0:n]).then_inc(slot_in[s], 16)

                def one_set(g, first, last):
                    for s, (kind, j) in enumerate(SET_ORDER):
                        if first:
                            f, fl, fn = freed(l, NT - PER_SET + s)
                            sp.wait_ge(f, at(f, fl, fn))
                        else:
                            sp.wait_ge(gu_ps if kind == "gu" else down_ps, at(gu_ps if kind == "gu" else down_ps, l, g))
                        i = g * PER_SET + (l * PER_LAYER + NT + s)
                        src = stream[bass.ds(i, 1)].rearrange("b p n -> p (b n)")
                        sp.dma_start(ring[:, s, :], src).then_inc(slot_in[s], 16)
                loop_sets(sp, one_set)
                late_stream(l)

            sp.wait_ge(out_ready, at(out_ready, 0, 2))
            sp.dma_start(a["out"].rearrange("b (t p) d -> p (b t) d", p=P), xn[:]).then_inc(out_done, 16)
            sp.wait_ge(out_done, at(out_done, 0, 1))

        @block.gpsimd
        def _(pool):
            pool.memset(st[:, 40:44], -0.5).then_inc(pool_const, 1)
            pool.wait_ge(pool_const, at(pool_const, 0, 1))
            pool.dma_start(rbias[:], a["rbias"].rearrange("l n -> (l n)").partition_broadcast(P)
                           .rearrange("p (l n) -> p l n", l=L)).then_inc(rbias_in, 16)
            for l in range(L):
                if l:
                    pool.wait_ge(b_ps, at(b_ps, l - 1))
                    pool.wait_ge(logit_sb, at(logit_sb, l - 1, 2))
                pool.dma_start(wup[:], a["up"][l]).then_inc(up_in, 16)
                pool.dma_start(cbias[:].rearrange("p h t -> p (h t)"), a["rel"][l]).then_inc(cb_in, 16)
                pool.wait_ge(cb_in, at(cb_in, l))
                if not l:
                    pool.wait_ge(consts_in, at(consts_in, 0, 3))
                for h in range(H):
                    pool.tensor_tensor(cbias[:, h, :], cbias[:, h, :], mask_of(1), ALU.add).then_inc(cb_masked, 1)
                for n, (lo, hi) in enumerate(((0, 2), (4, 8), (0, 2))):
                    pool.wait_ge(var_ready, at(var_ready, l, n + 1))
                    pool.tensor_tensor(st[:, lo + 8:hi + 8], st[:, lo:hi],
                                                     st[:, 40:40 + hi - lo], ALU.pow).then_inc(rstd_ready, 1)
            pool.wait_ge(var_ready, at(var_ready, L, 1))
            pool.tensor_tensor(st[:, 8:10], st[:, 0:2], st[:, 40:42], ALU.pow).then_inc(rstd_ready, 1)
            pool.wait_ge(x_added, at(x_added, L - 1))
            pool.dma_start(fgain, a["final_gain"].partition_broadcast(P)).then_inc(fgain_in, 16)

        @block.tensor
        def _(pe):
            def mm(out, lhsT, rhs, start=True, stop=True):
                return pe.matmul(out, lhsT, rhs, start=start, stop=stop)

            def late_products(l):
                with pe.If(any_late(pe, l)):
                    pe.wait_ge(down_ps, at(down_ps, l))
                    pe.sem_inc(late_done[l], 1)

                    with pe.Fori(0, NG) as g:
                        for j in range(XG):
                            e1 = XG * g + (j + 1)
                            pe.wait_ge(late_gu_in[l], at(late_gu_in[l], 0, e1))
                            w = ring[:, 0, :].rearrange("p (k n) -> p k n", k=KC)
                            for tt in range(TT):
                                for k in range(KC):
                                    ins = pe.matmul(ps[:, tt, :], hT[:, k, tt * P:(tt + 1) * P], w[:, k, :],
                                                    start=k == 0, stop=k == KC - 1)
                            ins.then_inc(late_gu_ps[l], 1)
                            pe.wait_ge(late_hid[l], at(late_hid[l], 0, TT * XG * g + TT * (j + 1)))
                            for f in range(2):
                                for tt in range(TT):
                                    ins = pe.transpose(ps[:, 2, f * T + tt * P:f * T + (tt + 1) * P],
                                                       hidl[:, tt, f * P:(f + 1) * P], ident)
                            ins.then_inc(late_hidT_ps[l], 1)
                            pe.wait_ge(late_hidT_sb[l], at(late_hidT_sb[l], 0, e1))
                            pe.wait_ge(late_d_in[l], at(late_d_in[l], 0, e1))
                            w = ring[:, 1, 0:BLK // 2].rearrange("p (f n) -> p f n", f=2)
                            for tt in range(TT):
                                for half in range(2):
                                    for f in range(2):
                                        ins = pe.matmul(ps[:, 4 + 2 * tt + half, :], hidTl[:, f, tt * P:(tt + 1) * P],
                                                        w[:, f, half * 512:(half + 1) * 512], start=f == 0, stop=f == 1)
                            ins.then_inc(late_done[l], 1)

            def slot_k(s, n, k=KC):
                return ring[:, s, 0:k * n].rearrange("p (k n) -> p k n", k=k)

            def arrived(l, i):
                pe.wait_ge(slot_in[i % RING], at(slot_in[i % RING], l, i // RING + 1))

            def turn_norm(l, half):
                for tt in range(TT):
                    pe.wait_ge(xn_ready, at(xn_ready, l, 2 * half + tt + 1))
                for k in range(KC):
                    for tt in range(TT):
                        o = (k % 2) * T + tt * P
                        ins = pe.transpose(ps[:, k // 2, o:o + P], xn[:, tt, k * P:(k + 1) * P], ident)
                    if k % 2:
                        ins.then_inc(xnT_ps, 1)

            def tokens_by(bank, n, i, tt):
                w = slot_k(i % RING, n)
                for k in range(KC):
                    ins = mm(ps[:, bank, 0:n], hT[:, k, tt * P:(tt + 1) * P], w[:, k, :], k == 0, k == KC - 1)
                return ins

            def features_by(bank, i, m0):
                w = slot_k(i % RING, 512)
                for m in (m0, m0 + 1):
                    for k in range(KC):
                        ins = mm(ps[:, bank, (m - m0) * T:(m - m0 + 1) * T], w[:, k, m * P:(m + 1) * P],
                                 hT[:, k, :], k == 0, k == KC - 1)
                return ins

            def gather(l, g):
                for q in range(2):
                    n = 2 * g + q
                    if not (isinstance(g, int) and g == 0):
                        pe.wait_ge(xg_sb, at(xg_sb, l, n - 1))
                    for k in range(4 * q, 4 * q + 4):
                        for tt in range(TT):
                            ins = mm(ps[:, q, (k % 4) * P:(k % 4 + 1) * P], xn[:, tt, k * P:(k + 1) * P],
                                     sel[:, tt, bass.ds(g * P, P)], tt == 0, tt == TT - 1)
                    ins.then_inc(gath_ps, 1)

            def gate_up(l, g, first):
                for j in range(XG):
                    pe.wait_ge(slot_in[GU_SLOT[j]], at(slot_in[GU_SLOT[j]], l, NT // RING + 1 + g))
                pe.wait_ge(xg_sb, at(xg_sb, l, 2 * g + 2))
                if not first:
                    pe.wait_ge(hid_sb, at(hid_sb, l, g))
                for k in range(KC):
                    for j in range(XG):
                        w = ring[:, GU_SLOT[j], :].rearrange("p (k n) -> p k n", k=KC)
                        ins = mm(ps[j * SLOTS:(j + 1) * SLOTS, 2, :], xg[:, k, j * SLOTS:(j + 1) * SLOTS],
                                 w[:, k, :], k == 0, k == KC - 1)
                ins.then_inc(gu_ps, 1)

            def turn_hidden(l, g):
                pe.wait_ge(hid_sb, at(hid_sb, l, g + 1))
                for f in range(2):
                    ins = pe.transpose(ps[:, 3, f * P:(f + 1) * P], hid[:, f * P:(f + 1) * P], ident)
                ins.then_inc(hidT_ps, 1)

            def down(l, g, first):
                pe.wait_ge(hidT_sb, at(hidT_sb, l, g + 1))
                for s in sorted(set(D_SLOT)):
                    pe.wait_ge(slot_in[s], at(slot_in[s], l, NT // RING + 1 + g))
                if not first:
                    pe.wait_ge(yg_sb, at(yg_sb, l, 2 * g))
                for half in range(2):
                    for f in range(2):
                        for j in range(XG):
                            w = ring[:, D_SLOT[j], :].rearrange("p (e f n) -> p e f n", e=2, f=2)
                            ins = mm(ps[j * SLOTS:(j + 1) * SLOTS, 4 + half, :],
                                     hidT[:, f, j * SLOTS:(j + 1) * SLOTS],
                                     w[:, j % 2, f, half * 512:(half + 1) * 512], f == 0, f == 1)
                ins.then_inc(down_ps, 1)

            def combine(l, g, tt):
                if tt == 0:
                    pe.wait_ge(yg_sb, at(yg_sb, l, 2 * g + 2))
                    pe.wait_ge(sw_sb, at(sw_sb, l, g + 1))
                pe.wait_ge(x_added, at(x_added, l, 4 * g + (4 + 2 * tt)))
                for half in range(2):
                    ins = mm(ps[:, 6 + half, :], sw[:, tt * P:(tt + 1) * P], yg[:, half * 512:(half + 1) * 512])
                ins.then_inc(comb_ps, 1)

            pe.wait_ge(consts_in, at(consts_in, 0, 3))
            for l in range(L):
                turn_norm(l, 0)
                pe.wait_ge(hT_dve, at(hT_dve, l, 4))
                pe.wait_ge(hT_act, at(hT_act, l, 4))
                for n in range(8):
                    i, tt = n // 2, n % 2
                    if tt == 0:
                        arrived(l, i)
                    tokens_by((4 + n) % 8, TOKEN_BLOCKS[i][1] - TOKEN_BLOCKS[i][0], i, tt).then_inc(tok_ps, 1)
                zdone = [1, 3, 7, 10]
                for n in range(4):
                    i = B_CQ + n // 2
                    if n % 2 == 0:
                        arrived(l, i)
                    pe.wait_ge(z_act if n % 2 == 0 else z_dve, at(z_act if n % 2 == 0 else z_dve, l, zdone[n // 2]))
                    features_by(4 + n, i, 2 * (n % 2)).then_inc(ckq_ps, 1)
                arrived(l, B_CV)
                for tt in range(TT):
                    pe.wait_ge(z_act if tt == 0 else z_dve, at(z_act if tt == 0 else z_dve, l, zdone[2]))
                    tokens_by(tt, 512, B_CV, tt).then_inc(cv_ps, 1)
                pe.wait_ge(z_act, at(z_act, l, 10))
                pe.wait_ge(z_dve, at(z_dve, l, 10))
                for n in range(4):
                    src = zaq if n < 2 else ziq
                    pe.wait_ge(roped, at(roped, l, 1 if n < 2 else 3))
                    if n >= 2:
                        pe.wait_ge(c_sb, at(c_sb, l, n - 1))
                    for h in range(4):
                        ins = pe.transpose(ps[:, 2 + n, h * P:(h + 1) * P], src[:, n % 2, h * P:(h + 1) * P], ident)
                    ins.then_inc(turn_ps, 1)
                pe.wait_ge(roped, at(roped, l, 4))
                pe.wait_ge(c_sb, at(c_sb, l, 3))
                for tt in range(TT):
                    pe.transpose(ps[:, 6, tt * T:tt * T + P], zkv[:, tt, 0:HD], ident)
                    ins = pe.transpose(ps[:, 6, tt * T + P:tt * T + 2 * P],
                                       zik[:, tt].rearrange("p a n -> p (a n)"), ident)
                ins.then_inc(turn_ps, 1)
                pe.wait_ge(bn_ready, at(bn_ready, l, 4))
                pe.wait_ge(c_sb, at(c_sb, l, 4))
                for k in range(2):
                    for tt in range(TT):
                        ins = pe.transpose(ps[:, 7, k * T + tt * P:k * T + (tt + 1) * P],
                                           zb[:, tt, k * P:(k + 1) * P], ident)
                ins.then_inc(turn_ps, 1)
                pe.wait_ge(c_sb, at(c_sb, l, 5))
                for tt in range(TT):
                    ins = pe.transpose(ps[:, 0, tt * P:(tt + 1) * P], zb[:, tt, BQ:BQ + BKV], ident)
                ins.then_inc(turn_ps, 1)
                pe.wait_ge(turn_act, at(turn_act, l, 3))
                pe.wait_ge(turn_dve, at(turn_dve, l, 2))
                for n in range(6):
                    qt = 0 if n < 2 else 1
                    odd = n % 2
                    if n == 0:
                        pe.wait_ge(c_sb, at(c_sb, l, 6))
                    r = slice(64 * odd, 64 * odd + 64)
                    for m in range(4 if qt == 0 else 2):
                        pair = m if qt == 0 else 2 * ((n - 2) // 2) + m
                        ins = mm(ps[:, 1 + n, m * keys(qt):(m + 1) * keys(qt)], iqT[r, pair, qt * P:(qt + 1) * P],
                                 keysT[r, 1, 0:keys(qt)])
                    ins.then_inc(idx_ps, 1)
                pe.wait_ge(up_in, at(up_in, l))
                pe.wait_ge(turn_dve, at(turn_dve, l, 5))
                uq = wup[:, 0:2 * H * (HD + BR)].rearrange("p (k h n) -> p k h n", k=2, h=H)
                ukv = wup[:, 2 * H * (HD + BR):NUP].rearrange("p (h n) -> p h n", h=H)
                for tt in range(TT):
                    for k in range(2):
                        ins = mm(ps[:, 7, tt * H * BR:(tt + 1) * H * BR].rearrange("p (h n) -> p h n", h=H),
                                 bcqT[:, k, tt * P:(tt + 1) * P], uq[:, k, :, HD:HD + BR], k == 0, k == 1)
                ins.then_inc(b_ps, 1)
                for n in range(2):
                    if n == 1:
                        pe.wait_ge(relu_sb, at(relu_sb, l, 1))
                    for m in range(2):
                        for k in range(2):
                            ins = mm(ps[:, n, m * T:(m + 1) * T], uq[:, k, 2 * n + m, 0:HD], bcqT[:, k, :],
                                     k == 0, k == 1)
                    ins.then_inc(b_ps, 1)
                for n in range(2):
                    pe.wait_ge(relu_sb, at(relu_sb, l, 2 + n))
                    for m in range(2):
                        ins = mm(ps[:, 2 + n, m * T:(m + 1) * T], ukv[:, 2 * n + m, 0:HD], bckvT[:])
                    ins.then_inc(b_ps, 1)
                for tt in range(TT):
                    pe.wait_ge(relu_sb, at(relu_sb, l, 4 + tt))
                    ins = mm(ps[:, 4 + tt, :].rearrange("p (h n) -> p h n", h=H), bckvT[:, tt * P:(tt + 1) * P],
                             ukv[:, :, HD:2 * HD])
                    ins.then_inc(b_ps, 1)
                pe.wait_ge(roped, at(roped, l, 6))
                pe.wait_ge(relu_sb, at(relu_sb, l, 6))
                for pair in range(2):
                    for tt in range(TT):
                        ins = pe.transpose(ps[:, 6, pair * T + tt * P:pair * T + (tt + 1) * P],
                                           zqr[:, tt, pair * P:(pair + 1) * P], ident)
                ins.then_inc(turn_ps, 1)
                pe.wait_ge(b_sb, at(b_sb, l, 1))
                for tt in range(TT):
                    ins = pe.transpose(ps[:, 7, tt * P:(tt + 1) * P], zkr[:, tt].rearrange("p a n -> p (a n)"), ident)
                ins.then_inc(turn_ps, 1)

                pe.wait_ge(b_sb, at(b_sb, l, 7))
                pe.wait_ge(turn_act, at(turn_act, l, 5))

                def scores(u):
                    m, qt = UNITS[u]
                    n = keys(qt)
                    q = slice(qt * P, (qt + 1) * P)
                    if u:
                        pe.wait_ge(logit_sb, at(logit_sb, l, u))
                    for pos in range(H):
                        out = ps[:, 2 + pos // 2, (pos % 2) * T:(pos % 2) * T + n]
                        h = HEAD_AT[m][pos]
                        if m == "a":
                            ins = mm(out, aqT[:, h, q], keysT[:, 0, 0:n])
                        elif m == "c":
                            ins = mm(out, cqT[:, h, q], ckT[:, h, 0:n])
                        else:
                            r = slice(64 * (h % 2), 64 * (h % 2) + 64)
                            mm(out, qnT[:, h, q], knT[:, h, 0:n], True, False)
                            ins = mm(out, qrT[r, h // 2, q], krT[r, 0:n], False, True)
                    ins.then_inc(score_ps, 1)

                def turn_probs(u):
                    m, qt = UNITS[u]
                    pe.wait_ge(probs_sb, at(probs_sb, l, u + 1))
                    if u:
                        pe.wait_ge(probsT_sb, at(probsT_sb, l, PT_COUNT[u - 1]))
                    for kt in range(qt + 1):
                        for pos in range(H):
                            ins = pe.transpose(ps[:, 4 + kt, pos * P:(pos + 1) * P],
                                               probs[:, pos, kt * P:(kt + 1) * P], ident)
                        ins.then_inc(probsT_ps, 1)

                def values(u):
                    m, qt = UNITS[u]
                    pe.wait_ge(probsT_sb, at(probsT_sb, l, PT_COUNT[u]))
                    if u:
                        pe.wait_ge(o_sb, at(o_sb, l, u))
                    for pos in range(H):
                        h = HEAD_AT[m][pos]
                        for kt in range(qt + 1):
                            v = {"a": zkv[:, kt, HD:2 * HD], "b": vB[:, kt, h * HD:(h + 1) * HD],
                                 "c": cv[:, kt, h * HD:(h + 1) * HD]}[m]
                            ins = mm(ps[:, 6, pos * P:(pos + 1) * P], v, probsT[:, kt, pos, :], kt == 0, kt == qt)
                    ins.then_inc(o_ps, 1)

                for n in range(12):
                    if 1 <= n <= len(UNITS):
                        turn_probs(n - 1)
                    if n < len(UNITS):
                        scores(n)
                    if 1 <= n <= len(UNITS):
                        values(n - 1)
                    i = B_GL + n // 2
                    if n % 2 == 0:
                        arrived(l, i)
                    if n >= 2:
                        pe.wait_ge(gate_sb, at(gate_sb, l, n - 1))
                    features_by(n % 2, i, 2 * (n % 2)).then_inc(gate_ps, 1)

                for n in range(12):
                    m, c = PROJ_ORDER[n // 4], 2 * (n % 4)
                    i = B_PROJ + n // 4
                    if n % 4 == 0:
                        arrived(l, i)
                        pe.wait_ge(o_sb, at(o_sb, l, 2 * (n // 4) + 2))
                    if n < 2:
                        pe.wait_ge(gate_sb, at(gate_sb, l, 11 + n))
                    elif n < 4:
                        pe.wait_ge(logit_sb, at(logit_sb, l, 6))
                    else:
                        pe.wait_ge(proj_used, at(proj_used, l, n - 3))
                    w = slot_k(i % RING, D, 4)
                    o = {"a": aqT, "b": qnT, "c": cqT}[m]
                    for cc in (c, c + 1):
                        for h in range(H):
                            ins = mm(ps[:, n % 4, (cc - c) * T:(cc - c + 1) * T], w[:, h, cc * P:(cc + 1) * P],
                                     o[:, h, :], h == 0, h == H - 1)
                    ins.then_inc(proj_ps, 1)
                for part in range(2):
                    arrived(l, B_WO + part)
                    w = slot_k((B_WO + part) % RING, D, 4)
                    for n in range(4):
                        tt, half = n // 2, n % 2
                        for k in range(4 * part, 4 * part + 4):
                            if n == 0 and k % 2 == 0:
                                pe.wait_ge(proj_used, at(proj_used, l, 8 + k // 2 + 1))
                            ins = mm(ps[:, 4 + n, :], mixT[:, k, tt * P:(tt + 1) * P],
                                     w[:, k % 4, half * 512:(half + 1) * 512], k == 0, k == KC - 1)
                        if part:
                            ins.then_inc(wo_ps, 1)
                    if not part:
                        ins.then_inc(wo_half, 1)

                turn_norm(l, 1)
                pe.wait_ge(hT_dve, at(hT_dve, l, 8))
                pe.wait_ge(hT_act, at(hT_act, l, 8))
                for tt in range(TT):
                    for k in range(KC):
                        ins = mm(ps[:, 4, tt * (G + E):(tt + 1) * (G + E)], hT[:, k, tt * P:(tt + 1) * P],
                                 small[:, l, S_R + k * (G + E):S_R + (k + 1) * (G + E)], k == 0, k == KC - 1)
                ins.then_inc(route_ps, 1)
                pe.wait_ge(asg_sb, at(asg_sb, l))
                mm(ps[:, 5, 0:E], tri, asg[:, 0, :])
                mm(ps[:, 5, E:2 * E], ones, asg[:, 0, :], True, False)
                mm(ps[:, 5, E:2 * E], tri, asg[:, 1, :], False, True)
                mm(ps[:, 5, 2 * E:3 * E], ones, asg[:, 0, :], True, False)
                ins = mm(ps[:, 5, 2 * E:3 * E], ones, asg[:, 1, :], False, True)
                ins.then_inc(rank_ps, 1)
                for tt in range(TT):
                    pe.wait_ge(sel_sb, at(sel_sb, l, tt + 1))
                gather(l, 0)
                for tt in range(TT):
                    pe.wait_ge(selw_sb, at(selw_sb, l, tt + 1))
                for n, bank in enumerate(SELW_BANKS):
                    for m in range(2):
                        for tt in range(TT):
                            ins = pe.transpose(ps[:, bank, m * T + tt * P:m * T + (tt + 1) * P],
                                               selws[tt][:, (2 * n + m) * P:(2 * n + m + 1) * P], ident)
                    ins.then_inc(selwT_ps, 1)
                pe.wait_ge(selwT_sb, at(selwT_sb, l, 4))

                def one_set(g, first, last):
                    gate_up(l, g, first)
                    if not first:
                        combine(l, g - 1, 0)
                    if not last:
                        gather(l, g + 1)
                    if not first:
                        combine(l, g - 1, 1)
                    turn_hidden(l, g)
                    down(l, g, first)
                loop_sets(pe, one_set)
                combine(l, NG - 1, 0)
                combine(l, NG - 1, 1)
                late_products(l)

        @block.scalar
        def _(act):
            def copy(out, in_, scale=1.0):
                return act.activation(out, in_, ACT.Copy, scale=scale)

            def late_tanhs(l):
                with act.If(any_late(act, l)):
                    with act.Fori(0, NG) as g:
                        for j in range(XG):
                            e1 = XG * g + (j + 1)
                            act.wait_ge(late_gu_ps[l], at(late_gu_ps[l], 0, e1))
                            for tt in range(TT):
                                act.activation(thl[:, tt, :], ps[:, tt, 0:FE], ACT.Tanh, scale=0.5).then_inc(late_tanh[l], 1)
                            act.wait_ge(late_hidT_ps[l], at(late_hidT_ps[l], 0, e1))
                            act.activation(hidTl, ps[:, 2, :].rearrange("p (f t) -> p f t", f=2),
                                           ACT.Copy).then_inc(late_hidT_sb[l], 1)

            def banks_hT(l, half):
                for k in range(KC // 2, KC):
                    act.wait_ge(xnT_ps, at(xnT_ps, l, 4 * half + k // 2 + 1))
                    gain = small[:, l, (S_GF if half else S_GA) + k:(S_GF if half else S_GA) + k + 1]
                    copy(hT[:, k, :], ps[:, k // 2, (k % 2) * T:(k % 2 + 1) * T], gain).then_inc(hT_act, 1)

            act.wait_ge(consts_in, at(consts_in, 0, 3))
            for l in range(L):
                banks_hT(l, 0)
                copy_tokens(act, l, 0, z_act, copy)
                for n in range(4):
                    act.wait_ge(ckq_ps, at(ckq_ps, l, n + 1))
                    dst = (cqT if n < 2 else ckT)[:, 2 * (n % 2):2 * (n % 2) + 2, :]
                    copy(dst, ps[:, 4 + n, :].rearrange("p (m t) -> p m t", m=2)).then_inc(c_sb, 1)
                for tt in range(TT):
                    act.wait_ge(cv_ps, at(cv_ps, l, tt + 1))
                    copy(cv[:, tt, :], ps[:, tt, :]).then_inc(c_sb, 1)
                act.wait_ge(turn_ps, at(turn_ps, l, 1))
                copy(aqT[:, :, 0:P], ps[:, 2, :].rearrange("p (h t) -> p h t", h=4)).then_inc(turn_act, 1)
                act.wait_ge(turn_ps, at(turn_ps, l, 3))
                copy(iqT[:, :, 0:P], ps[:, 4, :].rearrange("p (h t) -> p h t", h=4)).then_inc(turn_act, 1)
                act.wait_ge(turn_ps, at(turn_ps, l, 5))
                copy(keysT[:].rearrange("p s (t c) -> p t s c", c=P),
                                 ps[:, 6, :].rearrange("p (t s c) -> p t s c", t=TT, s=2)).then_inc(turn_act, 1)
                for n in range(6):
                    act.wait_ge(idx_ps, at(idx_ps, l, n + 1))
                    if n >= 2:
                        act.wait_ge(idx_used, at(idx_used, l, n - 1))
                    else:
                        act.wait_ge(roped, at(roped, l, 5))
                    act.activation(relu[:, n % 2, :], ps[:, 1 + n, :], ACT.Relu).then_inc(relu_sb, 1)
                act.wait_ge(b_ps, at(b_ps, l, 1))
                copy(zqr, ps[:, 7, :].rearrange("p (a n) -> p a n", a=TT)).then_inc(b_sb, 1)
                for n in range(2):
                    act.wait_ge(b_ps, at(b_ps, l, 2 + n))
                    copy(qnT[:, 2 * n:2 * n + 2, :], ps[:, n, :].rearrange("p (m t) -> p m t", m=2)).then_inc(b_sb, 1)
                for n in range(2):
                    act.wait_ge(b_ps, at(b_ps, l, 4 + n))
                    copy(knT[:, 2 * n:2 * n + 2, :], ps[:, 2 + n, :].rearrange("p (m t) -> p m t", m=2)).then_inc(b_sb, 1)
                for tt in range(TT):
                    act.wait_ge(b_ps, at(b_ps, l, 6 + tt))
                    copy(vB[:, tt, :], ps[:, 4 + tt, :]).then_inc(b_sb, 1)
                act.wait_ge(turn_ps, at(turn_ps, l, 8))
                copy(qrT[:], ps[:, 6, :].rearrange("p (m t) -> p m t", m=2)).then_inc(turn_act, 1)
                act.wait_ge(turn_ps, at(turn_ps, l, 9))
                copy(krT[:], ps[:, 7, 0:T]).then_inc(turn_act, 1)

                for n in range(12):
                    if 1 <= n <= len(UNITS):
                        u = n - 1
                        m, qt = UNITS[u]
                        for kt in range(qt + 1):
                            act.wait_ge(probsT_ps, at(probsT_ps, l, (PT_COUNT[u - 1] if u else 0) + kt + 1))
                            if u:
                                act.wait_ge(o_ps, at(o_ps, l, u))
                            copy(probsT[:, kt], ps[:, 4 + kt, :].rearrange("p (h q) -> p h q", h=H)).then_inc(probsT_sb, 1)
                        act.wait_ge(o_ps, at(o_ps, l, u + 1))
                        dst = {"a": aqT, "b": qnT, "c": cqT}[m]
                        src = ps[:, 6, :].rearrange("p (h q) -> p h q", h=H)
                        if m == "b":
                            dst = dst[:].rearrange("p (s o) t -> p o s t", o=2)[:, :, :, qt * P:(qt + 1) * P]
                            src = ps[:, 6, :].rearrange("p (o s q) -> p o s q", o=2, s=2)
                        else:
                            dst = dst[:, :, qt * P:(qt + 1) * P]
                        copy(dst, src).then_inc(o_sb, 1)
                    if n < len(UNITS):
                        m, qt = UNITS[n]
                        act.wait_ge(nmax_sb, at(nmax_sb, l, n + 1))
                        if n:
                            act.wait_ge(probsT_ps, at(probsT_ps, l, PT_COUNT[n - 1]))
                        for pos in range(H):
                            act.activation(probs[:, pos, 0:keys(qt)], logits[:, pos, 0:keys(qt)], ACT.Exp,
                                                     bias=st[:, 16 + pos:17 + pos], accum_out=st[:, 20 + pos:21 + pos]).then_inc(exp_sb, 1)
                    act.wait_ge(gate_ps, at(gate_ps, l, n + 1))
                    if n == SCORE_GATE:
                        act.wait_ge(logit_sb, at(logit_sb, l, 6))
                    c = 2 * n
                    act.activation(gates[:, c:c + 2, :], ps[:, n % 2, :].rearrange("p (m t) -> p m t", m=2),
                                              ACT.Tanh, scale=0.5).then_inc(gate_sb, 1)

                banks_hT(l, 1)
                act.wait_ge(gdiff_sb, at(gdiff_sb, l, 1))
                act.activation(eg, eg, ACT.Exp).then_inc(gexp_sb, 1)
                act.wait_ge(gdiff_sb, at(gdiff_sb, l, 2))
                act.activation(rw[:, 1, :], rw[:, 0, :], ACT.Exp).then_inc(gexp_sb, 1)
                for n, bank in enumerate(SELW_BANKS):
                    act.wait_ge(selwT_ps, at(selwT_ps, l, n + 1))
                    copy(selwT[:, 2 * n:2 * n + 2, :], ps[:, bank, :].rearrange("p (g t) -> p g t", g=2)).then_inc(selwT_sb, 1)

                def one_set(g, first, last):
                    act.wait_ge(gu_ps, at(gu_ps, l, g + 1))
                    if not first:
                        act.wait_ge(hid_sb, at(hid_sb, l, g))
                    act.activation(th, ps[:, 2, 0:FE], ACT.Tanh, scale=0.5).then_inc(tanh_sb, 1)
                    if first:
                        act.wait_ge(selwT_sb, at(selwT_sb, l, 4))
                    else:
                        act.wait_ge(comb_ps, at(comb_ps, l, 2 * g))
                    act.activation(sw, selwT[:, bass.ds(g, 1), :].rearrange("p g t -> p (g t)"),
                                            ACT.Copy).then_inc(sw_sb, 1)
                    act.wait_ge(hidT_ps, at(hidT_ps, l, g + 1))
                    copy(hidT, ps[:, 3, 0:2 * P].rearrange("p (f s) -> p f s", f=2)).then_inc(hidT_sb, 1)
                    act.wait_ge(down_ps, at(down_ps, l, g + 1))
                    for half in range(2):
                        copy(yg[:, half * 512:(half + 1) * 512], ps[:, 4 + half, :]).then_inc(yg_sb, 1)
                loop_sets(act, one_set)
                late_tanhs(l)

        @block.vector
        def _(dve):
            V = dve

            def copy(out, in_, scale=None):
                if scale is None:
                    return V.tensor_copy(out, in_)
                return V.tensor_scalar(out, in_, scale, None, ALU.mult)

            def route(l):
                V.wait_ge(route_ps, at(route_ps, l))
                V.tensor_tensor(lg, ps[:, 4, 0:2 * (G + E)].rearrange("p (a n) -> p a n", a=TT),
                                             rbias[:, l, :].unsqueeze(1).to_broadcast([P, TT, G + E]), ALU.add).then_inc(step, 1)
                V.wait_ge(step, steps(1))
                V.memset(g8[:], REPL).then_inc(step, 1)
                V.wait_ge(step, steps(1))
                V.tensor_copy(g8[:, :, 0:G], lg[:, :, 0:G]).then_inc(step, 1)
                V.wait_ge(step, steps(1))
                for tt in range(TT):
                    V.max(m8[:, tt, :], g8[:, tt, :]).then_inc(step, 1)
                V.wait_ge(step, steps(2))
                for tt in range(TT):
                    V.max_index(i8[:, tt, :], m8[:, tt, :], g8[:, tt, :]).then_inc(step, 1)
                V.wait_ge(step, steps(2))
                V.tensor_copy(fi[:, :, 0:1], i8[:, :, 0:1]).then_inc(step, 1)
                V.tensor_tensor(eg, lg[:, :, 0:G], m8[:, :, 0:1].to_broadcast([P, TT, G]), ALU.subtract).then_inc(step, 1)
                V.wait_ge(step, steps(2))
                V.tensor_tensor(ohg, iota[:, 0:G].unsqueeze(1).to_broadcast([P, TT, G]),
                                            fi[:, :, 0:1].to_broadcast([P, TT, G]), ALU.is_equal).then_inc(gdiff_sb, 1)
                V.wait_ge(gdiff_sb, at(gdiff_sb, l, 1))
                for tt in range(TT):
                    V.tensor_tensor(prod[:, tt, :].rearrange("p (g e) -> p g e", g=G),
                                               lg[:, tt, G:G + E].rearrange("p (g e) -> p g e", g=G),
                                               ohg[:, tt, :].unsqueeze(2).to_broadcast([P, G, EPG]), ALU.mult).then_inc(step, 1)
                V.wait_ge(step, steps(2))
                for tt in range(TT):
                    V.tensor_reduce(ein[:, tt, :], prod[:, tt, :].rearrange("p (g e) -> p e g", g=G),
                                               AX_X, ALU.add).then_inc(step, 1)
                V.wait_ge(step, steps(2))
                for tt in range(TT):
                    V.max(e8[:, tt, :], ein[:, tt, :]).then_inc(step, 1)
                V.wait_ge(step, steps(2))
                for tt in range(TT):
                    V.max_index(j8[:, tt, :], e8[:, tt, :], ein[:, tt, :]).then_inc(step, 1)
                V.wait_ge(step, steps(2))
                V.tensor_copy(fi[:, :, 1:3], j8[:, :, 0:2]).then_inc(step, 1)
                V.wait_ge(step, steps(1))
                V.tensor_tensor(rw[:, 0, :], e8[:, :, 1], e8[:, :, 0], ALU.subtract).then_inc(gdiff_sb, 1)
                V.tensor_tensor(oh1, iota[:, 0:EPG].unsqueeze(1).to_broadcast([P, TT, EPG]),
                                             fi[:, :, 1:2].to_broadcast([P, TT, EPG]), ALU.is_equal).then_inc(step, 1)
                V.tensor_tensor(oh2, iota[:, 0:EPG].unsqueeze(1).to_broadcast([P, TT, EPG]),
                                          fi[:, :, 2:3].to_broadcast([P, TT, EPG]), ALU.is_equal).then_inc(step, 1)
                V.wait_ge(step, steps(2))
                V.tensor_tensor(ce, oh1, oh2, ALU.add).then_inc(step, 1)
                V.wait_ge(step, steps(1))
                for tt in range(TT):
                    last = V.tensor_tensor(asg[:, tt, :].rearrange("p (g e) -> p g e", g=G),
                                           ohg[:, tt, :].unsqueeze(2).to_broadcast([P, G, EPG]),
                                           ce[:, tt, :].unsqueeze(1).to_broadcast([P, G, EPG]), ALU.mult)
                    if tt == 0:
                        last.then_inc(step, 1)
                        V.wait_ge(step, steps(1))
                last.then_inc(asg_sb, 1)
                V.wait_ge(gexp_sb, at(gexp_sb, l, 2))
                V.tensor_reduce(rw[:, 2, :], eg, AX_X, ALU.add).then_inc(step, 1)
                V.tensor_scalar(rw[:, 3, :], rw[:, 1, :], 1.0, None, ALU.add).then_inc(step, 1)
                V.wait_ge(step, steps(2))
                V.tensor_tensor(rw[:, 4, :], rw[:, 2, :], rw[:, 3, :], ALU.mult).then_inc(step, 1)
                V.wait_ge(step, steps(1))
                V.reciprocal(rw[:, 5, :], rw[:, 4, :]).then_inc(step, 1)
                V.wait_ge(step, steps(1))
                V.tensor_scalar(rw[:, 6, :], rw[:, 5, :], 0.5, None, ALU.mult).then_inc(step, 1)
                V.wait_ge(step, steps(1))
                V.tensor_tensor(rw[:, 7, :], rw[:, 6, :], rw[:, 1, :], ALU.mult).then_inc(step, 1)
                V.wait_ge(step, steps(1))
                V.tensor_tensor(oh1, oh1, rw[:, 6, :].unsqueeze(2).to_broadcast([P, TT, EPG]), ALU.mult).then_inc(step, 1)
                V.tensor_tensor(oh2, oh2, rw[:, 7, :].unsqueeze(2).to_broadcast([P, TT, EPG]), ALU.mult).then_inc(step, 1)
                V.wait_ge(step, steps(2))
                V.tensor_tensor(ce, oh1, oh2, ALU.add).then_inc(step, 1)
                V.wait_ge(step, steps(1))
                for tt in range(TT):
                    V.tensor_tensor(comb[:, tt, :].rearrange("p (g e) -> p g e", g=G),
                                               ohg[:, tt, :].unsqueeze(2).to_broadcast([P, G, EPG]),
                                               ce[:, tt, :].unsqueeze(1).to_broadcast([P, G, EPG]), ALU.mult).then_inc(step, 1)
                V.wait_ge(step, steps(2))
                V.wait_ge(rank_ps, at(rank_ps, l))
                V.wait_ge(asg_sb, at(asg_sb, l))
                V.scalar_tensor_tensor(rk, ps[:, 5, 0:2 * E].rearrange("p (a n) -> p a n", a=TT), 1.0,
                                                    asg, ALU.add, ALU.mult).then_inc(step, 1)
                V.wait_ge(step, steps(1))
                V.tensor_scalar(rk, rk, -1.0, None, ALU.add).then_inc(step, 1)
                V.wait_ge(step, steps(1))
                for tt in range(TT):
                    V.tensor_tensor(sel[:, tt, :].rearrange("p (e s) -> p e s", e=E),
                                              iota.unsqueeze(1).to_broadcast([P, E, SLOTS]),
                                              rk[:, tt, :].unsqueeze(2).to_broadcast([P, E, SLOTS]), ALU.is_equal).then_inc(sel_sb, 1)
                for tt in range(TT):
                    V.wait_ge(sel_sb, at(sel_sb, l, tt + 1))
                    V.tensor_tensor(selws[tt].rearrange("p (e s) -> p e s", e=E),
                                               sel[:, tt, :].rearrange("p (e s) -> p e s", e=E),
                                               comb[:, tt, :].unsqueeze(2).to_broadcast([P, E, SLOTS]), ALU.mult).then_inc(selw_sb, 1)
                V.tensor_scalar(late, rk, LATE_FROM - 0.5, None, ALU.is_gt).then_inc(step, 1)
                V.tensor_reduce(cnt, ps[:, 5, 2 * E:3 * E], AX_X, ALU.max).then_inc(step, 1)
                V.wait_ge(step, steps(2))
                V.tensor_tensor(late, late, comb, ALU.mult).then_inc(step, 1)
                V.wait_ge(step, steps(1))
                V.tensor_scalar(flag[:], cnt, LATE_FROM + 0.5, None, ALU.is_gt).then_inc(flag_sb, 1)

            def late_sums(l):
                with V.If(any_late(V, l)):
                    with V.Fori(0, NG) as g:
                        for j in range(XG):
                            for tt in range(TT):
                                n = TT * XG * g + (TT * j + tt + 1)
                                V.wait_ge(late_tanh[l], at(late_tanh[l], 0, n))
                                V.scalar_tensor_tensor(thl[:, tt, :], thl[:, tt, :], 1.0, ps[:, tt, 0:FE],
                                                       ALU.add, ALU.mult).then_inc(late_silu[l], 1)
                                V.wait_ge(late_silu[l], at(late_silu[l], 0, n))
                                w = late[:, tt, bass.ds(XG * g + j, 1)]
                                V.scalar_tensor_tensor(hidl[:, tt, :], thl[:, tt, :], w, ps[:, tt, FE:2 * FE],
                                                       ALU.mult, ALU.mult).then_inc(late_hid[l], 1)
                            V.wait_ge(late_done[l], at(late_done[l], 0, XG * g + (j + 2)))
                            for n in range(4):
                                xs = x[:, n // 2, (n % 2) * 512:(n % 2 + 1) * 512]
                                ins = V.tensor_tensor(xs, xs, ps[:, 4 + n, :], ALU.add)
                                ins.then_inc(late_added[l], 1)
                            V.wait_ge(late_added[l], at(late_added[l], 0, 4 * XG * g + 4 * (j + 1)))

            def mean_square(l, half):
                for tt in range(TT):
                    V.tensor_tensor_reduce(xn[:, tt, :], x[:, tt, :], x[:, tt, :], 1.0, 0.0,
                                                      ALU.mult, ALU.add, st[:, 2 + tt:3 + tt]).then_inc(step, 1)
                V.wait_ge(step, steps(2))
                V.tensor_scalar(st[:, 0:2], st[:, 2:4], 1.0 / D, EPS, ALU.mult, ALU.add).then_inc(var_ready, 1)

            def norm(l, half):
                mean_square(l, half)
                V.wait_ge(rstd_ready, at(rstd_ready, l, 3 if half else 1))
                for tt in range(TT):
                    V.tensor_scalar(xn[:, tt, :], x[:, tt, :], st[:, 8 + tt:9 + tt], None, ALU.mult).then_inc(xn_ready, 1)
                for k in range(KC // 2):
                    V.wait_ge(xnT_ps, at(xnT_ps, l, 4 * half + k // 2 + 1))
                    gain = small[:, l, (S_GF if half else S_GA) + k:(S_GF if half else S_GA) + k + 1]
                    copy(hT[:, k, :], ps[:, k // 2, (k % 2) * T:(k % 2 + 1) * T], gain).then_inc(hT_dve, 1)

            def rope(l, k, view, n, rot, oc, os):
                if k:
                    V.wait_ge(roped, at(roped, l, k))
                size = TT * n * rot
                t1 = rope1[:, 0:size].rearrange("p (a n r) -> p a n r", a=TT, n=n)
                t2 = rope2[:, 0:size].rearrange("p (a n r) -> p a n r", a=TT, n=n)
                cos = cst[:, oc:oc + TT * rot].rearrange("p (a r) -> p a r", a=TT).unsqueeze(2)
                sin = cst[:, os:os + TT * rot].rearrange("p (a r) -> p a r", a=TT).unsqueeze(2)
                hf = rot // 2
                z = view[:, :, :, 0:rot]
                V.tensor_tensor(t1, z, cos.to_broadcast([P, TT, n, rot]), ALU.mult).then_inc(step, 1)
                V.tensor_tensor(t2[:, :, :, 0:hf], z[:, :, :, hf:rot],
                                    sin[:, :, :, 0:hf].to_broadcast([P, TT, n, hf]), ALU.mult).then_inc(step, 1)
                V.tensor_tensor(t2[:, :, :, hf:rot], z[:, :, :, 0:hf],
                                    sin[:, :, :, hf:rot].to_broadcast([P, TT, n, hf]), ALU.mult).then_inc(step, 1)
                V.wait_ge(step, steps(3))
                V.tensor_tensor(z, t1, t2, ALU.add).then_inc(roped, 1)

            def heads(t, n):
                return t.rearrange("p a (n r) -> p a n r", n=n)

            def index_score(l, qt):
                n = keys(qt)
                out = score[:, qt, 0:n]
                first = True
                for b in (range(2) if qt == 0 else range(2, 6)):
                    V.wait_ge(relu_sb, at(relu_sb, l, b + 1))
                    count = 4 if qt == 0 else 2
                    for m in range(count):
                        pair = m if qt == 0 else 2 * ((b - 2) // 2) + m
                        h = 2 * pair + b % 2
                        r = relu[:, b % 2, m * n:(m + 1) * n]
                        w = ziw[:, qt, h:h + 1]
                        if first:
                            ins = V.tensor_scalar(out, r, w, None, ALU.mult)
                        else:
                            ins = V.scalar_tensor_tensor(out, r, w, out, ALU.mult, ALU.add)
                        first = False
                        if m == count - 1:
                            ins.then_inc(idx_used, 1)
                            V.wait_ge(idx_used, at(idx_used, l, b + 1))
                        else:
                            ins.then_inc(step, 1)
                            V.wait_ge(step, steps(1))
                V.tensor_tensor(out, out, mask_of(qt), ALU.add).then_inc(step, 1)
                V.wait_ge(step, steps(1))

            def top_keys(qt):
                out = score[:, qt, 0:keys(qt)]
                for _ in range(TOPK // 8):
                    V.max(st8[:], out).then_inc(step, 1)
                    V.wait_ge(step, steps(1))
                    V.match_replace(out, st8[:], out, REPL).then_inc(step, 1)
                    V.wait_ge(step, steps(1))
                V.tensor_scalar(out, out, REPL / 2, NEG, ALU.is_gt, ALU.mult).then_inc(step, 1)
                V.wait_ge(step, steps(1))

            def softmax(l, u):
                m, qt = UNITS[u]
                n = keys(qt)
                V.wait_ge(score_ps, at(score_ps, l, u + 1))
                if u:
                    V.wait_ge(exp_sb, at(exp_sb, l, 4 * u))
                src = ps[:, 2:4, :].rearrange("p b (s k) -> p (b s) k", k=T)[:, :, 0:n]
                if m == "c":
                    if u == 0:
                        V.wait_ge(cb_masked, at(cb_masked, l))
                    bias = cbias[:, :, P:2 * P] if qt == 0 else cbias[:]
                elif m == "b":
                    bias = mask_of(qt).unsqueeze(1).to_broadcast([P, H, n])
                else:
                    bias = score[:, qt, 0:n].unsqueeze(1).to_broadcast([P, H, n])
                scale = {"a": HD ** -0.5, "b": (HD + BR) ** -0.5, "c": HD ** -0.5}[m]
                V.scalar_tensor_tensor(logits[:, :, 0:n], src, scale, bias, ALU.mult, ALU.add).then_inc(logit_sb, 1)
                V.wait_ge(logit_sb, at(logit_sb, l, u + 1))
                V.tensor_reduce(st[:, 16:20], logits[:, :, 0:n], AX_X, ALU.max, negate=True).then_inc(nmax_sb, 1)
                V.wait_ge(exp_sb, at(exp_sb, l, 4 * u + 4))
                if u:
                    V.wait_ge(probs_sb, at(probs_sb, l, u))
                V.reciprocal(st[:, 24:28], st[:, 20:24]).then_inc(step, 1)
                V.wait_ge(step, steps(1))
                r = st[:, 24:28].unsqueeze(2).to_broadcast([P, H, n])
                V.tensor_tensor(probs[:, :, 0:n], probs[:, :, 0:n], r, ALU.mult).then_inc(probs_sb, 1)

            V.wait_ge(consts_in, at(consts_in, 0, 3))
            V.wait_ge(rbias_in, at(rbias_in, 0, 1))
            for l in range(L):
                norm(l, 0)
                copy_tokens(V, l, 1, z_dve, copy)
                V.wait_ge(z_act, at(z_act, l, 10))
                V.wait_ge(z_dve, at(z_dve, l, 10))
                rope(l, 0, heads(zaq, H), H, A_ROT, C_CA, C_SA)
                rope(l, 1, heads(zkv[:], 2)[:, :, 0:1, :], 1, A_ROT, C_CA, C_SA)
                rope(l, 2, heads(ziq, IH), IH, I_ROT, C_CI, C_SI)
                rope(l, 3, zik, 2, I_ROT, C_CI, C_SI)
                rope(l, 4, zkr, 2, BR, C_CB, C_SB)
                V.tensor_scalar(ziw, ziw, float(IH ** -0.5 * ID ** -0.5), None, ALU.mult).then_inc(step, 1)
                V.wait_ge(step, steps(1))
                junk = rope1[:, 0:BQ]
                V.wait_ge(roped, at(roped, l, 5))
                for n, (o, w) in enumerate(((0, BQ), (BQ, BKV))):
                    for tt in range(TT):
                        V.tensor_tensor_reduce([junk, rope2][tt][:, 0:w], zb[:, tt, o:o + w], zb[:, tt, o:o + w], 1.0,
                                                          0.0, ALU.mult, ALU.add, st[:, 28 + 2 * n + tt:29 + 2 * n + tt]).then_inc(step, 1)
                    V.wait_ge(step, steps(2))
                V.tensor_scalar(st[:, 4:6], st[:, 28:30], 1.0 / BQ, EPS, ALU.mult, ALU.add).then_inc(step, 1)
                V.wait_ge(step, steps(1))
                V.tensor_scalar(st[:, 6:8], st[:, 30:32], 1.0 / BKV, EPS, ALU.mult, ALU.add).then_inc(var_ready, 1)
                V.wait_ge(rstd_ready, at(rstd_ready, l, 2))
                for n, (o, w) in enumerate(((0, BQ), (BQ, BKV))):
                    for tt in range(TT):
                        V.tensor_scalar(zb[:, tt, o:o + w], zb[:, tt, o:o + w],
                                                    st[:, 12 + 2 * n + tt:13 + 2 * n + tt], None, ALU.mult).then_inc(bn_ready, 1)
                V.wait_ge(turn_ps, at(turn_ps, l, 2))
                copy(aqT[:, :, P:2 * P], ps[:, 3, :].rearrange("p (h t) -> p h t", h=4)).then_inc(turn_dve, 1)
                V.wait_ge(turn_ps, at(turn_ps, l, 4))
                copy(iqT[:, :, P:2 * P], ps[:, 5, :].rearrange("p (h t) -> p h t", h=4)).then_inc(turn_dve, 1)
                V.wait_ge(turn_ps, at(turn_ps, l, 6))
                for k in range(2):
                    copy(bcqT[:, k, :], ps[:, 7, k * T:(k + 1) * T], small[:, l, S_GQ + k:S_GQ + k + 1]).then_inc(turn_dve, 1)
                V.wait_ge(turn_ps, at(turn_ps, l, 7))
                copy(bckvT[:], ps[:, 0, 0:T], small[:, l, S_GKV:S_GKV + 1]).then_inc(turn_dve, 1)
                index_score(l, 0)
                index_score(l, 1)
                V.wait_ge(b_sb, at(b_sb, l, 1))
                rope(l, 5, heads(zqr, H), H, BR, C_CB, C_SB)
                for u in range(len(UNITS)):
                    softmax(l, u)
                    if u < TT:
                        top_keys(u)
                for n in range(12):
                    m, c = PROJ_ORDER[n // 4], 2 * (n % 4)
                    V.wait_ge(proj_ps, at(proj_ps, l, n + 1))
                    if n == 0:
                        V.wait_ge(gate_sb, at(gate_sb, l))
                        V.wait_ge(o_ps, at(o_ps, l))
                    g = gates[:, KC * "abc".index(m) + c:KC * "abc".index(m) + c + 2, :]
                    src = ps[:, n % 4, :].rearrange("p (m t) -> p m t", m=2)
                    dst = mixT[:, c:c + 2, :]
                    if n < 4:
                        V.scalar_tensor_tensor(dst, g, 1.0, src, ALU.add, ALU.mult).then_inc(proj_used, 1)
                    else:
                        V.scalar_tensor_tensor(g, g, 1.0, src, ALU.add, ALU.mult).then_inc(step, 1)
                        V.wait_ge(step, steps(1))
                        if n == 4:
                            V.wait_ge(proj_used, at(proj_used, l, 4))
                        elif n == 8:
                            V.wait_ge(proj_used, at(proj_used, l, 8))
                        V.tensor_tensor(dst, dst, g, ALU.add).then_inc(proj_used, 1)
                for n in range(4):
                    tt, half = n // 2, n % 2
                    V.wait_ge(wo_ps, at(wo_ps, l, n + 1))
                    xs = x[:, tt, half * 512:(half + 1) * 512]
                    V.scalar_tensor_tensor(xs, ps[:, 4 + n, :], 0.5, xs, ALU.mult, ALU.add).then_inc(x_added, 1)
                V.wait_ge(x_added, at(x_added, l, 4))
                norm(l, 1)
                route(l)

                def hidden(g, first):
                    V.wait_ge(tanh_sb, at(tanh_sb, l, g + 1))
                    V.scalar_tensor_tensor(th, th, 1.0, ps[:, 2, 0:FE], ALU.add, ALU.mult).then_inc(silu_sb, 1)
                    if not first:
                        V.wait_ge(hidT_ps, at(hidT_ps, l, g))
                    V.wait_ge(silu_sb, at(silu_sb, l, g + 1))
                    V.tensor_tensor(hid, th, ps[:, 2, FE:2 * FE], ALU.mult).then_inc(hid_sb, 1)

                def gathered(g):
                    for q in range(2):
                        V.wait_ge(gath_ps, at(gath_ps, l, 2 * g + q + 1))
                        gain = small[:, l, S_GF + 4 * q:S_GF + 4 * q + 4].unsqueeze(2).to_broadcast([P, 4, P])
                        V.tensor_tensor(xg[:, 4 * q:4 * q + 4, :],
                                                 ps[:, q, :].rearrange("p (k s) -> p k s", k=4), gain, ALU.mult).then_inc(xg_sb, 1)

                def add_back(g, tt):
                    V.wait_ge(comb_ps, at(comb_ps, l, 2 * g + tt + 1))
                    for half in range(2):
                        xs = x[:, tt, half * 512:(half + 1) * 512]
                        V.wait_ge(x_added, at(x_added, l, 4 * g + (2 * tt + half + 1)))
                        V.tensor_tensor(xs, xs, ps[:, 6 + half, :], ALU.add).then_inc(x_added, 1)

                gathered(0)

                def one_set(g, first, last):
                    hidden(g, first)
                    if not first:
                        add_back(g - 1, 0)
                    if not last:
                        V.wait_ge(gu_ps, at(gu_ps, l, g + 1))
                        gathered(g + 1)
                    if not first:
                        add_back(g - 1, 1)
                loop_sets(V, one_set)
                add_back(NG - 1, 0)
                add_back(NG - 1, 1)
                V.wait_ge(x_added, at(x_added, l))
                late_sums(l)

            mean_square(L, 0)
            V.wait_ge(rstd_ready, at(rstd_ready, L, 1))
            V.wait_ge(fgain_in, at(fgain_in, 0, 1))
            for tt in range(TT):
                V.scalar_tensor_tensor(xn[:, tt, :], x[:, tt, :], st[:, 8 + tt:9 + tt], fgain,
                                                    ALU.mult, ALU.mult).then_inc(out_ready, 1)


def blocks(w, k):
    return w.reshape(k, P, -1).transpose(1, 0, 2).reshape(P, -1)


def kernel(**inputs):
    import concourse.bacc as _bacc
    from concourse.bass_utils import run_bass_kernel_spmd as _run

    i = {k: np.asarray(v) for k, v in inputs.items()}
    stream = np.zeros((L * PER_LAYER, P, BLK), np.float32)
    small = np.zeros((L, P, NSMALL), np.float32)
    up = np.zeros((L, P, NUP), np.float32)
    for l in range(L):
        s = stream[l * PER_LAYER:(l + 1) * PER_LAYER]
        win = i["w_in"][l]
        for n, (lo, hi) in enumerate(TOKEN_BLOCKS + [(c, c + 512) for c in range(O_CQ, N_IN, 512)]):
            s[n, :, :KC * (hi - lo)] = blocks(win[:, lo:hi], KC)
        for n, m in enumerate(PROJ_ORDER):
            s[B_PROJ + n] = blocks(i[f"w_proj_{m}"][l], 4)
        for n in range(2):
            s[B_WO + n] = blocks(i["w_out"][l][n * 512:(n + 1) * 512], 4)
        for g in range(NG):
            for n, (kind, j) in enumerate(SET_ORDER):
                e = XG * g + j
                if kind == "gu":
                    w = blocks(np.concatenate([i["w_gate"][l, e], i["w_up"][l, e]], 1), KC)
                else:
                    w = blocks(i["w_down"][l, e:e + 2].reshape(2 * FE, D), 4)
                s[NT + PER_SET * g + n] = w
        small[l, :, S_GA:S_GA + KC] = i["attn_norm_g"][l].reshape(KC, P).T
        small[l, :, S_GF:S_GF + KC] = i["ffn_norm_g"][l].reshape(KC, P).T
        small[l, :, S_GQ:S_GQ + 2] = i["b_q_norm_g"][l].reshape(2, P).T
        small[l, :, S_GKV] = i["b_kv_norm_g"][l]
        small[l, :, S_R:] = blocks(np.concatenate([i["w_group"][l], i["w_router"][l]], 1), KC)
        up[l] = np.concatenate([blocks(i["b_w_uq"][l], 2), i["b_w_ukv"][l]], 1)
    at = np.minimum(P + np.arange(P)[:, None] - np.arange(T)[None, :], REL) + REL
    rel = i["c_rel_bias"][:, :, at].transpose(0, 2, 1, 3).reshape(L, P, H * T)
    arrays = {
        "x": i["x"], "consts": shape_constants(), "stream": stream, "small": small, "up": up,
        "rel": np.ascontiguousarray(rel), "final_gain": i["final_norm_g"],
        "rbias": np.concatenate([i["b_group"], i["b_router"]], 1),
    }
    nc = _bacc.Bacc("TRN2", target_bir_lowering=False, num_devices=1)
    a = {n: nc.dram_tensor(f"in_{n}", v.shape, mybir.dt.from_np(v.dtype), kind="ExternalInput").ap()
         for n, v in arrays.items()}
    a["out"] = nc.dram_tensor("out_dram", (1, T, D), F32, kind="ExternalOutput").ap()
    build(nc, a)
    r = _run(nc, [{f"in_{n}": v for n, v in arrays.items()}], core_ids=[0])
    return r.results[0]["out_dram"]
```

```python
from contextlib import ExitStack

import numpy as np
import concourse.bass as bass
from concourse import mybir

F32 = mybir.dt.float32
F32R = mybir.dt.float32r
U32 = mybir.dt.uint32
I32 = mybir.dt.int32
ALU = mybir.AluOpType
ACT = mybir.ActivationFunctionType
AX_X = mybir.AxisListType.X

P = 128
L = 2
D = 1024
T = 256
TT = T // P
KC = D // P
CHUNK = 64
EPS = 1e-6
H = 4
HD = 128
IH, ID = 8, 64
TOPK = 64
BQ, BKV, BR = 256, 128, 64
A_ROT, I_ROT = HD // 4, ID // 4
N_IN = 6408
REL = 128
G, EPG = 4, 8
E = G * EPG
FE = 256
SLOTS = 32
XG = P // SLOTS
NG = E // XG
LATE_FROM = SLOTS
SCORE_GATE = 9
NEG = -1.0e30
REPL = -3.0e38

O_AQ, O_KV, O_IQ, O_IK, O_IW = 0, 512, 768, 1280, 1344
O_BQ, O_BKV, O_BKR = 1352, 1608, 1736
O_CQ, O_CK, O_CV, O_GL = 1800, 2312, 2824, 3336

RING = 6
BLK = 4096
NT = 18
PER_SET = 6
PER_LAYER = NT + PER_SET * NG
TOKEN_BLOCKS = [(0, 512), (512, 1024), (1024, 1352), (1352, 1800)]
B_CQ, B_CK, B_CV, B_GL, B_PROJ, B_WO = 4, 5, 6, 7, 13, 16
PROJ_ORDER = "cba"
SPLIT = B_PROJ
HALVES = 2 * SPLIT
WAYS = 4
SET_ORDER = [("gu", 0), ("gu", 1), ("gu", 2), ("gu", 3), ("d", 0), ("d", 2)]
EXTRA = 2
FIRST_SET = [4, 5, "extra0", 2, 3, "extra1", 0, 1]
GU_SLOT = [0, 1, 2, 3]
D_SLOT = [4, 4, 5, 5]
TRUNK_IN_SLOT = [(NT + WAYS - 1 - s) // WAYS if s < WAYS else 0 for s in range(RING)]

C_ID, C_U, C_ONE, C_M = 0, 128, 256, 384
C_CA, C_SA = 640, 640 + 2 * A_ROT
C_CI, C_SI = C_SA + 2 * A_ROT, C_SA + 2 * A_ROT + 2 * I_ROT
C_CB, C_SB = C_SI + 2 * I_ROT, C_SI + 2 * I_ROT + 2 * BR
C_IOTA = C_SB + 2 * BR
NCONST = C_IOTA + SLOTS
S_GA, S_GF, S_GQ, S_GKV, S_R = 0, KC, 2 * KC, 2 * KC + 2, 2 * KC + 3
NSMALL = S_R + KC * (G + E)
NUP = 2 * H * (HD + BR) + H * 2 * HD


def shape_constants():
    c = np.zeros((P, NCONST), np.float32)
    c[:, C_ID:C_ID + P] = np.eye(P)
    c[:, C_U:C_U + P] = np.triu(np.ones((P, P)), 1)
    c[:, C_ONE:C_ONE + P] = 1.0
    c[:CHUNK, C_M + 3 * CHUNK:C_M + 4 * CHUNK] = NEG
    for rot, oc, os in ((A_ROT, C_CA, C_SA), (I_ROT, C_CI, C_SI), (BR, C_CB, C_SB)):
        pos = np.arange(T, dtype=np.float32)
        inv = np.float32(500000.0) ** (-np.arange(0, rot, 2, dtype=np.float32) / np.float32(rot))
        ang = pos[:, None] * inv[None, :].astype(np.float32)
        cos, sin = np.cos(ang), np.sin(ang)
        for tt in range(TT):
            r = slice(tt * P, tt * P + P)
            c[:, oc + tt * rot:oc + (tt + 1) * rot] = np.concatenate([cos[r], cos[r]], 1)
            c[:, os + tt * rot:os + (tt + 1) * rot] = np.concatenate([-sin[r], sin[r]], 1)
    c[:, C_IOTA:C_IOTA + SLOTS] = np.arange(SLOTS)
    c[:, C_IOTA + LATE_FROM:C_IOTA + SLOTS] = -5.0
    return c


def build(nc, a):
    ctx = ExitStack()
    with ctx:
        def sb(name, shape, dt=F32):
            return ctx.enter_context(nc.sbuf_tensor(name, shape, dt))

        counts = {}

        def sig(name, per, unit=1):
            handle = ctx.enter_context(nc.semaphore(name))
            counts[handle.name] = per, unit
            return handle

        def at(signal, l, n=None):
            per, unit = counts[signal.name]
            return (l * per + (per if n is None else n)) * unit

        ps = ctx.enter_context(nc.psum_tensor("ps", [P, 8, 512], F32))

        ring = sb("ring", [P, RING, BLK])
        ring_at = nc.lookup_mloc(ring).addr
        w_hi = nc.alloc_sbuf_tensor_at("w_hi", [P, 2, BLK // 2], F32R, offset=ring_at + 4 * WAYS * BLK)
        w_lo = nc.alloc_sbuf_tensor_at("w_lo", [P, 2, BLK // 2], F32R, offset=ring_at + 4 * (WAYS + 1) * BLK)
        x = sb("x", [P, TT, D])
        xn = sb("xn", [P, TT, D])
        hT = sb("hT", [P, KC, T])
        hT_hi = nc.alloc_sbuf_tensor_at("hT_hi", [P, KC, T], F32R, offset=nc.lookup_mloc(hT).addr)
        hT_lo = sb("hT_lo", [P, KC, T], F32R)
        wup = sb("wup", [P, NUP])
        cst = sb("cst", [P, NCONST])
        small = sb("small", [P, L, NSMALL])
        rbias = sb("rbias", [P, L, G + E])
        knT = wup[:, 0:H * T].rearrange("p (h t) -> p h t", h=H)
        qrT = wup[:, H * T:(H + 2) * T].rearrange("p (m t) -> p m t", m=2)
        krT = wup[:, (H + 2) * T:(H + 3) * T]
        cbias = sb("cbias", [P, H, T])
        aqT = sb("aqT", [P, H, T])
        cqT = sb("cqT", [P, H, T])
        qnT = sb("qnT", [P, H, T])
        extra = [nc.alloc_sbuf_tensor_at(f"extra{n}", [P, BLK], F32, offset=nc.lookup_mloc(t).addr)
                 for n, t in enumerate((hT_lo, cbias))]
        gates = sb("gates", [P, 3 * KC, T])
        keysT = sb("keysT", [P, 2, T])
        iqT = sb("iqT", [P, IH // 2, T])
        bckvT = sb("bckvT", [P, T])
        vB = sb("vB", [P, TT, H * HD])
        ckT = sb("ckT", [P, H, T])
        cv = sb("cv", [P, TT, H * HD])
        zkv = sb("zkv", [P, TT, 2 * HD])
        st = sb("st", [P, 64])
        st8 = sb("st8", [P, 8])
        flag = sb("flag", [P, 1], I32)

        gf = gates[:].rearrange("p c t -> p (c t)")
        zaq = gf[:, 0:1024].rearrange("p (a n) -> p a n", a=TT)
        ziq = gf[:, 1024:2048].rearrange("p (a n) -> p a n", a=TT)
        zb = gf[:, 2048:2816].rearrange("p (a n) -> p a n", a=TT)
        zik = gf[:, 2816:3072].rearrange("p (a s n) -> p a s n", a=TT, s=2)
        zkr = gf[:, 3072:3328].rearrange("p (a s n) -> p a s n", a=TT, s=2)
        ziw = gf[:, 3328:3344].rearrange("p (a n) -> p a n", a=TT)
        score = gf[:, SCORE_GATE * 512:SCORE_GATE * 512 + 512].rearrange("p (a n) -> p a n", a=TT)
        logits = iqT[:].rearrange("p s t -> p s t")
        xnf = xn[:].rearrange("p a d -> p (a d)")
        probsT = xnf[:, 0:1024].rearrange("p (k h q) -> p k h q", k=2, h=H)
        rope1 = xnf[:, 1024:1536]
        rope2 = xnf[:, 1536:2048]
        probs = xnf[:, 1024:2048].rearrange("p (h k) -> p h k", h=H)
        relu = xnf[:, 1024:2048].rearrange("p (b n) -> p b n", b=2)
        bcqT = xnf[:, 512:1024].rearrange("p (k t) -> p k t", k=2)
        zqr = xnf[:, 0:512].rearrange("p (a n) -> p a n", a=TT)
        mixT = xnf.rearrange("p (c t) -> p c t", c=KC)
        junk = gf[:, 0:2048].rearrange("p (n c) -> p n c", n=4)
        routerT = zkv[:].rearrange("p a n -> p (a n)")[0:G + E, 0:T]
        sel = gf[:, 0:2048].rearrange("p (a n) -> p a n", a=TT)
        selwT = gf[:, 2048:4096].rearrange("p (g t) -> p g t", g=NG)
        xg = gf[:, 4096:5120].rearrange("p (k s) -> p k s", k=KC)
        yg = gf[:, 5120:6144].rearrange("p d -> p d")
        cf = ckT[:].rearrange("p h t -> p (h t)")
        selw = vB[:].rearrange("p a n -> p (a n)")
        selw1 = iqT[:].rearrange("p s t -> p (s t)")
        selws = [selw, selw1]
        sw = cf[:, 0:256]
        hid = cf[:, 256:512]
        th = cf[:, 512:768]
        hidT = cf[:, 768:1024].rearrange("p (f s) -> p f s", f=2)
        cvf = cv[:].rearrange("p a n -> p (a n)")
        lg = cvf[:, 0:72].rearrange("p (a n) -> p a n", a=TT)
        g8 = cvf[:, 72:88].rearrange("p (a n) -> p a n", a=TT)
        m8 = cvf[:, 88:104].rearrange("p (a n) -> p a n", a=TT)
        i8 = cvf[:, 104:120].rearrange("p (a n) -> p a n", a=TT).bitcast(U32)
        prod = cvf[:, 120:184].rearrange("p (a n) -> p a n", a=TT)
        ein = cvf[:, 184:200].rearrange("p (a n) -> p a n", a=TT)
        e8 = cvf[:, 200:216].rearrange("p (a n) -> p a n", a=TT)
        j8 = cvf[:, 216:232].rearrange("p (a n) -> p a n", a=TT).bitcast(U32)
        fi = cvf[:, 232:240].rearrange("p (a n) -> p a n", a=TT)
        ohg = cvf[:, 240:248].rearrange("p (a n) -> p a n", a=TT)
        eg = cvf[:, 248:256].rearrange("p (a n) -> p a n", a=TT)
        rw = cvf[:, 256:272].rearrange("p (n a) -> p n a", a=TT)
        oh1 = cvf[:, 272:288].rearrange("p (a n) -> p a n", a=TT)
        oh2 = cvf[:, 288:304].rearrange("p (a n) -> p a n", a=TT)
        ce = cvf[:, 304:320].rearrange("p (a n) -> p a n", a=TT)
        comb = cvf[:, 320:384].rearrange("p (a n) -> p a n", a=TT)
        asg = cvf[:, 384:448].rearrange("p (a n) -> p a n", a=TT)
        rk = cvf[:, 448:512].rearrange("p (a n) -> p a n", a=TT)
        late = cvf[:, 512:576].rearrange("p (a n) -> p a n", a=TT)
        cnt = cvf[:, 576:577]
        thl = aqT[:].rearrange("p h t -> p (h t)")[:, 0:512].rearrange("p (a n) -> p a n", a=TT)
        hidl = cqT[:].rearrange("p h t -> p (h t)")[:, 0:512].rearrange("p (a n) -> p a n", a=TT)
        hidTl = cqT[:].rearrange("p h t -> p (h t)")[:, 512:1024].rearrange("p (f t) -> p f t", f=2)

        ident = cst[:, C_ID:C_ID + P]
        tri = cst[:, C_U:C_U + P]
        ones = cst[:, C_ONE:C_ONE + P]
        iota = cst[:, C_IOTA:C_IOTA + SLOTS]

        def mask_of(qt):
            return cst[:, C_M + P:C_M + 2 * P] if qt == 0 else cst[:, C_M:C_M + T]

        def keys(qt):
            return (qt + 1) * P

        x_in = sig("x_in", 0, 16)
        consts_in = sig("consts_in", 0, 16)
        sums_act = sig("sums_act", 6)
        xn1_ready = sig("xn1_ready", 2)
        rbias_in = sig("rbias_in", 0, 16)
        fgain_in = sig("fgain_in", 0, 16)
        up_in = sig("up_in", 1, 16)
        cb_in = sig("cb_in", 1, 16)
        slot_in = [sig(f"slot_in{s}", TRUNK_IN_SLOT[s] + NG - (s < EXTRA), 16) for s in range(RING)]
        extra_in = [sig(f"extra_in{n}", 1, 16) for n in range(EXTRA)]
        xn0_ready = sig("xn0_ready", 2)
        xnT_ps = sig("xnT_ps", 8)
        hT_dve = sig("hT_dve", 12)
        hT_act = sig("hT_act", 12)
        var_ready = sig("var_ready", 3)
        rstd_ready = sig("rstd_ready", 3)
        hi_made = sig("hi_made", HALVES)
        lo_made = sig("lo_made", HALVES)
        half_ps = sig("half_ps", HALVES)
        z_act = sig("z_act", 10)
        z_dve = sig("z_dve", 10)
        c_sb = sig("c_sb", 6)
        roped = sig("roped", 6)
        bn_ready = sig("bn_ready", 4)
        turn_ps = sig("turn_ps", 9)
        turn_act = sig("turn_act", 5)
        turn_dve = sig("turn_dve", 5)
        idx_ps = sig("idx_ps", 6)
        relu_sb = sig("relu_sb", 6)
        idx_used = sig("idx_used", 6)
        b_ps = sig("b_ps", 7)
        b_sb = sig("b_sb", 7)
        score_ps = sig("score_ps", 6)
        logit_sb = sig("logit_sb", 6)
        nmax_sb = sig("nmax_sb", 6)
        exp_sb = sig("exp_sb", 24)
        probs_sb = sig("probs_sb", 6)
        probsT_ps = sig("probsT_ps", 9)
        probsT_sb = sig("probsT_sb", 9)
        o_ps = sig("o_ps", 6)
        o_sb = sig("o_sb", 6)
        gate_sb = sig("gate_sb", 12)
        proj_ps = sig("proj_ps", 12)
        proj_used = sig("proj_used", 12)
        wo_half = sig("wo_half", 1)
        wo_ps = sig("wo_ps", 4)
        cb_masked = sig("cb_masked", H)
        routerT_ps = sig("routerT_ps", 1)
        routerT_sb = sig("routerT_sb", 1)
        route_ps = sig("route_ps", 1)
        gdiff_sb = sig("gdiff_sb", 2)
        gexp_sb = sig("gexp_sb", 2)
        asg_sb = sig("asg_sb", 1)
        rank_ps = sig("rank_ps", 1)
        count_ps = sig("count_ps", 1)
        flag_sb = sig("flag_sb", 1)
        sel_sb = sig("sel_sb", 4)
        selw_sb = sig("selw_sb", 2)
        selwT_ps = sig("selwT_ps", 4)
        selwT_sb = sig("selwT_sb", 4)
        gath_ps = sig("gath_ps", 2 * NG)
        xg_sb = sig("xg_sb", 2 * NG)
        gu_ps = sig("gu_ps", NG)
        tanh_sb = sig("tanh_sb", NG)
        silu_sb = sig("silu_sb", NG)
        hid_sb = sig("hid_sb", NG)
        hidT_ps = sig("hidT_ps", NG)
        hidT_sb = sig("hidT_sb", NG)
        down_half = sig("down_half", NG)
        down_ps = sig("down_ps", NG)
        yg_sb = sig("yg_sb", 2 * NG)
        sw_sb = sig("sw_sb", NG)
        comb_ps = sig("comb_ps", 4 * NG)
        x_added = sig("x_added", 4 + 4 * NG)
        late_gu_in = [sig(f"late_gu_in{l}", 0, 16) for l in range(L)]
        late_d_in = [sig(f"late_d_in{l}", 0, 16) for l in range(L)]
        late_gu_ps = [sig(f"late_gu_ps{l}", 0) for l in range(L)]
        late_tanh = [sig(f"late_tanh{l}", 0) for l in range(L)]
        late_silu = [sig(f"late_silu{l}", 0) for l in range(L)]
        late_hid = [sig(f"late_hid{l}", 0) for l in range(L)]
        late_hidT_ps = [sig(f"late_hidT_ps{l}", 0) for l in range(L)]
        late_hidT_sb = [sig(f"late_hidT_sb{l}", 0) for l in range(L)]
        late_added = [sig(f"late_added{l}", 0) for l in range(L)]
        late_done = [sig(f"late_done{l}", 0) for l in range(L)]
        late_settled = sig("late_settled", 1)
        out_ready = sig("out_ready", 0)
        out_done = sig("out_done", 0, 16)

        def slot(s):
            return ring[:, s, :]

        def slot_k(s, n, k=KC):
            return ring[:, s, 0:k * n].rearrange("p (k n) -> p k n", k=k)

        def freed(l, i):
            if i < SPLIT:
                return lo_made, l, 2 * i + 2
            if i < B_WO:
                return proj_ps, l, 4 * (i - B_PROJ) + 4
            if i == B_WO:
                return wo_half, l, 1
            if i == B_WO + 1:
                return wo_ps, l, 4

        def width(i):
            return TOKEN_BLOCKS[i][1] - TOKEN_BLOCKS[i][0] if i < len(TOKEN_BLOCKS) else 512

        def raw_half(n):
            i, h = n // 2, n % 2
            return slot_k(i % WAYS, width(i))[:, :, 256 * h:min(256 * h + 256, width(i))]

        def part_of(parts, n):
            m = min(256, width(n // 2) - 256 * (n % 2))
            return parts[:, n % 2, 0:KC * m].rearrange("p (k n) -> p k n", k=KC)

        def loop_sets(eng, body):
            body(0, True, False)
            with eng.Fori(1, NG - 1) as g:
                body(g, False, False)
            body(NG - 1, False, True)

        pool_const = sig("pool_const", 0)
        step = ctx.enter_context(nc.semaphore("step"))
        taken = [0]

        def steps(n):
            taken[0] += n
            return taken[0]

        fgain = vB[:].rearrange("p a n -> p (a n)")
        UNITS = [("c", 0), ("c", 1), ("b", 0), ("b", 1), ("a", 0), ("a", 1)]
        HEAD_AT = {"a": [0, 1, 2, 3], "b": [0, 2, 1, 3], "c": [0, 1, 2, 3]}
        PT_COUNT = [1, 3, 4, 6, 7, 9]
        SELW_BANKS = [3, 6, 7, 5]

        def copy_tokens(eng, l, tt, signal, copy, between=None):
            for i in range(4):
                if between:
                    between(2 * i + 2)
                eng.wait_ge(half_ps, at(half_ps, l, 2 * i + 2))
                b = ps[:, (4 + 2 * i + tt) % 8, :]
                if i == 0:
                    moves = [(zaq[:, tt, :], b)]
                elif i == 1:
                    moves = [(zkv[:, tt, :], b[:, 0:256]), (ziq[:, tt, 0:256], b[:, 256:512])]
                elif i == 2:
                    moves = [(ziq[:, tt, 256:512], b[:, 0:256]), (zik[:, tt, 0, :], b[:, 256:320]),
                             (zik[:, tt, 1, :], b[:, 256:320]), (ziw[:, tt, :], b[:, 320:328])]
                else:
                    moves = [(zb[:, tt, :], b[:, 0:384]), (zkr[:, tt, 0, :], b[:, 384:448]),
                             (zkr[:, tt, 1, :], b[:, 384:448])]
                for dst, src in moves:
                    copy(dst, src).then_inc(signal, 1)
                if between:
                    between(2 * i + 3)

        def any_late(eng, l):
            eng.wait_ge(flag_sb, at(flag_sb, l))
            return eng.value_load(flag[0:1, 0:1], min_val=0, max_val=1) > 0

        block = ctx.enter_context(nc.Block())

        @block.sync
        def _(sp):
            sp.dma_start(x[:], a["x"].rearrange("b (t p) d -> p (b t) d", p=P)).then_inc(x_in, 16)
            sp.dma_start(cst[:], a["consts"]).then_inc(consts_in, 16)
            sp.dma_start(small[:], a["small"].rearrange("l p n -> p l n")).then_inc(consts_in, 16)
            stream = a["stream"]

            def late_stream(l):
                with sp.If(any_late(sp, l)):
                    sp.wait_ge(gu_ps, at(gu_ps, l))
                    sp.wait_ge(down_ps, at(down_ps, l))

                    with sp.Fori(0, NG) as g:
                        for j in range(XG):
                            sp.wait_ge(late_done[l], at(late_done[l], 0, XG * g + (j + 1)))
                            i = g * PER_SET + (l * PER_LAYER + NT)
                            src = a["stream"][bass.ds(i + GU_SLOT[j], 1)].rearrange("b p n -> p (b n)")
                            sp.dma_start(ring[:, 0, :], src).then_inc(late_gu_in[l], 16)
                            src = a["stream"][bass.ds(i + D_SLOT[j], 1)].rearrange("b p n -> p (b n)")
                            h = (j % 2) * BLK // 2
                            sp.dma_start(ring[:, 1, 0:BLK // 2], src[:, h:h + BLK // 2]).then_inc(late_d_in[l], 16)
                    sp.wait_ge(late_done[l], at(late_done[l], 0, E + 1))

            for l in range(L):
                for i in range(NT):
                    s = i % WAYS
                    if i >= WAYS:
                        f, fl, fn = freed(l, i - WAYS)
                        sp.wait_ge(f, at(f, fl, fn))
                    elif l:
                        sp.wait_ge(gu_ps, at(gu_ps, l - 1, NG - 1 if i < EXTRA else NG))
                    n = KC * width(i) if i < SPLIT else BLK
                    sp.dma_start(ring[:, s, 0:n], stream[l * PER_LAYER + i, :, 0:n]).then_inc(slot_in[s], 16)

                def one_set(g, first, last):
                    for s in FIRST_SET if first else range(EXTRA if last else 0, PER_SET):
                        if s == "extra0" or s == "extra1":
                            n = int(s == "extra1")
                            if n:
                                sp.wait_ge(proj_ps, at(proj_ps, l))
                            else:
                                sp.wait_ge(half_ps, at(half_ps, l))
                                sp.wait_ge(score_ps, at(score_ps, l))
                            sp.dma_start(extra[n][:], stream[(l + 1) * PER_LAYER - PER_SET + n]).then_inc(extra_in[n], 16)
                            continue
                        kind = SET_ORDER[s][0]
                        if first and s >= WAYS:
                            sp.wait_ge(half_ps, at(half_ps, l))
                        elif first:
                            f, fl, fn = freed(l, NT - 1 - (NT - 1 - s) % WAYS)
                            sp.wait_ge(f, at(f, fl, fn))
                        else:
                            sp.wait_ge(gu_ps if kind == "gu" else down_ps, at(gu_ps if kind == "gu" else down_ps, l, g))
                        i = g * PER_SET + (l * PER_LAYER + NT + s)
                        src = stream[bass.ds(i, 1)].rearrange("b p n -> p (b n)")
                        sp.dma_start(ring[:, s, :], src).then_inc(slot_in[s], 16)
                loop_sets(sp, one_set)
                late_stream(l)

            for tt in range(TT):
                sp.wait_ge(out_ready, at(out_ready, 0, tt + 1))
                sp.dma_start(a["out"][0, tt * P:(tt + 1) * P, :], xn[:, tt, :]).then_inc(out_done, 16)
            sp.wait_ge(out_done, at(out_done, 0, TT))

        @block.gpsimd
        def _(pool):
            pool.memset(st[:, 40:44], -0.5).then_inc(pool_const, 1)
            pool.wait_ge(pool_const, at(pool_const, 0, 1))
            pool.dma_start(rbias[:], a["rbias"].rearrange("l n -> (l n)").partition_broadcast(P)
                           .rearrange("p (l n) -> p l n", l=L)).then_inc(rbias_in, 16)
            def low_part(l, n):
                pool.wait_ge(hi_made, at(hi_made, l, n + 1))
                pool.tensor_tensor(part_of(w_lo, n), raw_half(n), part_of(w_hi, n).bitcast(F32),
                                   ALU.subtract).then_inc(lo_made, 1)

            def rstd(l, n):
                lo, hi = ((0, 2), (4, 8), (0, 2))[n]
                pool.wait_ge(var_ready, at(var_ready, l, n + 1))
                pool.tensor_tensor(st[:, lo + 8:hi + 8], st[:, lo:hi],
                                   st[:, 40:40 + hi - lo], ALU.pow).then_inc(rstd_ready, 1)

            for l in range(L):
                if l:
                    pool.wait_ge(gu_ps, at(gu_ps, l - 1))
                pool.dma_start(wup[:], a["up"][l]).then_inc(up_in, 16)
                pool.dma_start(cbias[:].rearrange("p h t -> p (h t)"), a["rel"][l]).then_inc(cb_in, 16)
                rstd(l, 0)
                for n in range(2 * B_GL):
                    low_part(l, n)
                rstd(l, 1)
                pool.wait_ge(cb_in, at(cb_in, l))
                for h in range(H):
                    pool.tensor_tensor(cbias[:, h, :], cbias[:, h, :], mask_of(1), ALU.add).then_inc(cb_masked, 1)
                for n in range(2 * B_GL, HALVES):
                    low_part(l, n)
                rstd(l, 2)
            pool.wait_ge(selwT_ps, at(selwT_ps, L - 1))
            pool.dma_start(fgain, a["final_gain"].partition_broadcast(P)).then_inc(fgain_in, 16)
            pool.wait_ge(var_ready, at(var_ready, L, 1))
            pool.tensor_tensor(st[:, 8:10], st[:, 0:2], st[:, 40:42], ALU.pow).then_inc(rstd_ready, 1)

        @block.tensor
        def _(pe):
            def mm(out, lhsT, rhs, start=True, stop=True):
                return pe.matmul(out, lhsT, rhs, start=start, stop=stop)

            def late_products(l):
                with pe.If(any_late(pe, l)):
                    pe.wait_ge(down_ps, at(down_ps, l))
                    pe.sem_inc(late_done[l], 1)

                    with pe.Fori(0, NG) as g:
                        for j in range(XG):
                            e1 = XG * g + (j + 1)
                            pe.wait_ge(late_gu_in[l], at(late_gu_in[l], 0, e1))
                            w = ring[:, 0, :].rearrange("p (k n) -> p k n", k=KC)
                            for tt in range(TT):
                                for k in range(KC):
                                    ins = pe.matmul(ps[:, tt, :], hT[:, k, tt * P:(tt + 1) * P], w[:, k, :],
                                                    start=k == 0, stop=k == KC - 1)
                            ins.then_inc(late_gu_ps[l], 1)
                            pe.wait_ge(late_hid[l], at(late_hid[l], 0, TT * XG * g + TT * (j + 1)))
                            for f in range(2):
                                for tt in range(TT):
                                    ins = pe.transpose(ps[:, 2, f * T + tt * P:f * T + (tt + 1) * P],
                                                       hidl[:, tt, f * P:(f + 1) * P], ident)
                            ins.then_inc(late_hidT_ps[l], 1)
                            pe.wait_ge(late_hidT_sb[l], at(late_hidT_sb[l], 0, e1))
                            pe.wait_ge(late_d_in[l], at(late_d_in[l], 0, e1))
                            w = ring[:, 1, 0:BLK // 2].rearrange("p (f n) -> p f n", f=2)
                            for tt in range(TT):
                                for half in range(2):
                                    for f in range(2):
                                        ins = pe.matmul(ps[:, 4 + 2 * tt + half, :], hidTl[:, f, tt * P:(tt + 1) * P],
                                                        w[:, f, half * 512:(half + 1) * 512], start=f == 0, stop=f == 1)
                            ins.then_inc(late_done[l], 1)

            def arrived(l, i):
                pe.wait_ge(slot_in[i % WAYS], at(slot_in[i % WAYS], l, i // WAYS + 1))

            def turn_norm(l, half):
                for tt in range(TT):
                    if tt:
                        pe.wait_ge(xn1_ready, at(xn1_ready, l, half + 1))
                    else:
                        pe.wait_ge(xn0_ready, at(xn0_ready, l, half + 1))
                    for k in range(KC):
                        o = (k % 2) * T + tt * P
                        ins = pe.transpose(ps[:, k // 2, o:o + P], xn[:, tt, k * P:(k + 1) * P], ident)
                        if tt and k % 2:
                            ins.then_inc(xnT_ps, 1)

            def turned(l, k):
                if k % 4 == 0:
                    pe.wait_ge(hT_dve, at(hT_dve, l, 8 + k // 2 + 2))
                elif k % 4 == 2:
                    pe.wait_ge(hT_act, at(hT_act, l, 8 + k // 2 + 1))

            def tokens_by(l, bank, n, tt):
                hi, lo = part_of(w_hi, n), part_of(w_lo, n)
                o = 256 * (n % 2)
                out = ps[:, bank, o:o + hi.shape[2]]
                q = slice(tt * P, (tt + 1) * P)
                if tt == 0:
                    pe.wait_ge(hi_made, at(hi_made, l, n + 1))
                for k in range(KC):
                    if n == 0 and tt == 0:
                        pe.wait_ge(hT_act, at(hT_act, l, k + 1))
                    mm(out, hT_hi[:, k, q], hi[:, k, :], k == 0, False)
                    if n == 0 and tt == 0:
                        pe.wait_ge(hT_dve, at(hT_dve, l, k + 1))
                    mm(out, hT_lo[:, k, q], hi[:, k, :], False, False)
                if tt == 0:
                    pe.wait_ge(lo_made, at(lo_made, l, n + 1))
                for k in range(KC):
                    ins = mm(out, hT_hi[:, k, q], lo[:, k, :], False, k == KC - 1)
                return ins

            def features_by(l, bank, n):
                hi, lo = part_of(w_hi, n), part_of(w_lo, n)
                pe.wait_ge(hi_made, at(hi_made, l, n + 1))
                for m in range(2):
                    out = ps[:, bank, m * T:(m + 1) * T]
                    c = slice(m * P, (m + 1) * P)
                    for k in range(KC):
                        mm(out, hi[:, k, c], hT_hi[:, k, :], k == 0, False)
                        mm(out, hi[:, k, c], hT_lo[:, k, :], False, False)
                    if m == 0:
                        pe.wait_ge(lo_made, at(lo_made, l, n + 1))
                    for k in range(KC):
                        ins = mm(out, lo[:, k, c], hT_hi[:, k, :], False, k == KC - 1)
                return ins

            def gather(l, g):
                for q in range(2):
                    n = 2 * g + q
                    if not (isinstance(g, int) and g == 0):
                        pe.wait_ge(xg_sb, at(xg_sb, l, n - 1))
                    for k in range(4 * q, 4 * q + 4):
                        for tt in range(TT):
                            ins = mm(ps[:, q, (k % 4) * P:(k % 4 + 1) * P], xn[:, tt, k * P:(k + 1) * P],
                                     sel[:, tt, bass.ds(g * P, P)], tt == 0, tt == TT - 1)
                    ins.then_inc(gath_ps, 1)

            def gate_up(l, g, first, last):
                for j in range(XG):
                    if last and j < EXTRA:
                        pe.wait_ge(extra_in[j], at(extra_in[j], l))
                        continue
                    pe.wait_ge(slot_in[GU_SLOT[j]], at(slot_in[GU_SLOT[j]], l, TRUNK_IN_SLOT[GU_SLOT[j]] + 1 + g))
                pe.wait_ge(xg_sb, at(xg_sb, l, 2 * g + 2))
                if not first:
                    pe.wait_ge(hid_sb, at(hid_sb, l, g))
                for k in range(KC):
                    for j in range(XG):
                        w = extra[j][:] if last and j < EXTRA else ring[:, GU_SLOT[j], :]
                        w = w.rearrange("p (k n) -> p k n", k=KC)
                        ins = mm(ps[j * SLOTS:(j + 1) * SLOTS, 2, :], xg[:, k, j * SLOTS:(j + 1) * SLOTS],
                                 w[:, k, :], k == 0, k == KC - 1)
                ins.then_inc(gu_ps, 1)

            def turn_hidden(l, g):
                pe.wait_ge(hid_sb, at(hid_sb, l, g + 1))
                for f in range(2):
                    ins = pe.transpose(ps[:, 3, f * P:(f + 1) * P], hid[:, f * P:(f + 1) * P], ident)
                ins.then_inc(hidT_ps, 1)

            def down(l, g, first):
                pe.wait_ge(hidT_sb, at(hidT_sb, l, g + 1))
                for s in sorted(set(D_SLOT)):
                    pe.wait_ge(slot_in[s], at(slot_in[s], l, TRUNK_IN_SLOT[s] + 1 + g))
                if not first:
                    pe.wait_ge(yg_sb, at(yg_sb, l, 2 * g))
                for half in range(2):
                    for f in range(2):
                        for j in range(XG):
                            w = ring[:, D_SLOT[j], :].rearrange("p (e f n) -> p e f n", e=2, f=2)
                            ins = mm(ps[j * SLOTS:(j + 1) * SLOTS, 4 + half, :],
                                     hidT[:, f, j * SLOTS:(j + 1) * SLOTS],
                                     w[:, j % 2, f, half * 512:(half + 1) * 512], f == 0, f == 1)
                    if half:
                        ins.then_inc(down_ps, 1)
                    else:
                        ins.then_inc(down_half, 1)

            def combine(l, g, tt, bank):
                if tt == 0:
                    pe.wait_ge(yg_sb, at(yg_sb, l, 2 * g + 2))
                    pe.wait_ge(sw_sb, at(sw_sb, l, g + 1))
                if bank == 6:
                    pe.wait_ge(x_added, at(x_added, l, 4 * g + (4 + 2 * tt)))
                for half in range(2):
                    mm(ps[:, bank + half, :], sw[:, tt * P:(tt + 1) * P],
                       yg[:, half * 512:(half + 1) * 512]).then_inc(comb_ps, 1)

            pe.wait_ge(consts_in, at(consts_in, 0, 2))
            for l in range(L):
                turn_norm(l, 0)
                for n in range(2 * len(TOKEN_BLOCKS)):
                    bank = (4 + 2 * (n // 2)) % 8
                    tokens_by(l, bank, n, 0)
                    tokens_by(l, bank + 1, n, 1).then_inc(half_ps, 1)
                zdone = [1, 3, 7, 10]
                for n in range(4):
                    pe.wait_ge(z_act if n % 2 == 0 else z_dve, at(z_act if n % 2 == 0 else z_dve, l, zdone[n // 2]))
                    features_by(l, 4 + n, 2 * B_CQ + n).then_inc(half_ps, 1)
                pe.wait_ge(z_act, at(z_act, l, zdone[2]))
                pe.wait_ge(z_dve, at(z_dve, l, zdone[2]))
                for n in range(2 * B_CV, 2 * B_CV + 2):
                    tokens_by(l, 0, n, 0)
                    tokens_by(l, 1, n, 1).then_inc(half_ps, 1)
                pe.wait_ge(z_act, at(z_act, l, 10))
                pe.wait_ge(z_dve, at(z_dve, l, 10))
                for n in range(4):
                    src = zaq if n < 2 else ziq
                    pe.wait_ge(roped, at(roped, l, 1 if n < 2 else 3))
                    if n >= 2:
                        pe.wait_ge(c_sb, at(c_sb, l, n - 1))
                    for h in range(4):
                        ins = pe.transpose(ps[:, 2 + n, h * P:(h + 1) * P], src[:, n % 2, h * P:(h + 1) * P], ident)
                    ins.then_inc(turn_ps, 1)
                pe.wait_ge(roped, at(roped, l, 4))
                pe.wait_ge(c_sb, at(c_sb, l, 3))
                for tt in range(TT):
                    pe.transpose(ps[:, 6, tt * T:tt * T + P], zkv[:, tt, 0:HD], ident)
                    ins = pe.transpose(ps[:, 6, tt * T + P:tt * T + 2 * P],
                                       zik[:, tt].rearrange("p a n -> p (a n)"), ident)
                ins.then_inc(turn_ps, 1)
                pe.wait_ge(bn_ready, at(bn_ready, l, 4))
                pe.wait_ge(c_sb, at(c_sb, l, 4))
                for k in range(2):
                    for tt in range(TT):
                        ins = pe.transpose(ps[:, 7, k * T + tt * P:k * T + (tt + 1) * P],
                                           zb[:, tt, k * P:(k + 1) * P], ident)
                ins.then_inc(turn_ps, 1)
                pe.wait_ge(c_sb, at(c_sb, l, 5))
                for tt in range(TT):
                    ins = pe.transpose(ps[:, 0, tt * P:(tt + 1) * P], zb[:, tt, BQ:BQ + BKV], ident)
                ins.then_inc(turn_ps, 1)
                pe.wait_ge(turn_act, at(turn_act, l, 3))
                pe.wait_ge(turn_dve, at(turn_dve, l, 2))
                for n in range(6):
                    qt = 0 if n < 2 else 1
                    odd = n % 2
                    if n == 0:
                        pe.wait_ge(c_sb, at(c_sb, l, 6))
                    r = slice(64 * odd, 64 * odd + 64)
                    for m in range(4 if qt == 0 else 2):
                        pair = m if qt == 0 else 2 * ((n - 2) // 2) + m
                        ins = mm(ps[:, 1 + n, m * keys(qt):(m + 1) * keys(qt)], iqT[r, pair, qt * P:(qt + 1) * P],
                                 keysT[r, 1, 0:keys(qt)])
                    ins.then_inc(idx_ps, 1)
                pe.wait_ge(up_in, at(up_in, l))
                pe.wait_ge(turn_dve, at(turn_dve, l, 5))
                uq = wup[:, 0:2 * H * (HD + BR)].rearrange("p (k h n) -> p k h n", k=2, h=H)
                ukv = wup[:, 2 * H * (HD + BR):NUP].rearrange("p (h n) -> p h n", h=H)
                for tt in range(TT):
                    for k in range(2):
                        ins = mm(ps[:, 7, tt * H * BR:(tt + 1) * H * BR].rearrange("p (h n) -> p h n", h=H),
                                 bcqT[:, k, tt * P:(tt + 1) * P], uq[:, k, :, HD:HD + BR], k == 0, k == 1)
                ins.then_inc(b_ps, 1)
                for n in range(2):
                    if n == 1:
                        pe.wait_ge(relu_sb, at(relu_sb, l, 1))
                    for m in range(2):
                        for k in range(2):
                            ins = mm(ps[:, n, m * T:(m + 1) * T], uq[:, k, 2 * n + m, 0:HD], bcqT[:, k, :],
                                     k == 0, k == 1)
                    ins.then_inc(b_ps, 1)
                for n in range(2):
                    pe.wait_ge(relu_sb, at(relu_sb, l, 2 + n))
                    for m in range(2):
                        ins = mm(ps[:, 2 + n, m * T:(m + 1) * T], ukv[:, 2 * n + m, 0:HD], bckvT[:])
                    ins.then_inc(b_ps, 1)
                for tt in range(TT):
                    pe.wait_ge(relu_sb, at(relu_sb, l, 4 + tt))
                    ins = mm(ps[:, 4 + tt, :].rearrange("p (h n) -> p h n", h=H), bckvT[:, tt * P:(tt + 1) * P],
                             ukv[:, :, HD:2 * HD])
                    ins.then_inc(b_ps, 1)
                pe.wait_ge(roped, at(roped, l, 6))
                pe.wait_ge(relu_sb, at(relu_sb, l, 6))
                for pair in range(2):
                    for tt in range(TT):
                        ins = pe.transpose(ps[:, 6, pair * T + tt * P:pair * T + (tt + 1) * P],
                                           zqr[:, tt, pair * P:(pair + 1) * P], ident)
                ins.then_inc(turn_ps, 1)
                pe.wait_ge(b_sb, at(b_sb, l, 1))
                for tt in range(TT):
                    ins = pe.transpose(ps[:, 7, tt * P:(tt + 1) * P], zkr[:, tt].rearrange("p a n -> p (a n)"), ident)
                ins.then_inc(turn_ps, 1)

                pe.wait_ge(b_sb, at(b_sb, l, 7))
                pe.wait_ge(turn_act, at(turn_act, l, 5))

                def scores(u):
                    m, qt = UNITS[u]
                    n = keys(qt)
                    q = slice(qt * P, (qt + 1) * P)
                    if u:
                        pe.wait_ge(logit_sb, at(logit_sb, l, u))
                    for pos in range(H):
                        out = ps[:, 2 + pos // 2, (pos % 2) * T:(pos % 2) * T + n]
                        h = HEAD_AT[m][pos]
                        if m == "a":
                            ins = mm(out, aqT[:, h, q], keysT[:, 0, 0:n])
                        elif m == "c":
                            ins = mm(out, cqT[:, h, q], ckT[:, h, 0:n])
                        else:
                            r = slice(64 * (h % 2), 64 * (h % 2) + 64)
                            mm(out, qnT[:, h, q], knT[:, h, 0:n], True, False)
                            ins = mm(out, qrT[r, h // 2, q], krT[r, 0:n], False, True)
                    ins.then_inc(score_ps, 1)

                def turn_probs(u):
                    m, qt = UNITS[u]
                    pe.wait_ge(probs_sb, at(probs_sb, l, u + 1))
                    if u:
                        pe.wait_ge(probsT_sb, at(probsT_sb, l, PT_COUNT[u - 1]))
                    for kt in range(qt + 1):
                        for pos in range(H):
                            ins = pe.transpose(ps[:, 4 + kt, pos * P:(pos + 1) * P],
                                               probs[:, pos, kt * P:(kt + 1) * P], ident)
                        ins.then_inc(probsT_ps, 1)

                def values(u):
                    m, qt = UNITS[u]
                    pe.wait_ge(probsT_sb, at(probsT_sb, l, PT_COUNT[u]))
                    if u:
                        pe.wait_ge(o_sb, at(o_sb, l, u))
                    for pos in range(H):
                        h = HEAD_AT[m][pos]
                        for kt in range(qt + 1):
                            v = {"a": zkv[:, kt, HD:2 * HD], "b": vB[:, kt, h * HD:(h + 1) * HD],
                                 "c": cv[:, kt, h * HD:(h + 1) * HD]}[m]
                            ins = mm(ps[:, 6, pos * P:(pos + 1) * P], v, probsT[:, kt, pos, :], kt == 0, kt == qt)
                    ins.then_inc(o_ps, 1)

                for n in range(12):
                    if 1 <= n <= len(UNITS):
                        turn_probs(n - 1)
                    if n < len(UNITS):
                        scores(n)
                    if 1 <= n <= len(UNITS):
                        values(n - 1)
                    if n >= 2:
                        pe.wait_ge(gate_sb, at(gate_sb, l, n - 1))
                    features_by(l, n % 2, 2 * B_GL + n).then_inc(half_ps, 1)

                for n in range(12):
                    m, c = PROJ_ORDER[n // 4], 2 * (n % 4)
                    i = B_PROJ + n // 4
                    if n % 4 == 0:
                        arrived(l, i)
                        pe.wait_ge(o_sb, at(o_sb, l, 2 * (n // 4) + 2))
                    if n < 2:
                        pe.wait_ge(gate_sb, at(gate_sb, l, 11 + n))
                    elif n < 4:
                        pe.wait_ge(logit_sb, at(logit_sb, l, 6))
                    else:
                        pe.wait_ge(proj_used, at(proj_used, l, n - 3))
                    w = slot_k(i % WAYS, D, 4)
                    o = {"a": aqT, "b": qnT, "c": cqT}[m]
                    for cc in (c, c + 1):
                        for h in range(H):
                            ins = mm(ps[:, n % 4, (cc - c) * T:(cc - c + 1) * T], w[:, h, cc * P:(cc + 1) * P],
                                     o[:, h, :], h == 0, h == H - 1)
                    ins.then_inc(proj_ps, 1)
                for part in range(2):
                    arrived(l, B_WO + part)
                    w = slot_k((B_WO + part) % WAYS, D, 4)
                    for n in range(4):
                        tt, half = n // 2, n % 2
                        for k in range(4 * part, 4 * part + 4):
                            if n == 0 and k % 2 == 0:
                                pe.wait_ge(proj_used, at(proj_used, l, 8 + k // 2 + 1))
                            ins = mm(ps[:, 4 + n, :], mixT[:, k, tt * P:(tt + 1) * P],
                                     w[:, k % 4, half * 512:(half + 1) * 512], k == 0, k == KC - 1)
                        if part:
                            ins.then_inc(wo_ps, 1)
                    if not part:
                        ins.then_inc(wo_half, 1)

                turn_norm(l, 1)
                for k in range(KC):
                    turned(l, k)
                    ins = mm(ps[0:G + E, 4, 0:T], small[:, l, S_R + k * (G + E):S_R + (k + 1) * (G + E)],
                             hT[:, k, :], k == 0, k == KC - 1)
                ins.then_inc(routerT_ps, 1)
                pe.wait_ge(routerT_sb, at(routerT_sb, l))
                for tt in range(TT):
                    ins = pe.transpose(ps[:, 6, tt * (G + E):(tt + 1) * (G + E)], routerT[:, tt * P:(tt + 1) * P],
                                       cst[0:G + E, C_ID:C_ID + G + E])
                ins.then_inc(route_ps, 1)
                pe.wait_ge(asg_sb, at(asg_sb, l))
                mm(ps[:, 5, 0:E], tri, asg[:, 0, :])
                mm(ps[:, 5, E:2 * E], ones, asg[:, 0, :], True, False)
                ins = mm(ps[:, 5, E:2 * E], tri, asg[:, 1, :], False, True)
                ins.then_inc(rank_ps, 1)
                mm(ps[:, 4, 0:E], ones, asg[:, 0, :], True, False)
                ins = mm(ps[:, 4, 0:E], ones, asg[:, 1, :], False, True)
                ins.then_inc(count_ps, 1)
                for tt in range(TT):
                    pe.wait_ge(sel_sb, at(sel_sb, l, tt + 1))
                gather(l, 0)

                def turn_weights():
                    for tt in range(TT):
                        pe.wait_ge(selw_sb, at(selw_sb, l, tt + 1))
                    for n, bank in enumerate(SELW_BANKS):
                        for m in range(2):
                            for tt in range(TT):
                                ins = pe.transpose(ps[:, bank, m * T + tt * P:m * T + (tt + 1) * P],
                                                   selws[tt][:, (2 * n + m) * P:(2 * n + m + 1) * P], ident)
                        ins.then_inc(selwT_ps, 1)

                def one_set(g, first, last):
                    gate_up(l, g, first, last)
                    if first:
                        turn_weights()
                    else:
                        combine(l, g - 1, 0, 6)
                    if last:
                        turn_hidden(l, g)
                    else:
                        gather(l, g + 1)
                    if not first:
                        combine(l, g - 1, 1, 0 if last else 6)
                    if first:
                        pe.wait_ge(selwT_sb, at(selwT_sb, l, 4))
                    if not last:
                        turn_hidden(l, g)
                    down(l, g, first)
                loop_sets(pe, one_set)
                combine(l, NG - 1, 0, 6)
                combine(l, NG - 1, 1, 4)
                late_products(l)

        @block.scalar
        def _(act):
            def copy(out, in_, scale=1.0):
                return act.activation(out, in_, ACT.Copy, scale=scale)

            def late_tanhs(l):
                with act.If(any_late(act, l)):
                    with act.Fori(0, NG) as g:
                        for j in range(XG):
                            e1 = XG * g + (j + 1)
                            act.wait_ge(late_gu_ps[l], at(late_gu_ps[l], 0, e1))
                            for tt in range(TT):
                                act.activation(thl[:, tt, :], ps[:, tt, 0:FE], ACT.Tanh, scale=0.5).then_inc(late_tanh[l], 1)
                            act.wait_ge(late_hidT_ps[l], at(late_hidT_ps[l], 0, e1))
                            act.activation(hidTl, ps[:, 2, :].rearrange("p (f t) -> p f t", f=2),
                                           ACT.Copy).then_inc(late_hidT_sb[l], 1)

            def square(l, n):
                tt, half = n // 2, n % 2
                act.activation(junk[:, n, :], x[:, tt, half * 512:(half + 1) * 512], ACT.Square, scale=D ** -0.5,
                               accum_out=st[:, 32 + n:33 + n]).then_inc(sums_act, 1)

            def high_part(l, n):
                if n >= HALVES:
                    return
                s = n // 2 % WAYS
                act.wait_ge(slot_in[s], at(slot_in[s], l, n // 2 // WAYS + 1))
                if n >= 2:
                    act.wait_ge(half_ps, at(half_ps, l, n - 1))
                elif l:
                    act.wait_ge(down_ps, at(down_ps, l - 1))
                copy(part_of(w_hi, n), raw_half(n)).then_inc(hi_made, 1)

            def turned_norm(l, half):
                act.wait_ge(rstd_ready, at(rstd_ready, l, 3 if half else 1))
                copy(xn[:, 1, :], x[:, 1, :], st[:, 9:10]).then_inc(xn1_ready, 1)
                if not l and not half:
                    act.wait_ge(consts_in, at(consts_in, 0, 2))
                for k in (2, 3, 6, 7) if half else range(KC):
                    act.wait_ge(xnT_ps, at(xnT_ps, l, 4 * half + k // 2 + 1))
                    gain = small[:, l, (S_GF if half else S_GA) + k:(S_GF if half else S_GA) + k + 1]
                    dst = hT if half else hT_hi
                    copy(dst[:, k, :], ps[:, k // 2, (k % 2) * T:(k % 2 + 1) * T], gain).then_inc(hT_act, 1)

            act.wait_ge(x_in, at(x_in, 0, 1))
            for l in range(L):
                if l:
                    act.wait_ge(late_settled, at(late_settled, l - 1, 1))
                for n in range(2):
                    square(l, n)
                if l:
                    high_part(l, 0)
                turned_norm(l, 0)
                if not l:
                    high_part(l, 0)
                high_part(l, 1)

                def next_high(n):
                    high_part(l, n)
                copy_tokens(act, l, 0, z_act, copy, next_high)
                for n in range(4):
                    high_part(l, 2 * B_CQ + n + 2)
                    act.wait_ge(half_ps, at(half_ps, l, 2 * B_CQ + n + 1))
                    dst = (cqT if n < 2 else ckT)[:, 2 * (n % 2):2 * (n % 2) + 2, :]
                    copy(dst, ps[:, 4 + n, :].rearrange("p (m t) -> p m t", m=2)).then_inc(c_sb, 1)
                for tt in range(TT):
                    high_part(l, 2 * B_CV + tt + 2)
                    act.wait_ge(half_ps, at(half_ps, l, 2 * B_CV + 2))
                    copy(cv[:, tt, :], ps[:, tt, :]).then_inc(c_sb, 1)
                act.wait_ge(turn_ps, at(turn_ps, l, 1))
                copy(aqT[:, :, 0:P], ps[:, 2, :].rearrange("p (h t) -> p h t", h=4)).then_inc(turn_act, 1)
                act.wait_ge(turn_ps, at(turn_ps, l, 3))
                copy(iqT[:, :, 0:P], ps[:, 4, :].rearrange("p (h t) -> p h t", h=4)).then_inc(turn_act, 1)
                act.wait_ge(turn_ps, at(turn_ps, l, 5))
                copy(keysT[:].rearrange("p s (t c) -> p t s c", c=P),
                                 ps[:, 6, :].rearrange("p (t s c) -> p t s c", t=TT, s=2)).then_inc(turn_act, 1)
                for n in range(6):
                    act.wait_ge(idx_ps, at(idx_ps, l, n + 1))
                    if n >= 2:
                        act.wait_ge(idx_used, at(idx_used, l, n - 1))
                    else:
                        act.wait_ge(roped, at(roped, l, 5))
                    act.activation(relu[:, n % 2, :], ps[:, 1 + n, :], ACT.Relu).then_inc(relu_sb, 1)
                act.wait_ge(b_ps, at(b_ps, l, 1))
                copy(zqr, ps[:, 7, :].rearrange("p (a n) -> p a n", a=TT)).then_inc(b_sb, 1)
                for n in range(2):
                    act.wait_ge(b_ps, at(b_ps, l, 2 + n))
                    copy(qnT[:, 2 * n:2 * n + 2, :], ps[:, n, :].rearrange("p (m t) -> p m t", m=2)).then_inc(b_sb, 1)
                for n in range(2):
                    act.wait_ge(b_ps, at(b_ps, l, 4 + n))
                    copy(knT[:, 2 * n:2 * n + 2, :], ps[:, 2 + n, :].rearrange("p (m t) -> p m t", m=2)).then_inc(b_sb, 1)
                for tt in range(TT):
                    act.wait_ge(b_ps, at(b_ps, l, 6 + tt))
                    copy(vB[:, tt, :], ps[:, 4 + tt, :]).then_inc(b_sb, 1)
                act.wait_ge(turn_ps, at(turn_ps, l, 8))
                copy(qrT, ps[:, 6, :].rearrange("p (m t) -> p m t", m=2)).then_inc(turn_act, 1)
                act.wait_ge(turn_ps, at(turn_ps, l, 9))
                copy(krT, ps[:, 7, 0:T]).then_inc(turn_act, 1)

                for n in range(12):
                    if 1 <= n <= len(UNITS):
                        u = n - 1
                        m, qt = UNITS[u]
                        for kt in range(qt + 1):
                            act.wait_ge(probsT_ps, at(probsT_ps, l, (PT_COUNT[u - 1] if u else 0) + kt + 1))
                            if u:
                                act.wait_ge(o_ps, at(o_ps, l, u))
                            copy(probsT[:, kt], ps[:, 4 + kt, :].rearrange("p (h q) -> p h q", h=H)).then_inc(probsT_sb, 1)
                        act.wait_ge(o_ps, at(o_ps, l, u + 1))
                        dst = {"a": aqT, "b": qnT, "c": cqT}[m]
                        src = ps[:, 6, :].rearrange("p (h q) -> p h q", h=H)
                        if m == "b":
                            dst = dst[:].rearrange("p (s o) t -> p o s t", o=2)[:, :, :, qt * P:(qt + 1) * P]
                            src = ps[:, 6, :].rearrange("p (o s q) -> p o s q", o=2, s=2)
                        else:
                            dst = dst[:, :, qt * P:(qt + 1) * P]
                        copy(dst, src).then_inc(o_sb, 1)
                    if n < len(UNITS):
                        m, qt = UNITS[n]
                        act.wait_ge(nmax_sb, at(nmax_sb, l, n + 1))
                        if n:
                            act.wait_ge(probsT_ps, at(probsT_ps, l, PT_COUNT[n - 1]))
                        for pos in range(H):
                            act.activation(probs[:, pos, 0:keys(qt)], logits[:, pos, 0:keys(qt)], ACT.Exp,
                                                     bias=st[:, 16 + pos:17 + pos], accum_out=st[:, 20 + pos:21 + pos]).then_inc(exp_sb, 1)
                    act.wait_ge(half_ps, at(half_ps, l, 2 * B_GL + n + 1))
                    if n == SCORE_GATE:
                        act.wait_ge(logit_sb, at(logit_sb, l, 6))
                    c = 2 * n
                    act.activation(gates[:, c:c + 2, :], ps[:, n % 2, :].rearrange("p (m t) -> p m t", m=2),
                                              ACT.Tanh, scale=0.5).then_inc(gate_sb, 1)
                    high_part(l, 2 * B_GL + n + 2)

                for n in range(4):
                    act.wait_ge(x_added, at(x_added, l, n + 1))
                    square(l, n)
                turned_norm(l, 1)
                act.wait_ge(routerT_ps, at(routerT_ps, l))
                copy(routerT, ps[0:G + E, 4, 0:T]).then_inc(routerT_sb, 1)
                act.wait_ge(gdiff_sb, at(gdiff_sb, l, 1))
                act.activation(eg, eg, ACT.Exp).then_inc(gexp_sb, 1)
                act.wait_ge(gdiff_sb, at(gdiff_sb, l, 2))
                act.activation(rw[:, 1, :], rw[:, 0, :], ACT.Exp).then_inc(gexp_sb, 1)

                def one_set(g, first, last):
                    act.wait_ge(gu_ps, at(gu_ps, l, g + 1))
                    if not first:
                        act.wait_ge(hid_sb, at(hid_sb, l, g))
                    act.activation(th, ps[:, 2, 0:FE], ACT.Tanh, scale=0.5).then_inc(tanh_sb, 1)
                    if first:
                        for n, bank in enumerate(SELW_BANKS):
                            act.wait_ge(selwT_ps, at(selwT_ps, l, n + 1))
                            copy(selwT[:, 2 * n:2 * n + 2, :],
                                 ps[:, bank, :].rearrange("p (g t) -> p g t", g=2)).then_inc(selwT_sb, 1)
                        act.wait_ge(selwT_sb, at(selwT_sb, l, 4))
                    else:
                        act.wait_ge(comb_ps, at(comb_ps, l, 4 * g))
                    act.activation(sw, selwT[:, bass.ds(g, 1), :].rearrange("p g t -> p (g t)"),
                                            ACT.Copy).then_inc(sw_sb, 1)
                    act.wait_ge(hidT_ps, at(hidT_ps, l, g + 1))
                    copy(hidT, ps[:, 3, 0:2 * P].rearrange("p (f s) -> p f s", f=2)).then_inc(hidT_sb, 1)
                    for half in range(2):
                        if half:
                            act.wait_ge(down_ps, at(down_ps, l, g + 1))
                        else:
                            act.wait_ge(down_half, at(down_half, l, g + 1))
                            if not first:
                                act.wait_ge(comb_ps, at(comb_ps, l, 4 * g))
                        copy(yg[:, half * 512:(half + 1) * 512], ps[:, 4 + half, :]).then_inc(yg_sb, 1)
                loop_sets(act, one_set)
                late_tanhs(l)

            act.wait_ge(late_settled, at(late_settled, L - 1, 1))
            for n in range(2):
                square(L, n)

        @block.vector
        def _(dve):
            V = dve

            def copy(out, in_, scale=None):
                if scale is None:
                    return V.tensor_copy(out, in_)
                return V.tensor_scalar(out, in_, scale, None, ALU.mult)

            def route(l):
                V.wait_ge(route_ps, at(route_ps, l))
                V.wait_ge(rbias_in, at(rbias_in, 0, 1))
                V.tensor_tensor(lg, ps[:, 6, 0:2 * (G + E)].rearrange("p (a n) -> p a n", a=TT),
                                             rbias[:, l, :].unsqueeze(1).to_broadcast([P, TT, G + E]), ALU.add).then_inc(step, 1)
                V.wait_ge(step, steps(1))
                V.memset(g8[:], REPL).then_inc(step, 1)
                V.wait_ge(step, steps(1))
                V.tensor_copy(g8[:, :, 0:G], lg[:, :, 0:G]).then_inc(step, 1)
                V.wait_ge(step, steps(1))
                for tt in range(TT):
                    V.max(m8[:, tt, :], g8[:, tt, :]).then_inc(step, 1)
                V.wait_ge(step, steps(2))
                for tt in range(TT):
                    V.max_index(i8[:, tt, :], m8[:, tt, :], g8[:, tt, :]).then_inc(step, 1)
                V.wait_ge(step, steps(2))
                V.tensor_copy(fi[:, :, 0:1], i8[:, :, 0:1]).then_inc(step, 1)
                V.tensor_tensor(eg, lg[:, :, 0:G], m8[:, :, 0:1].to_broadcast([P, TT, G]), ALU.subtract).then_inc(step, 1)
                V.wait_ge(step, steps(2))
                V.tensor_tensor(ohg, iota[:, 0:G].unsqueeze(1).to_broadcast([P, TT, G]),
                                            fi[:, :, 0:1].to_broadcast([P, TT, G]), ALU.is_equal).then_inc(gdiff_sb, 1)
                V.wait_ge(gdiff_sb, at(gdiff_sb, l, 1))
                for tt in range(TT):
                    V.tensor_tensor(prod[:, tt, :].rearrange("p (g e) -> p g e", g=G),
                                               lg[:, tt, G:G + E].rearrange("p (g e) -> p g e", g=G),
                                               ohg[:, tt, :].unsqueeze(2).to_broadcast([P, G, EPG]), ALU.mult).then_inc(step, 1)
                V.wait_ge(step, steps(2))
                for tt in range(TT):
                    V.tensor_reduce(ein[:, tt, :], prod[:, tt, :].rearrange("p (g e) -> p e g", g=G),
                                               AX_X, ALU.add).then_inc(step, 1)
                V.wait_ge(step, steps(2))
                for tt in range(TT):
                    V.max(e8[:, tt, :], ein[:, tt, :]).then_inc(step, 1)
                V.wait_ge(step, steps(2))
                for tt in range(TT):
                    V.max_index(j8[:, tt, :], e8[:, tt, :], ein[:, tt, :]).then_inc(step, 1)
                V.wait_ge(step, steps(2))
                V.tensor_copy(fi[:, :, 1:3], j8[:, :, 0:2]).then_inc(step, 1)
                V.wait_ge(step, steps(1))
                V.tensor_tensor(rw[:, 0, :], e8[:, :, 1], e8[:, :, 0], ALU.subtract).then_inc(gdiff_sb, 1)
                V.tensor_tensor(oh1, iota[:, 0:EPG].unsqueeze(1).to_broadcast([P, TT, EPG]),
                                             fi[:, :, 1:2].to_broadcast([P, TT, EPG]), ALU.is_equal).then_inc(step, 1)
                V.tensor_tensor(oh2, iota[:, 0:EPG].unsqueeze(1).to_broadcast([P, TT, EPG]),
                                          fi[:, :, 2:3].to_broadcast([P, TT, EPG]), ALU.is_equal).then_inc(step, 1)
                V.wait_ge(step, steps(2))
                V.tensor_tensor(ce, oh1, oh2, ALU.add).then_inc(step, 1)
                V.wait_ge(step, steps(1))
                for tt in range(TT):
                    last = V.tensor_tensor(asg[:, tt, :].rearrange("p (g e) -> p g e", g=G),
                                           ohg[:, tt, :].unsqueeze(2).to_broadcast([P, G, EPG]),
                                           ce[:, tt, :].unsqueeze(1).to_broadcast([P, G, EPG]), ALU.mult)
                    if tt == 0:
                        last.then_inc(step, 1)
                        V.wait_ge(step, steps(1))
                last.then_inc(asg_sb, 1)
                V.wait_ge(gexp_sb, at(gexp_sb, l, 2))
                V.tensor_reduce(rw[:, 2, :], eg, AX_X, ALU.add).then_inc(step, 1)
                V.tensor_scalar(rw[:, 3, :], rw[:, 1, :], 1.0, None, ALU.add).then_inc(step, 1)
                V.wait_ge(step, steps(2))
                V.tensor_tensor(rw[:, 4, :], rw[:, 2, :], rw[:, 3, :], ALU.mult).then_inc(step, 1)
                V.wait_ge(step, steps(1))
                V.reciprocal(rw[:, 5, :], rw[:, 4, :]).then_inc(step, 1)
                V.wait_ge(step, steps(1))
                V.tensor_scalar(rw[:, 6, :], rw[:, 5, :], 0.5, None, ALU.mult).then_inc(step, 1)
                V.wait_ge(step, steps(1))
                V.tensor_tensor(rw[:, 7, :], rw[:, 6, :], rw[:, 1, :], ALU.mult).then_inc(step, 1)
                V.wait_ge(step, steps(1))
                V.tensor_tensor(oh1, oh1, rw[:, 6, :].unsqueeze(2).to_broadcast([P, TT, EPG]), ALU.mult).then_inc(step, 1)
                V.tensor_tensor(oh2, oh2, rw[:, 7, :].unsqueeze(2).to_broadcast([P, TT, EPG]), ALU.mult).then_inc(step, 1)
                V.wait_ge(step, steps(2))
                V.tensor_tensor(ce, oh1, oh2, ALU.add).then_inc(step, 1)
                V.wait_ge(step, steps(1))
                for tt in range(TT):
                    V.tensor_tensor(comb[:, tt, :].rearrange("p (g e) -> p g e", g=G),
                                               ohg[:, tt, :].unsqueeze(2).to_broadcast([P, G, EPG]),
                                               ce[:, tt, :].unsqueeze(1).to_broadcast([P, G, EPG]), ALU.mult).then_inc(step, 1)
                V.wait_ge(step, steps(2))
                V.wait_ge(rank_ps, at(rank_ps, l))
                V.wait_ge(asg_sb, at(asg_sb, l))
                V.scalar_tensor_tensor(rk, ps[:, 5, 0:2 * E].rearrange("p (a n) -> p a n", a=TT), 1.0,
                                                    asg, ALU.add, ALU.mult).then_inc(step, 1)
                V.wait_ge(step, steps(1))
                V.tensor_scalar(rk, rk, -1.0, None, ALU.add).then_inc(step, 1)
                V.wait_ge(step, steps(1))
                for lo, hi in ((0, XG), (XG, E)):
                    for tt in range(TT):
                        V.tensor_tensor(sel[:, tt, lo * SLOTS:hi * SLOTS].rearrange("p (e s) -> p e s", e=hi - lo),
                                        iota.unsqueeze(1).to_broadcast([P, hi - lo, SLOTS]),
                                        rk[:, tt, lo:hi].unsqueeze(2).to_broadcast([P, hi - lo, SLOTS]),
                                        ALU.is_equal).then_inc(sel_sb, 1)
                for tt in range(TT):
                    V.wait_ge(sel_sb, at(sel_sb, l, TT + tt + 1))
                    V.tensor_tensor(selws[tt].rearrange("p (e s) -> p e s", e=E),
                                               sel[:, tt, :].rearrange("p (e s) -> p e s", e=E),
                                               comb[:, tt, :].unsqueeze(2).to_broadcast([P, E, SLOTS]), ALU.mult).then_inc(selw_sb, 1)
                V.tensor_scalar(late, rk, LATE_FROM - 0.5, None, ALU.is_gt).then_inc(step, 1)
                V.wait_ge(count_ps, at(count_ps, l))
                V.tensor_reduce(cnt, ps[:, 4, 0:E], AX_X, ALU.max).then_inc(step, 1)
                V.wait_ge(step, steps(2))
                V.tensor_tensor(late, late, comb, ALU.mult).then_inc(step, 1)
                V.wait_ge(step, steps(1))
                V.tensor_scalar(flag[:], cnt, LATE_FROM + 0.5, None, ALU.is_gt).then_inc(flag_sb, 1)

            def late_sums(l):
                with V.If(any_late(V, l)):
                    with V.Fori(0, NG) as g:
                        for j in range(XG):
                            for tt in range(TT):
                                n = TT * XG * g + (TT * j + tt + 1)
                                V.wait_ge(late_tanh[l], at(late_tanh[l], 0, n))
                                V.scalar_tensor_tensor(thl[:, tt, :], thl[:, tt, :], 1.0, ps[:, tt, 0:FE],
                                                       ALU.add, ALU.mult).then_inc(late_silu[l], 1)
                                V.wait_ge(late_silu[l], at(late_silu[l], 0, n))
                                w = late[:, tt, bass.ds(XG * g + j, 1)]
                                V.scalar_tensor_tensor(hidl[:, tt, :], thl[:, tt, :], w, ps[:, tt, FE:2 * FE],
                                                       ALU.mult, ALU.mult).then_inc(late_hid[l], 1)
                            V.wait_ge(late_done[l], at(late_done[l], 0, XG * g + (j + 2)))
                            for n in range(4):
                                xs = x[:, n // 2, (n % 2) * 512:(n % 2 + 1) * 512]
                                ins = V.tensor_tensor(xs, xs, ps[:, 4 + n, :], ALU.add)
                                ins.then_inc(late_added[l], 1)
                            V.wait_ge(late_added[l], at(late_added[l], 0, 4 * XG * g + 4 * (j + 1)))

            def mean_square(l, half):
                if not half:
                    for n in (2, 3):
                        xs = x[:, 1, (n - 2) * 512:(n - 1) * 512]
                        V.tensor_tensor_reduce(junk[:, n, :], xs, xs, 1.0 / D, 0.0,
                                               ALU.mult, ALU.add, st[:, 32 + n:33 + n]).then_inc(step, 1)
                    V.wait_ge(step, steps(2))
                V.wait_ge(sums_act, at(sums_act, l, 6 if half else 2))
                sums = st[:, 32:36].rearrange("p (a n) -> p n a", a=TT)
                V.scalar_tensor_tensor(st[:, 0:2], sums[:, 0, :], EPS, sums[:, 1, :], ALU.add, ALU.add).then_inc(var_ready, 1)

            def norm(l, half):
                mean_square(l, half)
                V.wait_ge(rstd_ready, at(rstd_ready, l, 3 if half else 1))
                V.tensor_scalar(xn[:, 0, :], x[:, 0, :], st[:, 8:9], None, ALU.mult).then_inc(xn0_ready, 1)
                if not l and not half:
                    V.wait_ge(consts_in, at(consts_in, 0, 2))
                for k in (0, 1, 4, 5) if half else range(KC):
                    gain = small[:, l, (S_GF if half else S_GA) + k:(S_GF if half else S_GA) + k + 1]
                    if not half:
                        V.wait_ge(hT_act, at(hT_act, l, 2 * (k // 2) + 2))
                        V.scalar_tensor_tensor(hT_lo[:, k, :], ps[:, k // 2, (k % 2) * T:(k % 2 + 1) * T], gain,
                                               hT_hi[:, k, :].bitcast(F32), ALU.mult, ALU.subtract).then_inc(hT_dve, 1)
                        continue
                    V.wait_ge(xnT_ps, at(xnT_ps, l, 4 + k // 2 + 1))
                    copy(hT[:, k, :], ps[:, k // 2, (k % 2) * T:(k % 2 + 1) * T], gain).then_inc(hT_dve, 1)

            def rope(l, k, view, n, rot, oc, os):
                if k:
                    V.wait_ge(roped, at(roped, l, k))
                size = TT * n * rot
                t1 = rope1[:, 0:size].rearrange("p (a n r) -> p a n r", a=TT, n=n)
                t2 = rope2[:, 0:size].rearrange("p (a n r) -> p a n r", a=TT, n=n)
                cos = cst[:, oc:oc + TT * rot].rearrange("p (a r) -> p a r", a=TT).unsqueeze(2)
                sin = cst[:, os:os + TT * rot].rearrange("p (a r) -> p a r", a=TT).unsqueeze(2)
                hf = rot // 2
                z = view[:, :, :, 0:rot]
                V.tensor_tensor(t1, z, cos.to_broadcast([P, TT, n, rot]), ALU.mult).then_inc(step, 1)
                V.tensor_tensor(t2[:, :, :, 0:hf], z[:, :, :, hf:rot],
                                    sin[:, :, :, 0:hf].to_broadcast([P, TT, n, hf]), ALU.mult).then_inc(step, 1)
                V.tensor_tensor(t2[:, :, :, hf:rot], z[:, :, :, 0:hf],
                                    sin[:, :, :, hf:rot].to_broadcast([P, TT, n, hf]), ALU.mult).then_inc(step, 1)
                V.wait_ge(step, steps(3))
                V.tensor_tensor(z, t1, t2, ALU.add).then_inc(roped, 1)

            def heads(t, n):
                return t.rearrange("p a (n r) -> p a n r", n=n)

            def index_score(l, qt):
                n = keys(qt)
                out = score[:, qt, 0:n]
                first = True
                for b in (range(2) if qt == 0 else range(2, 6)):
                    V.wait_ge(relu_sb, at(relu_sb, l, b + 1))
                    count = 4 if qt == 0 else 2
                    for m in range(count):
                        pair = m if qt == 0 else 2 * ((b - 2) // 2) + m
                        h = 2 * pair + b % 2
                        r = relu[:, b % 2, m * n:(m + 1) * n]
                        w = ziw[:, qt, h:h + 1]
                        if first:
                            ins = V.tensor_scalar(out, r, w, None, ALU.mult)
                        else:
                            ins = V.scalar_tensor_tensor(out, r, w, out, ALU.mult, ALU.add)
                        first = False
                        if m == count - 1:
                            ins.then_inc(idx_used, 1)
                            V.wait_ge(idx_used, at(idx_used, l, b + 1))
                        else:
                            ins.then_inc(step, 1)
                            V.wait_ge(step, steps(1))
                V.tensor_tensor(out, out, mask_of(qt), ALU.add).then_inc(step, 1)
                V.wait_ge(step, steps(1))

            def top_keys(qt):
                out = score[:, qt, 0:keys(qt)]
                for _ in range(TOPK // 8):
                    V.max(st8[:], out).then_inc(step, 1)
                    V.wait_ge(step, steps(1))
                    V.match_replace(out, st8[:], out, REPL).then_inc(step, 1)
                    V.wait_ge(step, steps(1))
                V.tensor_scalar(out, out, REPL / 2, NEG, ALU.is_gt, ALU.mult).then_inc(step, 1)
                V.wait_ge(step, steps(1))

            def softmax(l, u):
                m, qt = UNITS[u]
                n = keys(qt)
                V.wait_ge(score_ps, at(score_ps, l, u + 1))
                if u:
                    V.wait_ge(exp_sb, at(exp_sb, l, 4 * u))
                src = ps[:, 2:4, :].rearrange("p b (s k) -> p (b s) k", k=T)[:, :, 0:n]
                if m == "c":
                    if u == 0:
                        V.wait_ge(cb_masked, at(cb_masked, l))
                    bias = cbias[:, :, P:2 * P] if qt == 0 else cbias[:]
                elif m == "b":
                    bias = mask_of(qt).unsqueeze(1).to_broadcast([P, H, n])
                else:
                    bias = score[:, qt, 0:n].unsqueeze(1).to_broadcast([P, H, n])
                scale = {"a": HD ** -0.5, "b": (HD + BR) ** -0.5, "c": HD ** -0.5}[m]
                V.scalar_tensor_tensor(logits[:, :, 0:n], src, scale, bias, ALU.mult, ALU.add).then_inc(logit_sb, 1)
                V.wait_ge(logit_sb, at(logit_sb, l, u + 1))
                V.tensor_reduce(st[:, 16:20], logits[:, :, 0:n], AX_X, ALU.max, negate=True).then_inc(nmax_sb, 1)
                V.wait_ge(exp_sb, at(exp_sb, l, 4 * u + 4))
                if u:
                    V.wait_ge(probs_sb, at(probs_sb, l, u))
                V.reciprocal(st[:, 24:28], st[:, 20:24]).then_inc(step, 1)
                V.wait_ge(step, steps(1))
                r = st[:, 24:28].unsqueeze(2).to_broadcast([P, H, n])
                V.tensor_tensor(probs[:, :, 0:n], probs[:, :, 0:n], r, ALU.mult).then_inc(probs_sb, 1)

            V.wait_ge(x_in, at(x_in, 0, 1))
            for l in range(L):
                norm(l, 0)
                copy_tokens(V, l, 1, z_dve, copy)
                V.wait_ge(z_act, at(z_act, l, 10))
                V.wait_ge(z_dve, at(z_dve, l, 10))
                rope(l, 0, heads(zaq, H), H, A_ROT, C_CA, C_SA)
                rope(l, 1, heads(zkv[:], 2)[:, :, 0:1, :], 1, A_ROT, C_CA, C_SA)
                rope(l, 2, heads(ziq, IH), IH, I_ROT, C_CI, C_SI)
                rope(l, 3, zik, 2, I_ROT, C_CI, C_SI)
                rope(l, 4, zkr, 2, BR, C_CB, C_SB)
                V.tensor_scalar(ziw, ziw, float(IH ** -0.5 * ID ** -0.5), None, ALU.mult).then_inc(step, 1)
                V.wait_ge(step, steps(1))
                squares = rope1[:, 0:BQ]
                V.wait_ge(roped, at(roped, l, 5))
                for n, (o, w) in enumerate(((0, BQ), (BQ, BKV))):
                    for tt in range(TT):
                        V.tensor_tensor_reduce([squares, rope2][tt][:, 0:w], zb[:, tt, o:o + w], zb[:, tt, o:o + w], 1.0,
                                                          0.0, ALU.mult, ALU.add, st[:, 28 + 2 * n + tt:29 + 2 * n + tt]).then_inc(step, 1)
                    V.wait_ge(step, steps(2))
                V.tensor_scalar(st[:, 4:6], st[:, 28:30], 1.0 / BQ, EPS, ALU.mult, ALU.add).then_inc(step, 1)
                V.wait_ge(step, steps(1))
                V.tensor_scalar(st[:, 6:8], st[:, 30:32], 1.0 / BKV, EPS, ALU.mult, ALU.add).then_inc(var_ready, 1)
                V.wait_ge(rstd_ready, at(rstd_ready, l, 2))
                for n, (o, w) in enumerate(((0, BQ), (BQ, BKV))):
                    for tt in range(TT):
                        V.tensor_scalar(zb[:, tt, o:o + w], zb[:, tt, o:o + w],
                                                    st[:, 12 + 2 * n + tt:13 + 2 * n + tt], None, ALU.mult).then_inc(bn_ready, 1)
                V.wait_ge(turn_ps, at(turn_ps, l, 2))
                copy(aqT[:, :, P:2 * P], ps[:, 3, :].rearrange("p (h t) -> p h t", h=4)).then_inc(turn_dve, 1)
                V.wait_ge(turn_ps, at(turn_ps, l, 4))
                copy(iqT[:, :, P:2 * P], ps[:, 5, :].rearrange("p (h t) -> p h t", h=4)).then_inc(turn_dve, 1)
                V.wait_ge(turn_ps, at(turn_ps, l, 6))
                for k in range(2):
                    copy(bcqT[:, k, :], ps[:, 7, k * T:(k + 1) * T], small[:, l, S_GQ + k:S_GQ + k + 1]).then_inc(turn_dve, 1)
                V.wait_ge(turn_ps, at(turn_ps, l, 7))
                copy(bckvT[:], ps[:, 0, 0:T], small[:, l, S_GKV:S_GKV + 1]).then_inc(turn_dve, 1)
                index_score(l, 0)
                index_score(l, 1)
                V.wait_ge(b_sb, at(b_sb, l, 1))
                rope(l, 5, heads(zqr, H), H, BR, C_CB, C_SB)
                for u in range(len(UNITS)):
                    softmax(l, u)
                    if u < TT:
                        top_keys(u)
                for n in range(12):
                    m, c = PROJ_ORDER[n // 4], 2 * (n % 4)
                    V.wait_ge(proj_ps, at(proj_ps, l, n + 1))
                    if n == 0:
                        V.wait_ge(gate_sb, at(gate_sb, l))
                        V.wait_ge(o_ps, at(o_ps, l))
                    g = gates[:, KC * "abc".index(m) + c:KC * "abc".index(m) + c + 2, :]
                    src = ps[:, n % 4, :].rearrange("p (m t) -> p m t", m=2)
                    dst = mixT[:, c:c + 2, :]
                    if n < 4:
                        V.scalar_tensor_tensor(dst, g, 1.0, src, ALU.add, ALU.mult).then_inc(proj_used, 1)
                    else:
                        V.scalar_tensor_tensor(g, g, 1.0, src, ALU.add, ALU.mult).then_inc(step, 1)
                        V.wait_ge(step, steps(1))
                        if n == 4:
                            V.wait_ge(proj_used, at(proj_used, l, 4))
                        elif n == 8:
                            V.wait_ge(proj_used, at(proj_used, l, 8))
                        V.tensor_tensor(dst, dst, g, ALU.add).then_inc(proj_used, 1)
                for n in range(4):
                    tt, half = n // 2, n % 2
                    V.wait_ge(wo_ps, at(wo_ps, l, n + 1))
                    xs = x[:, tt, half * 512:(half + 1) * 512]
                    V.scalar_tensor_tensor(xs, ps[:, 4 + n, :], 0.5, xs, ALU.mult, ALU.add).then_inc(x_added, 1)
                norm(l, 1)
                route(l)

                def hidden(g, first):
                    V.wait_ge(tanh_sb, at(tanh_sb, l, g + 1))
                    V.scalar_tensor_tensor(th, th, 1.0, ps[:, 2, 0:FE], ALU.add, ALU.mult).then_inc(silu_sb, 1)
                    if not first:
                        V.wait_ge(hidT_ps, at(hidT_ps, l, g))
                    V.wait_ge(silu_sb, at(silu_sb, l, g + 1))
                    V.tensor_tensor(hid, th, ps[:, 2, FE:2 * FE], ALU.mult).then_inc(hid_sb, 1)

                def gathered(g):
                    for q in range(2):
                        V.wait_ge(gath_ps, at(gath_ps, l, 2 * g + q + 1))
                        gain = small[:, l, S_GF + 4 * q:S_GF + 4 * q + 4].unsqueeze(2).to_broadcast([P, 4, P])
                        V.tensor_tensor(xg[:, 4 * q:4 * q + 4, :],
                                                 ps[:, q, :].rearrange("p (k s) -> p k s", k=4), gain, ALU.mult).then_inc(xg_sb, 1)

                def add_back(g, tt, bank):
                    for half in range(2):
                        V.wait_ge(comb_ps, at(comb_ps, l, 4 * g + (2 * tt + half + 1)))
                        xs = x[:, tt, half * 512:(half + 1) * 512]
                        V.wait_ge(x_added, at(x_added, l, 4 * g + (2 * tt + half + 1)))
                        V.tensor_tensor(xs, xs, ps[:, bank + half, :], ALU.add).then_inc(x_added, 1)

                gathered(0)

                def one_set(g, first, last):
                    hidden(g, first)
                    if not first:
                        add_back(g - 1, 0, 6)
                    if not last:
                        V.wait_ge(gu_ps, at(gu_ps, l, g + 1))
                        gathered(g + 1)
                    if not first:
                        add_back(g - 1, 1, 0 if last else 6)
                loop_sets(V, one_set)
                add_back(NG - 1, 0, 6)
                add_back(NG - 1, 1, 4)
                V.wait_ge(x_added, at(x_added, l))
                late_sums(l)
                V.sem_inc(late_settled, 1)

            mean_square(L, 0)
            V.wait_ge(rstd_ready, at(rstd_ready, L, 1))
            V.wait_ge(fgain_in, at(fgain_in, 0, 1))
            for tt in range(TT):
                V.scalar_tensor_tensor(xn[:, tt, :], x[:, tt, :], st[:, 8 + tt:9 + tt], fgain,
                                                    ALU.mult, ALU.mult).then_inc(out_ready, 1)


def blocks(w, k):
    return w.reshape(k, P, -1).transpose(1, 0, 2).reshape(P, -1)


def kernel(**inputs):
    import concourse.bacc as _bacc
    from concourse.bass_utils import run_bass_kernel_spmd as _run

    i = {k: np.asarray(v) for k, v in inputs.items()}
    stream = np.zeros((L * PER_LAYER, P, BLK), np.float32)
    small = np.zeros((L, P, NSMALL), np.float32)
    up = np.zeros((L, P, NUP), np.float32)
    for l in range(L):
        s = stream[l * PER_LAYER:(l + 1) * PER_LAYER]
        win = i["w_in"][l]
        for n, (lo, hi) in enumerate(TOKEN_BLOCKS + [(c, c + 512) for c in range(O_CQ, N_IN, 512)]):
            s[n, :, :KC * (hi - lo)] = blocks(win[:, lo:hi], KC)
        for n, m in enumerate(PROJ_ORDER):
            s[B_PROJ + n] = blocks(i[f"w_proj_{m}"][l], 4)
        for n in range(2):
            s[B_WO + n] = blocks(i["w_out"][l][n * 512:(n + 1) * 512], 4)
        for g in range(NG):
            for n, (kind, j) in enumerate(SET_ORDER):
                e = XG * g + j
                if kind == "gu":
                    w = blocks(np.concatenate([i["w_gate"][l, e], i["w_up"][l, e]], 1), KC)
                else:
                    w = blocks(i["w_down"][l, e:e + 2].reshape(2 * FE, D), 4)
                s[NT + PER_SET * g + n] = w
        small[l, :, S_GA:S_GA + KC] = i["attn_norm_g"][l].reshape(KC, P).T
        small[l, :, S_GF:S_GF + KC] = i["ffn_norm_g"][l].reshape(KC, P).T
        small[l, :, S_GQ:S_GQ + 2] = i["b_q_norm_g"][l].reshape(2, P).T
        small[l, :, S_GKV] = i["b_kv_norm_g"][l]
        small[l, :, S_R:] = blocks(np.concatenate([i["w_group"][l], i["w_router"][l]], 1), KC)
        up[l] = np.concatenate([blocks(i["b_w_uq"][l], 2), i["b_w_ukv"][l]], 1)
    at = np.minimum(P + np.arange(P)[:, None] - np.arange(T)[None, :], REL) + REL
    rel = i["c_rel_bias"][:, :, at].transpose(0, 2, 1, 3).reshape(L, P, H * T)
    arrays = {
        "x": i["x"], "consts": shape_constants(), "stream": stream, "small": small, "up": up,
        "rel": np.ascontiguousarray(rel), "final_gain": i["final_norm_g"],
        "rbias": np.concatenate([i["b_group"], i["b_router"]], 1),
    }
    nc = _bacc.Bacc("TRN2", target_bir_lowering=False, num_devices=1)
    a = {n: nc.dram_tensor(f"in_{n}", v.shape, mybir.dt.from_np(v.dtype), kind="ExternalInput").ap()
         for n, v in arrays.items()}
    a["out"] = nc.dram_tensor("out_dram", (1, T, D), F32, kind="ExternalOutput").ap()
    build(nc, a)
    r = _run(nc, [{f"in_{n}": v for n, v in arrays.items()}], core_ids=[0])
    return r.results[0]["out_dram"]
```

```python
from contextlib import ExitStack

import numpy as np
import concourse.bass as bass
from concourse import mybir

F32 = mybir.dt.float32
F32R = mybir.dt.float32r
U32 = mybir.dt.uint32
I32 = mybir.dt.int32
ALU = mybir.AluOpType
ACT = mybir.ActivationFunctionType
AX_X = mybir.AxisListType.X

P = 128
L = 2
D = 1024
T = 256
TT = T // P
KC = D // P
CHUNK = 64
EPS = 1e-6
H = 4
HD = 128
IH, ID = 8, 64
TOPK = 64
BQ, BKV, BR = 256, 128, 64
A_ROT, I_ROT = HD // 4, ID // 4
N_IN = 6408
REL = 128
G, EPG = 4, 8
E = G * EPG
FE = 256
SLOTS = 32
XG = P // SLOTS
NG = E // XG
LATE_FROM = SLOTS
SCORE_GATE = 9
NEG = -1.0e30
REPL = -3.0e38

O_AQ, O_KV, O_IQ, O_IK, O_IW = 0, 512, 768, 1280, 1344
O_BQ, O_BKV, O_BKR = 1352, 1608, 1736
O_CQ, O_CK, O_CV, O_GL = 1800, 2312, 2824, 3336

RING = 6
BLK = 4096
NT = 18
PER_SET = 6
PER_LAYER = NT + PER_SET * NG
TOKEN_BLOCKS = [(0, 512), (512, 1024), (1024, 1412), (1412, 1800)]
B_CQ, B_CK, B_CV, B_GL, B_PROJ, B_WO = 4, 5, 6, 7, 13, 16
PROJ_ORDER = "cba"
HALVES = 2 * NT
WAYS = 4
SET_ORDER = [("gu", 0), ("gu", 1), ("gu", 2), ("gu", 3), ("d", 0), ("d", 2)]
EXTRA = 3
FIRST_SET = ["extra0", 2, 3, "extra1", 0, 1, 4, 5, "extra2"]
GU_SLOT = [0, 1, 2, 3]
D_SLOT = [4, 4, 5, 5]
LAST_D_SLOT = [1, 1, 2, 2]
TRUNK_IN_SLOT = [(NT + WAYS - 1 - s) // WAYS if s < WAYS else 0 for s in range(RING)]

C_ID, C_U, C_ONE, C_M = 0, 128, 256, 384
C_CA, C_SA = 640, 640 + 2 * A_ROT
C_CI, C_SI = C_SA + 2 * A_ROT, C_SA + 2 * A_ROT + 2 * I_ROT
C_CB, C_SB = C_SI + 2 * I_ROT, C_SI + 2 * I_ROT + 2 * BR
C_IOTA = C_SB + 2 * BR
NCONST = C_IOTA + SLOTS
S_GA, S_GF, S_GQ, S_GKV, S_R = 0, KC, 2 * KC, 2 * KC + 2, 2 * KC + 3
NSMALL = S_R + KC * (G + E)
NUP = 2 * H * (HD + BR) + H * 2 * HD


def shape_constants():
    c = np.zeros((P, NCONST), np.float32)
    c[:, C_ID:C_ID + P] = np.eye(P)
    c[:, C_U:C_U + P] = np.triu(np.ones((P, P)), 1)
    c[:, C_ONE:C_ONE + P] = 1.0
    c[:CHUNK, C_M + 3 * CHUNK:C_M + 4 * CHUNK] = NEG
    for rot, oc, os in ((A_ROT, C_CA, C_SA), (I_ROT, C_CI, C_SI), (BR, C_CB, C_SB)):
        pos = np.arange(T, dtype=np.float32)
        inv = np.float32(500000.0) ** (-np.arange(0, rot, 2, dtype=np.float32) / np.float32(rot))
        ang = pos[:, None] * inv[None, :].astype(np.float32)
        cos, sin = np.cos(ang), np.sin(ang)
        for tt in range(TT):
            r = slice(tt * P, tt * P + P)
            c[:, oc + tt * rot:oc + (tt + 1) * rot] = np.concatenate([cos[r], cos[r]], 1)
            c[:, os + tt * rot:os + (tt + 1) * rot] = np.concatenate([-sin[r], sin[r]], 1)
    c[:, C_IOTA:C_IOTA + SLOTS] = np.arange(SLOTS)
    c[:, C_IOTA + LATE_FROM:C_IOTA + SLOTS] = -5.0
    return c


def build(nc, a):
    ctx = ExitStack()
    with ctx:
        def sb(name, shape, dt=F32):
            return ctx.enter_context(nc.sbuf_tensor(name, shape, dt))

        counts = {}

        def sig(name, per, unit=1):
            handle = ctx.enter_context(nc.semaphore(name))
            counts[handle.name] = per, unit
            return handle

        def at(signal, l, n=None):
            per, unit = counts[signal.name]
            return (l * per + (per if n is None else n)) * unit

        ps = ctx.enter_context(nc.psum_tensor("ps", [P, 8, 512], F32))

        ring = sb("ring", [P, RING, BLK])
        ring_at = nc.lookup_mloc(ring).addr
        w_hi = nc.alloc_sbuf_tensor_at("w_hi", [P, 2, BLK // 2], F32R, offset=ring_at + 4 * WAYS * BLK)
        w_lo = nc.alloc_sbuf_tensor_at("w_lo", [P, 2, BLK // 2], F32R, offset=ring_at + 4 * (WAYS + 1) * BLK)
        x = sb("x", [P, TT, D])
        xn = sb("xn", [P, TT, D])
        hT = sb("hT", [P, KC, T])
        hT_hi = nc.alloc_sbuf_tensor_at("hT_hi", [P, KC, T], F32R, offset=nc.lookup_mloc(hT).addr)
        ckT = sb("ckT", [P, H, T])
        iqT = sb("iqT", [P, IH // 2, T])
        hT_lo = sb("hT_lo", [P, KC, T], F32R)
        wup = sb("wup", [P, NUP])
        cst = sb("cst", [P, NCONST])
        small = sb("small", [P, L, NSMALL])
        rbias = sb("rbias", [P, L, G + E])
        knT = wup[:, 0:H * T].rearrange("p (h t) -> p h t", h=H)
        qrT = wup[:, H * T:(H + 2) * T].rearrange("p (m t) -> p m t", m=2)
        krT = wup[:, (H + 2) * T:(H + 3) * T]
        cbias = sb("cbias", [P, H, T])
        aqT = sb("aqT", [P, H, T])
        cqT = sb("cqT", [P, H, T])
        qnT = sb("qnT", [P, H, T])
        extra = [nc.alloc_sbuf_tensor_at(f"extra{n}", [P, BLK], F32, offset=nc.lookup_mloc(t).addr)
                 for n, t in enumerate((hT_lo, cbias, hT))]
        gates = sb("gates", [P, 3 * KC, T])
        keysT = sb("keysT", [P, 2, T])
        bckvT = sb("bckvT", [P, T])
        vB = sb("vB", [P, TT, H * HD])
        cv = sb("cv", [P, TT, H * HD])
        zkv = sb("zkv", [P, TT, 2 * HD])
        st = sb("st", [P, 64])
        st8 = sb("st8", [P, 8])
        flag = sb("flag", [P, 1], I32)

        o_parts = {}
        for m, places in (("c", (cv, ckT)), ("b", (vB, iqT)), ("a", (cv, ckT))):
            o_parts[m] = [nc.alloc_sbuf_tensor_at(f"o_{m}_{part}", [P, H, T], F32R, offset=nc.lookup_mloc(t).addr)
                          for part, t in zip(("hi", "lo"), places)]
        mix_hi = nc.alloc_sbuf_tensor_at("mix_hi", [P, KC, T], F32R, offset=nc.lookup_mloc(hT).addr)
        mix_lo = nc.alloc_sbuf_tensor_at("mix_lo", [P, KC, T], F32R, offset=nc.lookup_mloc(xn).addr)

        gf = gates[:].rearrange("p c t -> p (c t)")
        zaq = gf[:, 0:1024].rearrange("p (a n) -> p a n", a=TT)
        ziq = gf[:, 1024:2048].rearrange("p (a n) -> p a n", a=TT)
        zb = gf[:, 2048:2816].rearrange("p (a n) -> p a n", a=TT)
        zik = gf[:, 2816:3072].rearrange("p (a s n) -> p a s n", a=TT, s=2)
        zkr = gf[:, 3072:3328].rearrange("p (a s n) -> p a s n", a=TT, s=2)
        ziw = gf[:, 3328:3344].rearrange("p (a n) -> p a n", a=TT)
        score = gf[:, SCORE_GATE * 512:SCORE_GATE * 512 + 512].rearrange("p (a n) -> p a n", a=TT)
        logits = iqT[:].rearrange("p s t -> p s t")
        xnf = xn[:].rearrange("p a d -> p (a d)")
        probsT = xnf[:, 0:1024].rearrange("p (k h q) -> p k h q", k=2, h=H)
        rope1 = xnf[:, 1024:1536]
        rope2 = xnf[:, 1536:2048]
        probs = xnf[:, 1024:2048].rearrange("p (h k) -> p h k", h=H)
        relu = xnf[:, 1024:2048].rearrange("p (b n) -> p b n", b=2)
        bcqT = xnf[:, 512:1024].rearrange("p (k t) -> p k t", k=2)
        zqr = xnf[:, 0:512].rearrange("p (a n) -> p a n", a=TT)
        mixT = xnf.rearrange("p (c t) -> p c t", c=KC)
        junk = gf[:, 0:2048].rearrange("p (n c) -> p n c", n=4)
        routerT = bckvT[0:G + E, :]
        sel = gf[:, 0:2048].rearrange("p (a n) -> p a n", a=TT)
        selwT = gf[:, 2048:4096].rearrange("p (g t) -> p g t", g=NG)
        xg = gf[:, 4096:5120].rearrange("p (k s) -> p k s", k=KC)
        yg = gf[:, 5120:6144]
        kf = keysT[:].rearrange("p s t -> p (s t)")
        zf = zkv[:].rearrange("p a n -> p (a n)")
        selws = [yg, xn[:, 0, :]]
        xe = [vB[:].rearrange("p a n -> p (a n)"), xn[:, 1, :]]
        sw = kf[:, 0:256]
        hid = zf[:, 0:256]
        th = kf[:, 256:512]
        hidT = zf[:, 256:512].rearrange("p (f s) -> p f s", f=2)
        cvf = cv[:].rearrange("p a n -> p (a n)")
        lg = cvf[:, 0:72].rearrange("p (a n) -> p a n", a=TT)
        g8 = cvf[:, 72:88].rearrange("p (a n) -> p a n", a=TT)
        m8 = cvf[:, 88:104].rearrange("p (a n) -> p a n", a=TT)
        i8 = cvf[:, 104:120].rearrange("p (a n) -> p a n", a=TT).bitcast(U32)
        prod = cvf[:, 120:184].rearrange("p (a n) -> p a n", a=TT)
        ein = cvf[:, 184:200].rearrange("p (a n) -> p a n", a=TT)
        e8 = cvf[:, 200:216].rearrange("p (a n) -> p a n", a=TT)
        j8 = cvf[:, 216:232].rearrange("p (a n) -> p a n", a=TT).bitcast(U32)
        fi = cvf[:, 232:240].rearrange("p (a n) -> p a n", a=TT)
        ohg = cvf[:, 240:248].rearrange("p (a n) -> p a n", a=TT)
        eg = cvf[:, 248:256].rearrange("p (a n) -> p a n", a=TT)
        rw = cvf[:, 256:272].rearrange("p (n a) -> p n a", a=TT)
        oh1 = cvf[:, 272:288].rearrange("p (a n) -> p a n", a=TT)
        oh2 = cvf[:, 288:304].rearrange("p (a n) -> p a n", a=TT)
        ce = cvf[:, 304:320].rearrange("p (a n) -> p a n", a=TT)
        comb = cvf[:, 320:384].rearrange("p (a n) -> p a n", a=TT)
        asg = cvf[:, 384:448].rearrange("p (a n) -> p a n", a=TT)
        rk = cvf[:, 448:512].rearrange("p (a n) -> p a n", a=TT)
        late = cvf[:, 512:576].rearrange("p (a n) -> p a n", a=TT)
        cnt = cvf[:, 576:577]
        thl = aqT[:].rearrange("p h t -> p (h t)")[:, 0:512].rearrange("p (a n) -> p a n", a=TT)
        hidl = cqT[:].rearrange("p h t -> p (h t)")[:, 0:512].rearrange("p (a n) -> p a n", a=TT)
        hidTl = cqT[:].rearrange("p h t -> p (h t)")[:, 512:1024].rearrange("p (f t) -> p f t", f=2)

        ident = cst[:, C_ID:C_ID + P]
        tri = cst[:, C_U:C_U + P]
        ones = cst[:, C_ONE:C_ONE + P]
        iota = cst[:, C_IOTA:C_IOTA + SLOTS]

        def mask_of(qt):
            return cst[:, C_M + P:C_M + 2 * P] if qt == 0 else cst[:, C_M:C_M + T]

        def keys(qt):
            return (qt + 1) * P

        x_in = sig("x_in", 0, 16)
        consts_in = sig("consts_in", 0, 16)
        sums_act = sig("sums_act", 6)
        xn_act = sig("xn_act", 1)
        rbias_in = sig("rbias_in", 0, 16)
        fgain_in = sig("fgain_in", 0, 16)
        up_in = sig("up_in", 1, 16)
        cb_in = sig("cb_in", 1, 16)
        slot_in = [sig(f"slot_in{s}", TRUNK_IN_SLOT[s] + NG - (s not in LAST_D_SLOT and s != EXTRA), 16) for s in range(RING)]
        extra_in = [sig(f"extra_in{n}", 1, 16) for n in range(EXTRA)]
        xn_dve = sig("xn_dve", 4)
        xnT_ps = sig("xnT_ps", 8)
        hT_dve = sig("hT_dve", 12)
        hT_act = sig("hT_act", 12)
        var_ready = sig("var_ready", 4)
        rstd_ready = sig("rstd_ready", 4)
        hi_made = sig("hi_made", HALVES)
        lo_made = sig("lo_made", HALVES)
        half_ps = sig("half_ps", HALVES)
        z_act = sig("z_act", 11)
        z_dve = sig("z_dve", 11)
        c_sb = sig("c_sb", 6)
        roped = sig("roped", 6)
        bn_ready = sig("bn_ready", 4)
        turn_ps = sig("turn_ps", 9)
        turn_act = sig("turn_act", 5)
        turn_dve = sig("turn_dve", 5)
        idx_ps = sig("idx_ps", 6)
        relu_sb = sig("relu_sb", 6)
        idx_used = sig("idx_used", 6)
        b_ps = sig("b_ps", 7)
        b_sb = sig("b_sb", 7)
        score_ps = sig("score_ps", 6)
        logit_sb = sig("logit_sb", 6)
        nmax_sb = sig("nmax_sb", 6)
        exp_sb = sig("exp_sb", 24)
        probs_sb = sig("probs_sb", 6)
        probsT_ps = sig("probsT_ps", 9)
        probsT_sb = sig("probsT_sb", 9)
        o_ps = sig("o_ps", 6)
        o_sb = sig("o_sb", 6)
        gate_sb = sig("gate_sb", 12)
        o_hi_made = sig("o_hi_made", 3)
        o_lo_made = sig("o_lo_made", 3)
        proj_ps = sig("proj_ps", 6)
        proj_used = sig("proj_used", 12)
        mix_hi_made = sig("mix_hi_made", 4)
        mix_lo_made = sig("mix_lo_made", 4)
        wo_ps = sig("wo_ps", 2)
        cb_masked = sig("cb_masked", H)
        routerT_ps = sig("routerT_ps", 1)
        routerT_sb = sig("routerT_sb", 1)
        route_ps = sig("route_ps", 1)
        gdiff_sb = sig("gdiff_sb", 2)
        gexp_sb = sig("gexp_sb", 2)
        asg_sb = sig("asg_sb", 1)
        rank_ps = sig("rank_ps", 1)
        count_ps = sig("count_ps", 1)
        flag_sb = sig("flag_sb", 1)
        sel_sb = sig("sel_sb", 4)
        selw_sb = sig("selw_sb", 2)
        selwT_ps = sig("selwT_ps", 4)
        selwT_sb = sig("selwT_sb", 4)
        gath_ps = sig("gath_ps", 2 * NG)
        xg_sb = sig("xg_sb", 2 * NG)
        gu_ps = sig("gu_ps", NG)
        tanh_sb = sig("tanh_sb", NG)
        silu_sb = sig("silu_sb", NG)
        hid_sb = sig("hid_sb", NG)
        hidT_ps = sig("hidT_ps", NG)
        hidT_sb = sig("hidT_sb", NG)
        down_half = sig("down_half", NG)
        down_ps = sig("down_ps", NG)
        yg_sb = sig("yg_sb", 2 * NG)
        sw_sb = sig("sw_sb", NG)
        comb_ps = sig("comb_ps", 4 * NG)
        x_added = sig("x_added", 4 + 4 * NG)
        late_gu_in = [sig(f"late_gu_in{l}", 0, 16) for l in range(L)]
        late_d_in = [sig(f"late_d_in{l}", 0, 16) for l in range(L)]
        late_gu_ps = [sig(f"late_gu_ps{l}", 0) for l in range(L)]
        late_tanh = [sig(f"late_tanh{l}", 0) for l in range(L)]
        late_silu = [sig(f"late_silu{l}", 0) for l in range(L)]
        late_hid = [sig(f"late_hid{l}", 0) for l in range(L)]
        late_hidT_ps = [sig(f"late_hidT_ps{l}", 0) for l in range(L)]
        late_hidT_sb = [sig(f"late_hidT_sb{l}", 0) for l in range(L)]
        late_added = [sig(f"late_added{l}", 0) for l in range(L)]
        late_xnT_ps = [sig(f"late_xnT_ps{l}", 0) for l in range(L)]
        late_hT = [sig(f"late_hT{l}", 0) for l in range(L)]
        late_done = [sig(f"late_done{l}", 0) for l in range(L)]
        late_settled = sig("late_settled", 1)
        out_ready = sig("out_ready", 0)
        out_done = sig("out_done", 0, 16)

        def slot(s):
            return ring[:, s, :]

        def slot_k(s, n, k=KC):
            return ring[:, s, 0:k * n].rearrange("p (k n) -> p k n", k=k)

        def width(i):
            return TOKEN_BLOCKS[i][1] - TOKEN_BLOCKS[i][0] if i < len(TOKEN_BLOCKS) else 512

        def raw_half(n):
            i, h = n // 2, n % 2
            if i >= B_PROJ:
                return slot_k(i % WAYS, D, 4)[:, :, 512 * h:512 * h + 512]
            m = width(i) // 2
            return slot_k(i % WAYS, width(i))[:, :, m * h:m * h + m]

        def part_of(parts, n):
            if n >= 2 * B_PROJ:
                return parts[:, n % 2, :].rearrange("p (k n) -> p k n", k=4)
            m = width(n // 2) // 2
            return parts[:, n % 2, 0:KC * m].rearrange("p (k n) -> p k n", k=KC)

        def loop_sets(eng, body):
            body(0, True, False)
            with eng.Fori(1, NG - 1) as g:
                body(g, False, False)
            body(NG - 1, False, True)

        pool_const = sig("pool_const", 0)
        step = ctx.enter_context(nc.semaphore("step"))
        taken = [0]

        def steps(n):
            taken[0] += n
            return taken[0]

        fgain = xn[:, 0, :]
        outs = [gf[:, 2048:3072], gf[:, 3072:4096]]
        UNITS = [("c", 0), ("c", 1), ("b", 0), ("b", 1), ("a", 0), ("a", 1)]
        HEAD_AT = {"a": [0, 1, 2, 3], "b": [0, 2, 1, 3], "c": [0, 1, 2, 3]}
        PT_COUNT = [1, 3, 4, 6, 7, 9]
        ADDED = [0, 2, 1, 3]
        SELW_BANKS = [3, 6, 7, 5]

        def copy_tokens(eng, l, tt, signal, copy, between=None):
            cut = TOKEN_BLOCKS[2][1] - O_BQ
            for i in range(4):
                if between:
                    between(2 * i + 2)
                eng.wait_ge(half_ps, at(half_ps, l, 2 * i + 2))
                b = ps[:, (4 + 2 * i + tt) % 8, :]
                if i == 0:
                    moves = [(zaq[:, tt, :], b)]
                elif i == 1:
                    moves = [(zkv[:, tt, :], b[:, 0:256]), (ziq[:, tt, 0:256], b[:, 256:512])]
                elif i == 2:
                    moves = [(ziq[:, tt, 256:512], b[:, 0:256]), (zik[:, tt, 0, :], b[:, 256:320]),
                             (zik[:, tt, 1, :], b[:, 256:320]), (ziw[:, tt, :], b[:, 320:328]),
                             (zb[:, tt, 0:cut], b[:, 328:328 + cut])]
                else:
                    o = BQ + BKV - cut
                    moves = [(zb[:, tt, cut:], b[:, 0:o]), (zkr[:, tt, 0, :], b[:, o:o + BR]),
                             (zkr[:, tt, 1, :], b[:, o:o + BR])]
                for dst, src in moves:
                    copy(dst, src).then_inc(signal, 1)
                if between:
                    between(2 * i + 3)

        def any_late(eng, l):
            eng.wait_ge(flag_sb, at(flag_sb, l))
            return eng.value_load(flag[0:1, 0:1], min_val=0, max_val=1) > 0

        block = ctx.enter_context(nc.Block())

        @block.sync
        def _(sp):
            sp.dma_start(x[:], a["x"].rearrange("b (t p) d -> p (b t) d", p=P)).then_inc(x_in, 16)
            sp.dma_start(cst[:], a["consts"]).then_inc(consts_in, 16)
            sp.dma_start(small[:], a["small"].rearrange("l p n -> p l n")).then_inc(consts_in, 16)
            stream = a["stream"]

            def late_stream(l):
                with sp.If(any_late(sp, l)):
                    sp.wait_ge(gu_ps, at(gu_ps, l))
                    sp.wait_ge(down_ps, at(down_ps, l))

                    with sp.Fori(0, NG) as g:
                        for j in range(XG):
                            sp.wait_ge(late_done[l], at(late_done[l], 0, XG * g + (j + 1)))
                            i = g * PER_SET + (l * PER_LAYER + NT)
                            src = a["stream"][bass.ds(i + GU_SLOT[j], 1)].rearrange("b p n -> p (b n)")
                            sp.dma_start(ring[:, 0, :], src).then_inc(late_gu_in[l], 16)
                            src = a["stream"][bass.ds(i + D_SLOT[j], 1)].rearrange("b p n -> p (b n)")
                            h = (j % 2) * BLK // 2
                            sp.dma_start(ring[:, 1, 0:BLK // 2], src[:, h:h + BLK // 2]).then_inc(late_d_in[l], 16)
                    sp.wait_ge(late_done[l], at(late_done[l], 0, E + 1))

            for l in range(L):
                for i in range(NT):
                    s = i % WAYS
                    if i >= WAYS:
                        sp.wait_ge(lo_made, at(lo_made, l, 2 * (i - WAYS) + 2))
                    elif l:
                        if s in LAST_D_SLOT:
                            sp.wait_ge(down_ps, at(down_ps, l - 1))
                        else:
                            sp.wait_ge(gu_ps, at(gu_ps, l - 1, NG - 1 if s < EXTRA else NG))
                    n = KC * width(i) if i < B_PROJ else BLK
                    sp.dma_start(ring[:, s, 0:n], stream[l * PER_LAYER + i, :, 0:n]).then_inc(slot_in[s], 16)

                def one_set(g, first, last):
                    for s in FIRST_SET if first else range(EXTRA if last else 0, PER_SET):
                        if s == "extra0" or s == "extra1" or s == "extra2":
                            n = int(s[-1])
                            if n == 2:
                                sp.wait_ge(routerT_ps, at(routerT_ps, l))
                            elif n == 1:
                                sp.wait_ge(half_ps, at(half_ps, l, 2 * B_WO))
                            else:
                                sp.wait_ge(half_ps, at(half_ps, l, 2 * B_PROJ))
                                sp.wait_ge(score_ps, at(score_ps, l))
                            sp.dma_start(extra[n][:], stream[(l + 1) * PER_LAYER - PER_SET + n]).then_inc(extra_in[n], 16)
                            continue
                        kind, j = SET_ORDER[s]
                        if first and s >= WAYS:
                            sp.wait_ge(half_ps, at(half_ps, l))
                        elif first:
                            i = NT - 1 - (NT - 1 - s) % WAYS
                            sp.wait_ge(lo_made, at(lo_made, l, 2 * i + 2))
                        elif last:
                            sp.wait_ge(gu_ps, at(gu_ps, l, g))
                        else:
                            used = gu_ps if kind == "gu" else down_ps
                            sp.wait_ge(used, at(used, l, g))
                        i = g * PER_SET + (l * PER_LAYER + NT + s)
                        src = stream[bass.ds(i, 1)].rearrange("b p n -> p (b n)")
                        if last and kind == "d":
                            s = LAST_D_SLOT[j]
                        sp.dma_start(ring[:, s, :], src).then_inc(slot_in[s], 16)
                loop_sets(sp, one_set)
                late_stream(l)

            for tt in range(TT):
                sp.wait_ge(out_ready, at(out_ready, 0, tt + 1))
                sp.dma_start(a["out"][0, tt * P:(tt + 1) * P, :], outs[tt]).then_inc(out_done, 16)
            sp.wait_ge(out_done, at(out_done, 0, TT))

        @block.gpsimd
        def _(pool):
            pool.memset(st[:, 40:44], -0.5).then_inc(pool_const, 1)
            pool.wait_ge(pool_const, at(pool_const, 0, 1))
            pool.dma_start(rbias[:], a["rbias"].rearrange("l n -> (l n)").partition_broadcast(P)
                           .rearrange("p (l n) -> p l n", l=L)).then_inc(rbias_in, 16)
            def low_part(l, n):
                pool.wait_ge(hi_made, at(hi_made, l, n + 1))
                pool.tensor_tensor(part_of(w_lo, n), raw_half(n), part_of(w_hi, n).bitcast(F32),
                                   ALU.subtract).then_inc(lo_made, 1)

            def rstd(l, n):
                lo, hi = ((0, 2), (4, 8), (0, 1), (1, 2))[n]
                pool.wait_ge(var_ready, at(var_ready, l, n + 1))
                pool.tensor_tensor(st[:, lo + 8:hi + 8], st[:, lo:hi],
                                   st[:, 40:40 + hi - lo], ALU.pow).then_inc(rstd_ready, 1)

            for l in range(L):
                if l:
                    pool.wait_ge(gu_ps, at(gu_ps, l - 1))
                pool.dma_start(wup[:], a["up"][l]).then_inc(up_in, 16)
                pool.dma_start(cbias[:].rearrange("p h t -> p (h t)"), a["rel"][l]).then_inc(cb_in, 16)
                if l:
                    low_part(l, 0)
                rstd(l, 0)
                if not l:
                    pool.wait_ge(lo_made, at(lo_made, 0, 1))
                for n in range(1, 2 * B_GL):
                    low_part(l, n)
                rstd(l, 1)
                pool.wait_ge(cb_in, at(cb_in, l))
                for h in range(H):
                    pool.tensor_tensor(cbias[:, h, :], cbias[:, h, :], mask_of(1), ALU.add).then_inc(cb_masked, 1)
                for n in range(2 * B_GL, HALVES):
                    low_part(l, n)
                rstd(l, 2)
                rstd(l, 3)
            pool.wait_ge(selwT_ps, at(selwT_ps, L - 1))
            pool.dma_start(fgain, a["final_gain"].partition_broadcast(P)).then_inc(fgain_in, 16)
            pool.wait_ge(var_ready, at(var_ready, L, 1))
            pool.tensor_tensor(st[:, 8:10], st[:, 0:2], st[:, 40:42], ALU.pow).then_inc(rstd_ready, 1)

        @block.tensor
        def _(pe):
            def mm(out, lhsT, rhs, start=True, stop=True):
                return pe.matmul(out, lhsT, rhs, start=start, stop=stop)

            def late_products(l):
                with pe.If(any_late(pe, l)):
                    pe.wait_ge(down_ps, at(down_ps, l))
                    pe.wait_ge(x_added, at(x_added, l))
                    for k in range(KC):
                        for tt in range(TT):
                            ins = turn_chunk(k, tt)
                    ins.then_inc(late_xnT_ps[l], 1)
                    pe.wait_ge(late_hT[l], at(late_hT[l], 0, KC))
                    pe.sem_inc(late_done[l], 1)

                    with pe.Fori(0, NG) as g:
                        for j in range(XG):
                            e1 = XG * g + (j + 1)
                            pe.wait_ge(late_gu_in[l], at(late_gu_in[l], 0, e1))
                            w = ring[:, 0, :].rearrange("p (k n) -> p k n", k=KC)
                            for tt in range(TT):
                                for k in range(KC):
                                    ins = pe.matmul(ps[:, tt, :], hT[:, k, tt * P:(tt + 1) * P], w[:, k, :],
                                                    start=k == 0, stop=k == KC - 1)
                            ins.then_inc(late_gu_ps[l], 1)
                            pe.wait_ge(late_hid[l], at(late_hid[l], 0, TT * XG * g + TT * (j + 1)))
                            for f in range(2):
                                for tt in range(TT):
                                    ins = pe.transpose(ps[:, 2, f * T + tt * P:f * T + (tt + 1) * P],
                                                       hidl[:, tt, f * P:(f + 1) * P], ident)
                            ins.then_inc(late_hidT_ps[l], 1)
                            pe.wait_ge(late_hidT_sb[l], at(late_hidT_sb[l], 0, e1))
                            pe.wait_ge(late_d_in[l], at(late_d_in[l], 0, e1))
                            w = ring[:, 1, 0:BLK // 2].rearrange("p (f n) -> p f n", f=2)
                            for tt in range(TT):
                                for half in range(2):
                                    for f in range(2):
                                        ins = pe.matmul(ps[:, 4 + 2 * tt + half, :], hidTl[:, f, tt * P:(tt + 1) * P],
                                                        w[:, f, half * 512:(half + 1) * 512], start=f == 0, stop=f == 1)
                            ins.then_inc(late_done[l], 1)

            def turn_norm(l):
                for tt in range(TT):
                    pe.wait_ge(xn_dve, at(xn_dve, l, tt + 1))
                    for k in range(KC):
                        o = (k % 2) * T + tt * P
                        ins = pe.transpose(ps[:, k // 2, o:o + P], xn[:, tt, k * P:(k + 1) * P], ident)
                        if tt and k % 2:
                            ins.then_inc(xnT_ps, 1)

            def turn_chunk(k, tt):
                o = (k % 2) * T + tt * P
                return pe.transpose(ps[:, k // 2, o:o + P], xe[tt][:, k * P:(k + 1) * P], ident)

            def router_logits(l, k):
                turned(l, k)
                return mm(ps[0:G + E, 4, 0:T], small[:, l, S_R + k * (G + E):S_R + (k + 1) * (G + E)],
                          hT[:, k, :], k == 0, k == KC - 1)

            def turned(l, k):
                if k % 4 == 0:
                    pe.wait_ge(hT_dve, at(hT_dve, l, 8 + k // 2 + 2))
                elif k % 4 == 2:
                    pe.wait_ge(hT_act, at(hT_act, l, 8 + k // 2 + 1))

            def tokens_by(l, bank, n):
                hi, lo = part_of(w_hi, n), part_of(w_lo, n)
                m = width(n // 2) // 2
                passes = [(hT_hi, hi), (hT_lo, hi), (hT_hi, lo)]
                if n == 0 and l:
                    passes = [(hT_hi, hi), (hT_hi, lo), (hT_lo, hi)]
                pe.wait_ge(hi_made, at(hi_made, l, n + 1))
                for i, (h, w) in enumerate(passes):
                    if w is lo:
                        pe.wait_ge(lo_made, at(lo_made, l, n + 1))
                    for tt in range(TT):
                        for k in range(KC):
                            if n == 0 and tt == 0 and i == 0:
                                pe.wait_ge(hT_act, at(hT_act, l, k + 1))
                            if n == 0 and tt == 0 and h is hT_lo:
                                pe.wait_ge(hT_dve, at(hT_dve, l, k + 1))
                            ins = mm(ps[:, bank + tt, m * (n % 2):m * (n % 2) + m],
                                     h[:, k, tt * P:(tt + 1) * P], w[:, k, :], i == 0 and k == 0, i == 2 and k == KC - 1)
                return ins

            def features_by(l, bank, n):
                hi, lo = part_of(w_hi, n), part_of(w_lo, n)
                pe.wait_ge(hi_made, at(hi_made, l, n + 1))
                for m in range(2):
                    out = ps[:, bank, m * T:(m + 1) * T]
                    c = slice(m * P, (m + 1) * P)
                    for k in range(KC):
                        mm(out, hi[:, k, c], hT_hi[:, k, :], k == 0, False)
                        mm(out, hi[:, k, c], hT_lo[:, k, :], False, False)
                    if m == 0:
                        pe.wait_ge(lo_made, at(lo_made, l, n + 1))
                    for k in range(KC):
                        ins = mm(out, lo[:, k, c], hT_hi[:, k, :], False, k == KC - 1)
                return ins

            def gather(l, g):
                for q in range(2):
                    n = 2 * g + q
                    if not (isinstance(g, int) and g == 0):
                        pe.wait_ge(xg_sb, at(xg_sb, l, n - 1))
                    for k in range(4 * q, 4 * q + 4):
                        for tt in range(TT):
                            ins = mm(ps[:, q, (k % 4) * P:(k % 4 + 1) * P], xe[tt][:, k * P:(k + 1) * P],
                                     sel[:, tt, bass.ds(g * P, P)], tt == 0, tt == TT - 1)
                    ins.then_inc(gath_ps, 1)

            def gate_up(l, g, first, last):
                for j in range(XG):
                    if last and j < EXTRA:
                        pe.wait_ge(extra_in[j], at(extra_in[j], l))
                        continue
                    pe.wait_ge(slot_in[GU_SLOT[j]], at(slot_in[GU_SLOT[j]], l, TRUNK_IN_SLOT[GU_SLOT[j]] + 1 + g))
                pe.wait_ge(xg_sb, at(xg_sb, l, 2 * g + 2))
                if not first:
                    pe.wait_ge(hid_sb, at(hid_sb, l, g))
                for k in range(KC):
                    for j in range(XG):
                        w = extra[j][:] if last and j < EXTRA else ring[:, GU_SLOT[j], :]
                        w = w.rearrange("p (k n) -> p k n", k=KC)
                        ins = mm(ps[j * SLOTS:(j + 1) * SLOTS, 2, :], xg[:, k, j * SLOTS:(j + 1) * SLOTS],
                                 w[:, k, :], k == 0, k == KC - 1)
                ins.then_inc(gu_ps, 1)

            def turn_hidden(l, g):
                pe.wait_ge(hid_sb, at(hid_sb, l, g + 1))
                for f in range(2):
                    ins = pe.transpose(ps[:, 3, f * P:(f + 1) * P], hid[:, f * P:(f + 1) * P], ident)
                ins.then_inc(hidT_ps, 1)

            def down(l, g, first, last):
                pe.wait_ge(hidT_sb, at(hidT_sb, l, g + 1))
                d_slot = LAST_D_SLOT if last else D_SLOT
                for s in sorted(set(d_slot)):
                    pe.wait_ge(slot_in[s], at(slot_in[s], l, TRUNK_IN_SLOT[s] + 1 + g))
                if not first:
                    pe.wait_ge(yg_sb, at(yg_sb, l, 2 * g))
                for half in range(2):
                    for f in range(2):
                        for j in range(XG):
                            w = ring[:, d_slot[j], :].rearrange("p (e f n) -> p e f n", e=2, f=2)
                            ins = mm(ps[j * SLOTS:(j + 1) * SLOTS, 4 + half, :],
                                     hidT[:, f, j * SLOTS:(j + 1) * SLOTS],
                                     w[:, j % 2, f, half * 512:(half + 1) * 512], f == 0, f == 1)
                    if half:
                        ins.then_inc(down_ps, 1)
                    else:
                        ins.then_inc(down_half, 1)

            def combine(l, g, tt, bank):
                if tt == 0:
                    pe.wait_ge(yg_sb, at(yg_sb, l, 2 * g + 2))
                    pe.wait_ge(sw_sb, at(sw_sb, l, g + 1))
                if bank == 6:
                    pe.wait_ge(x_added, at(x_added, l, 4 * g + (4 + 2 * tt)))
                for half in range(2):
                    mm(ps[:, bank + half, :], sw[:, tt * P:(tt + 1) * P],
                       yg[:, half * 512:(half + 1) * 512]).then_inc(comb_ps, 1)

            pe.wait_ge(consts_in, at(consts_in, 0, 2))
            for l in range(L):
                turn_norm(l)
                for n in range(2 * len(TOKEN_BLOCKS)):
                    tokens_by(l, (4 + 2 * (n // 2)) % 8, n).then_inc(half_ps, 1)
                zdone = [1, 3, 8, 11]
                for n in range(4):
                    z_copied = z_dve if n % 2 else z_act
                    pe.wait_ge(z_copied, at(z_copied, l, zdone[n // 2]))
                    features_by(l, 4 + n, 2 * B_CQ + n).then_inc(half_ps, 1)
                pe.wait_ge(z_act, at(z_act, l, zdone[2]))
                pe.wait_ge(z_dve, at(z_dve, l, zdone[2]))
                for n in range(2 * B_CV, 2 * B_CV + 2):
                    tokens_by(l, 0, n).then_inc(half_ps, 1)
                pe.wait_ge(z_act, at(z_act, l))
                pe.wait_ge(z_dve, at(z_dve, l))
                for n in range(4):
                    src = zaq if n < 2 else ziq
                    pe.wait_ge(roped, at(roped, l, 1 if n < 2 else 3))
                    if n >= 2:
                        pe.wait_ge(c_sb, at(c_sb, l, n - 1))
                    for h in range(4):
                        ins = pe.transpose(ps[:, 2 + n, h * P:(h + 1) * P], src[:, n % 2, h * P:(h + 1) * P], ident)
                    ins.then_inc(turn_ps, 1)
                pe.wait_ge(roped, at(roped, l, 4))
                pe.wait_ge(c_sb, at(c_sb, l, 3))
                for tt in range(TT):
                    pe.transpose(ps[:, 6, tt * T:tt * T + P], zkv[:, tt, 0:HD], ident)
                    ins = pe.transpose(ps[:, 6, tt * T + P:tt * T + 2 * P],
                                       zik[:, tt].rearrange("p a n -> p (a n)"), ident)
                ins.then_inc(turn_ps, 1)
                pe.wait_ge(bn_ready, at(bn_ready, l, 4))
                pe.wait_ge(c_sb, at(c_sb, l, 4))
                for k in range(2):
                    for tt in range(TT):
                        ins = pe.transpose(ps[:, 7, k * T + tt * P:k * T + (tt + 1) * P],
                                           zb[:, tt, k * P:(k + 1) * P], ident)
                ins.then_inc(turn_ps, 1)
                pe.wait_ge(c_sb, at(c_sb, l, 5))
                for tt in range(TT):
                    ins = pe.transpose(ps[:, 0, tt * P:(tt + 1) * P], zb[:, tt, BQ:BQ + BKV], ident)
                ins.then_inc(turn_ps, 1)
                pe.wait_ge(turn_act, at(turn_act, l, 3))
                pe.wait_ge(turn_dve, at(turn_dve, l, 2))
                for n in range(6):
                    qt = 0 if n < 2 else 1
                    odd = n % 2
                    if n == 0:
                        pe.wait_ge(c_sb, at(c_sb, l, 6))
                    r = slice(64 * odd, 64 * odd + 64)
                    for m in range(4 if qt == 0 else 2):
                        pair = m if qt == 0 else 2 * ((n - 2) // 2) + m
                        ins = mm(ps[:, 1 + n, m * keys(qt):(m + 1) * keys(qt)], iqT[r, pair, qt * P:(qt + 1) * P],
                                 keysT[r, 1, 0:keys(qt)])
                    ins.then_inc(idx_ps, 1)
                pe.wait_ge(up_in, at(up_in, l))
                pe.wait_ge(turn_dve, at(turn_dve, l, 5))
                uq = wup[:, 0:2 * H * (HD + BR)].rearrange("p (k h n) -> p k h n", k=2, h=H)
                ukv = wup[:, 2 * H * (HD + BR):NUP].rearrange("p (h n) -> p h n", h=H)
                for tt in range(TT):
                    for k in range(2):
                        ins = mm(ps[:, 7, tt * H * BR:(tt + 1) * H * BR].rearrange("p (h n) -> p h n", h=H),
                                 bcqT[:, k, tt * P:(tt + 1) * P], uq[:, k, :, HD:HD + BR], k == 0, k == 1)
                ins.then_inc(b_ps, 1)
                for n in range(2):
                    if n == 1:
                        pe.wait_ge(relu_sb, at(relu_sb, l, 1))
                    for m in range(2):
                        for k in range(2):
                            ins = mm(ps[:, n, m * T:(m + 1) * T], uq[:, k, 2 * n + m, 0:HD], bcqT[:, k, :],
                                     k == 0, k == 1)
                    ins.then_inc(b_ps, 1)
                for n in range(2):
                    pe.wait_ge(relu_sb, at(relu_sb, l, 2 + n))
                    for m in range(2):
                        ins = mm(ps[:, 2 + n, m * T:(m + 1) * T], ukv[:, 2 * n + m, 0:HD], bckvT[:])
                    ins.then_inc(b_ps, 1)
                for tt in range(TT):
                    pe.wait_ge(relu_sb, at(relu_sb, l, 4 + tt))
                    ins = mm(ps[:, 4 + tt, :].rearrange("p (h n) -> p h n", h=H), bckvT[:, tt * P:(tt + 1) * P],
                             ukv[:, :, HD:2 * HD])
                    ins.then_inc(b_ps, 1)
                pe.wait_ge(roped, at(roped, l, 6))
                pe.wait_ge(relu_sb, at(relu_sb, l, 6))
                for pair in range(2):
                    for tt in range(TT):
                        ins = pe.transpose(ps[:, 6, pair * T + tt * P:pair * T + (tt + 1) * P],
                                           zqr[:, tt, pair * P:(pair + 1) * P], ident)
                ins.then_inc(turn_ps, 1)
                pe.wait_ge(b_sb, at(b_sb, l, 1))
                for tt in range(TT):
                    ins = pe.transpose(ps[:, 7, tt * P:(tt + 1) * P], zkr[:, tt].rearrange("p a n -> p (a n)"), ident)
                ins.then_inc(turn_ps, 1)

                pe.wait_ge(b_sb, at(b_sb, l, 7))
                pe.wait_ge(turn_act, at(turn_act, l, 5))

                def scores(u):
                    m, qt = UNITS[u]
                    n = keys(qt)
                    q = slice(qt * P, (qt + 1) * P)
                    if u:
                        pe.wait_ge(logit_sb, at(logit_sb, l, u))
                    for pos in range(H):
                        out = ps[:, 2 + pos // 2, (pos % 2) * T:(pos % 2) * T + n]
                        h = HEAD_AT[m][pos]
                        if m == "a":
                            ins = mm(out, aqT[:, h, q], keysT[:, 0, 0:n])
                        elif m == "c":
                            ins = mm(out, cqT[:, h, q], ckT[:, h, 0:n])
                        else:
                            r = slice(64 * (h % 2), 64 * (h % 2) + 64)
                            mm(out, qnT[:, h, q], knT[:, h, 0:n], True, False)
                            ins = mm(out, qrT[r, h // 2, q], krT[r, 0:n], False, True)
                    ins.then_inc(score_ps, 1)

                def turn_probs(u):
                    m, qt = UNITS[u]
                    pe.wait_ge(probs_sb, at(probs_sb, l, u + 1))
                    if u:
                        pe.wait_ge(probsT_sb, at(probsT_sb, l, PT_COUNT[u - 1]))
                    for kt in range(qt + 1):
                        for pos in range(H):
                            ins = pe.transpose(ps[:, 4 + kt, pos * P:(pos + 1) * P],
                                               probs[:, pos, kt * P:(kt + 1) * P], ident)
                        ins.then_inc(probsT_ps, 1)

                def values(u):
                    m, qt = UNITS[u]
                    pe.wait_ge(probsT_sb, at(probsT_sb, l, PT_COUNT[u]))
                    if u:
                        pe.wait_ge(o_sb, at(o_sb, l, u))
                    if m == "a":
                        for kt in range(qt + 1):
                            ins = mm(ps[:, 6, :], zkv[:, kt, HD:2 * HD],
                                     probsT[:, kt].rearrange("p h q -> p (h q)"), kt == 0, kt == qt)
                    for pos in range(H) if m != "a" else ():
                        h = HEAD_AT[m][pos]
                        for kt in range(qt + 1):
                            v = {"b": vB[:, kt, h * HD:(h + 1) * HD],
                                 "c": cv[:, kt, h * HD:(h + 1) * HD]}[m]
                            ins = mm(ps[:, 6, pos * P:(pos + 1) * P], v, probsT[:, kt, pos, :], kt == 0, kt == qt)
                    ins.then_inc(o_ps, 1)

                for n in range(12):
                    if 1 <= n <= len(UNITS):
                        turn_probs(n - 1)
                    if n < len(UNITS):
                        scores(n)
                    if n >= 2:
                        pe.wait_ge(gate_sb, at(gate_sb, l, n - 1))
                    features_by(l, n % 2, 2 * B_GL + n).then_inc(half_ps, 1)
                    if 1 <= n <= len(UNITS):
                        values(n - 1)

                for n in range(2 * B_PROJ, 2 * B_WO):
                    j = (n - 2 * B_PROJ) // 2
                    o_hi, o_lo = o_parts[PROJ_ORDER[j]]
                    hi, lo = part_of(w_hi, n), part_of(w_lo, n)
                    pe.wait_ge(hi_made, at(hi_made, l, n + 1))
                    pe.wait_ge(o_hi_made, at(o_hi_made, l, j + 1))
                    pe.wait_ge(o_lo_made, at(o_lo_made, l, j + 1))

                    def tile(m, with_high, with_low):
                        out = ps[:, (2 * (n - 2 * B_PROJ) + m // 2) % 4, (m % 2) * T:(m % 2 + 1) * T]
                        c = slice(m * P, (m + 1) * P)
                        for h in range(H) if with_high else ():
                            mm(out, hi[:, h, c], o_hi[:, h, :], h == 0, False)
                            mm(out, hi[:, h, c], o_lo[:, h, :], False, False)
                        for h in range(H) if with_low else ():
                            ins = mm(out, lo[:, h, c], o_hi[:, h, :], False, h == H - 1)
                        return ins if with_low else None

                    for m in (0, 2):
                        pair = 2 * (n - 2 * B_PROJ) + m // 2
                        if pair < 2:
                            pe.wait_ge(gate_sb, at(gate_sb, l, 11 + pair))
                        elif pair < 4:
                            pe.wait_ge(logit_sb, at(logit_sb, l, 6))
                        else:
                            pe.wait_ge(proj_used, at(proj_used, l, pair - 3))
                        tile(m, True, False)
                    pe.wait_ge(lo_made, at(lo_made, l, n + 1))
                    tile(0, False, True)
                    tile(1, True, True).then_inc(proj_ps, 1)
                    tile(2, False, True)
                    tile(3, True, True).then_inc(half_ps, 1)
                for n in range(2 * B_WO, HALVES):
                    part, half = (n - 2 * B_WO) // 2, n % 2
                    hi, lo = part_of(w_hi, n), part_of(w_lo, n)
                    pe.wait_ge(hi_made, at(hi_made, l, n + 1))
                    pe.wait_ge(mix_hi_made, at(mix_hi_made, l, 2 * part + 2))
                    pe.wait_ge(mix_lo_made, at(mix_lo_made, l, 2 * part + 2))
                    for tt in range(TT):
                        out = ps[:, 4 + 2 * tt + half, :]
                        q = slice(tt * P, (tt + 1) * P)
                        for k in range(4):
                            mm(out, mix_hi[:, 4 * part + k, q], hi[:, k, :], part == 0 and k == 0, False)
                            mm(out, mix_lo[:, 4 * part + k, q], hi[:, k, :], False, False)
                        if tt == 0:
                            pe.wait_ge(lo_made, at(lo_made, l, n + 1))
                        for k in range(4):
                            ins = mm(out, mix_hi[:, 4 * part + k, q], lo[:, k, :], False, part == 1 and k == 3)
                        if tt == 0 and part:
                            ins.then_inc(wo_ps, 1)
                    ins.then_inc(half_ps, 1)

                pe.wait_ge(xn_dve, at(xn_dve, l, 3))
                for k in range(KC):
                    turn_chunk(k, 0)
                pe.wait_ge(xn_dve, at(xn_dve, l, 4))
                for k in range(KC):
                    if k == KC // 2:
                        pe.wait_ge(xn_act, at(xn_act, l, 1))
                    ins = turn_chunk(k, 1)
                    if k % 2:
                        ins.then_inc(xnT_ps, 1)
                        if k >= 3:
                            router_logits(l, k - 3)
                            router_logits(l, k - 2)
                router_logits(l, KC - 2)
                ins = router_logits(l, KC - 1)
                ins.then_inc(routerT_ps, 1)
                pe.wait_ge(routerT_sb, at(routerT_sb, l))
                for tt in range(TT):
                    ins = pe.transpose(ps[:, 6, tt * (G + E):(tt + 1) * (G + E)], routerT[:, tt * P:(tt + 1) * P],
                                       cst[0:G + E, C_ID:C_ID + G + E])
                ins.then_inc(route_ps, 1)
                pe.wait_ge(asg_sb, at(asg_sb, l))
                mm(ps[:, 5, 0:E], tri, asg[:, 0, :])
                mm(ps[:, 5, E:2 * E], ones, asg[:, 0, :], True, False)
                ins = mm(ps[:, 5, E:2 * E], tri, asg[:, 1, :], False, True)
                ins.then_inc(rank_ps, 1)
                mm(ps[:, 4, 0:E], ones, asg[:, 0, :], True, False)
                ins = mm(ps[:, 4, 0:E], ones, asg[:, 1, :], False, True)
                ins.then_inc(count_ps, 1)
                for tt in range(TT):
                    pe.wait_ge(sel_sb, at(sel_sb, l, tt + 1))
                gather(l, 0)

                def turn_weights():
                    for tt in range(TT):
                        pe.wait_ge(selw_sb, at(selw_sb, l, tt + 1))
                    for n, bank in enumerate(SELW_BANKS):
                        for m in range(2):
                            for tt in range(TT):
                                ins = pe.transpose(ps[:, bank, m * T + tt * P:m * T + (tt + 1) * P],
                                                   selws[tt][:, (2 * n + m) * P:(2 * n + m + 1) * P], ident)
                        ins.then_inc(selwT_ps, 1)

                def one_set(g, first, last):
                    gate_up(l, g, first, last)
                    if first:
                        turn_weights()
                    else:
                        combine(l, g - 1, 0, 6)
                    if last:
                        turn_hidden(l, g)
                    else:
                        gather(l, g + 1)
                    if not first:
                        combine(l, g - 1, 1, 0 if last else 6)
                    if first:
                        pe.wait_ge(selwT_sb, at(selwT_sb, l, 4))
                    if not last:
                        turn_hidden(l, g)
                    down(l, g, first, last)
                loop_sets(pe, one_set)
                combine(l, NG - 1, 0, 6)
                combine(l, NG - 1, 1, 4)
                late_products(l)

        @block.scalar
        def _(act):
            def copy(out, in_, scale=1.0):
                return act.activation(out, in_, ACT.Copy, scale=scale)

            def late_tanhs(l):
                with act.If(any_late(act, l)):
                    with act.Fori(0, NG) as g:
                        for j in range(XG):
                            e1 = XG * g + (j + 1)
                            act.wait_ge(late_gu_ps[l], at(late_gu_ps[l], 0, e1))
                            for tt in range(TT):
                                act.activation(thl[:, tt, :], ps[:, tt, 0:FE], ACT.Tanh, scale=0.5).then_inc(late_tanh[l], 1)
                            act.wait_ge(late_hidT_ps[l], at(late_hidT_ps[l], 0, e1))
                            act.activation(hidTl, ps[:, 2, :].rearrange("p (f t) -> p f t", f=2),
                                           ACT.Copy).then_inc(late_hidT_sb[l], 1)

            def square(l, n):
                tt, half = n // 2, n % 2
                act.activation(junk[:, n, :], x[:, tt, half * 512:(half + 1) * 512], ACT.Square, scale=D ** -0.5,
                               accum_out=st[:, 32 + n:33 + n]).then_inc(sums_act, 1)

            def high_part(l, n):
                s = n // 2 % WAYS
                act.wait_ge(slot_in[s], at(slot_in[s], l, n // 2 // WAYS + 1))
                if n >= 2:
                    act.wait_ge(half_ps, at(half_ps, l, n - 1))
                elif l:
                    act.wait_ge(down_ps, at(down_ps, l - 1))
                copy(part_of(w_hi, n), raw_half(n)).then_inc(hi_made, 1)

            def high_output(l, j, o):
                act.wait_ge(o_sb, at(o_sb, l, 2 * j + 2))
                if j == 2:
                    act.wait_ge(half_ps, at(half_ps, l, 2 * B_PROJ + 2))
                copy(o_parts[PROJ_ORDER[j]][0][:], o[:]).then_inc(o_hi_made, 1)

            def turned_norm(l, half):
                if half:
                    act.wait_ge(rstd_ready, at(rstd_ready, l, 4))
                    copy(xn[:, 1, D // 2:D], x[:, 1, D // 2:D], st[:, 9:10]).then_inc(xn_act, 1)
                if not l and not half:
                    act.wait_ge(consts_in, at(consts_in, 0, 2))
                for k in (2, 3, 6, 7) if half else range(KC):
                    act.wait_ge(xnT_ps, at(xnT_ps, l, 4 * half + k // 2 + 1))
                    gain = small[:, l, (S_GF if half else S_GA) + k:(S_GF if half else S_GA) + k + 1]
                    dst = hT if half else hT_hi
                    copy(dst[:, k, :], ps[:, k // 2, (k % 2) * T:(k % 2 + 1) * T], gain).then_inc(hT_act, 1)

            act.wait_ge(x_in, at(x_in, 0, 1))
            for l in range(L):
                if l:
                    high_part(l, 0)
                    high_part(l, 1)
                    act.wait_ge(late_settled, at(late_settled, l - 1, 1))
                for n in range(2):
                    square(l, n)
                turned_norm(l, 0)
                if not l:
                    high_part(l, 0)
                    high_part(l, 1)

                def next_high(n):
                    high_part(l, n)
                copy_tokens(act, l, 0, z_act, copy, next_high)
                for n in range(4):
                    high_part(l, 2 * B_CQ + n + 2)
                    act.wait_ge(half_ps, at(half_ps, l, 2 * B_CQ + n + 1))
                    dst = (cqT if n < 2 else ckT)[:, 2 * (n % 2):2 * (n % 2) + 2, :]
                    copy(dst, ps[:, 4 + n, :].rearrange("p (m t) -> p m t", m=2)).then_inc(c_sb, 1)
                for tt in range(TT):
                    high_part(l, 2 * B_CV + tt + 2)
                    act.wait_ge(half_ps, at(half_ps, l, 2 * B_CV + 2))
                    copy(cv[:, tt, :], ps[:, tt, :]).then_inc(c_sb, 1)
                act.wait_ge(turn_ps, at(turn_ps, l, 1))
                copy(aqT[:, :, 0:P], ps[:, 2, :].rearrange("p (h t) -> p h t", h=4)).then_inc(turn_act, 1)
                act.wait_ge(turn_ps, at(turn_ps, l, 3))
                copy(iqT[:, :, 0:P], ps[:, 4, :].rearrange("p (h t) -> p h t", h=4)).then_inc(turn_act, 1)
                act.wait_ge(turn_ps, at(turn_ps, l, 5))
                copy(keysT[:].rearrange("p s (t c) -> p t s c", c=P),
                     ps[:, 6, :].rearrange("p (t s c) -> p t s c", t=TT, s=2)).then_inc(turn_act, 1)
                for n in range(6):
                    act.wait_ge(idx_ps, at(idx_ps, l, n + 1))
                    if n >= 2:
                        act.wait_ge(idx_used, at(idx_used, l, n - 1))
                    else:
                        act.wait_ge(roped, at(roped, l, 5))
                    act.activation(relu[:, n % 2, :], ps[:, 1 + n, :], ACT.Relu).then_inc(relu_sb, 1)
                act.wait_ge(b_ps, at(b_ps, l, 1))
                copy(zqr, ps[:, 7, :].rearrange("p (a n) -> p a n", a=TT)).then_inc(b_sb, 1)
                for n in range(2):
                    act.wait_ge(b_ps, at(b_ps, l, 2 + n))
                    copy(qnT[:, 2 * n:2 * n + 2, :], ps[:, n, :].rearrange("p (m t) -> p m t", m=2)).then_inc(b_sb, 1)
                for n in range(2):
                    act.wait_ge(b_ps, at(b_ps, l, 4 + n))
                    copy(knT[:, 2 * n:2 * n + 2, :], ps[:, 2 + n, :].rearrange("p (m t) -> p m t", m=2)).then_inc(b_sb, 1)
                for tt in range(TT):
                    act.wait_ge(b_ps, at(b_ps, l, 6 + tt))
                    copy(vB[:, tt, :], ps[:, 4 + tt, :]).then_inc(b_sb, 1)
                act.wait_ge(turn_ps, at(turn_ps, l, 8))
                copy(qrT, ps[:, 6, :].rearrange("p (m t) -> p m t", m=2)).then_inc(turn_act, 1)
                act.wait_ge(turn_ps, at(turn_ps, l, 9))
                copy(krT, ps[:, 7, 0:T]).then_inc(turn_act, 1)

                for n in range(12):
                    if 1 <= n <= len(UNITS):
                        u = n - 1
                        m, qt = UNITS[u]
                        for kt in range(qt + 1):
                            act.wait_ge(probsT_ps, at(probsT_ps, l, (PT_COUNT[u - 1] if u else 0) + kt + 1))
                            if u:
                                act.wait_ge(o_ps, at(o_ps, l, u))
                            copy(probsT[:, kt], ps[:, 4 + kt, :].rearrange("p (h q) -> p h q", h=H)).then_inc(probsT_sb, 1)
                    if n < len(UNITS):
                        m, qt = UNITS[n]
                        act.wait_ge(nmax_sb, at(nmax_sb, l, n + 1))
                        if n:
                            act.wait_ge(probsT_ps, at(probsT_ps, l, PT_COUNT[n - 1]))
                        for pos in range(H):
                            act.activation(probs[:, pos, 0:keys(qt)], logits[:, pos, 0:keys(qt)], ACT.Exp,
                                           bias=st[:, 16 + pos:17 + pos], accum_out=st[:, 20 + pos:21 + pos]).then_inc(exp_sb, 1)
                    act.wait_ge(half_ps, at(half_ps, l, 2 * B_GL + n + 1))
                    if n == SCORE_GATE:
                        act.wait_ge(logit_sb, at(logit_sb, l, 6))
                    c = 2 * n
                    act.activation(gates[:, c:c + 2, :], ps[:, n % 2, :].rearrange("p (m t) -> p m t", m=2),
                                   ACT.Tanh, scale=0.5).then_inc(gate_sb, 1)
                    high_part(l, 2 * B_GL + n + 2)
                    if 1 <= n <= len(UNITS):
                        u = n - 1
                        m, qt = UNITS[u]
                        act.wait_ge(o_ps, at(o_ps, l, u + 1))
                        dst = {"a": aqT, "b": qnT, "c": cqT}[m]
                        src = ps[:, 6, :].rearrange("p (h q) -> p h q", h=H)
                        if m == "b":
                            dst = dst[:].rearrange("p (s o) t -> p o s t", o=2)[:, :, :, qt * P:(qt + 1) * P]
                            src = ps[:, 6, :].rearrange("p (o s q) -> p o s q", o=2, s=2)
                        else:
                            dst = dst[:, :, qt * P:(qt + 1) * P]
                        copy(dst, src).then_inc(o_sb, 1)
                    if n == 8:
                        high_output(l, 0, cqT)
                        high_output(l, 1, qnT)

                high_part(l, 2 * B_PROJ + 2)
                high_part(l, 2 * B_PROJ + 3)
                high_output(l, 2, aqT)
                for n in range(2 * B_PROJ + 4, HALVES):
                    high_part(l, n)
                    if n == 2 * B_WO or n == 2 * B_WO + 1:
                        for p in (0, 1) if n == 2 * B_WO else (2, 3):
                            act.wait_ge(proj_used, at(proj_used, l, 8 + p + 1))
                            copy(mix_hi[:, 2 * p:2 * p + 2, :], mixT[:, 2 * p:2 * p + 2, :]).then_inc(mix_hi_made, 1)

                for n, part in enumerate(ADDED):
                    act.wait_ge(x_added, at(x_added, l, n + 1))
                    square(l, part)
                turned_norm(l, 1)
                act.wait_ge(routerT_ps, at(routerT_ps, l))
                copy(routerT, ps[0:G + E, 4, 0:T]).then_inc(routerT_sb, 1)
                act.wait_ge(gdiff_sb, at(gdiff_sb, l, 1))
                act.activation(eg, eg, ACT.Exp).then_inc(gexp_sb, 1)
                act.wait_ge(gdiff_sb, at(gdiff_sb, l, 2))
                act.activation(rw[:, 1, :], rw[:, 0, :], ACT.Exp).then_inc(gexp_sb, 1)

                def one_set(g, first, last):
                    act.wait_ge(gu_ps, at(gu_ps, l, g + 1))
                    if not first:
                        act.wait_ge(hid_sb, at(hid_sb, l, g))
                    act.activation(th, ps[:, 2, 0:FE], ACT.Tanh, scale=0.5).then_inc(tanh_sb, 1)
                    if first:
                        for n, bank in enumerate(SELW_BANKS):
                            act.wait_ge(selwT_ps, at(selwT_ps, l, n + 1))
                            copy(selwT[:, 2 * n:2 * n + 2, :],
                                 ps[:, bank, :].rearrange("p (g t) -> p g t", g=2)).then_inc(selwT_sb, 1)
                        act.wait_ge(selwT_sb, at(selwT_sb, l, 4))
                    else:
                        act.wait_ge(comb_ps, at(comb_ps, l, 4 * g))
                    act.activation(sw, selwT[:, bass.ds(g, 1), :].rearrange("p g t -> p (g t)"),
                                   ACT.Copy).then_inc(sw_sb, 1)
                    act.wait_ge(hidT_ps, at(hidT_ps, l, g + 1))
                    copy(hidT, ps[:, 3, 0:2 * P].rearrange("p (f s) -> p f s", f=2)).then_inc(hidT_sb, 1)
                    for half in range(2):
                        if half:
                            act.wait_ge(down_ps, at(down_ps, l, g + 1))
                        else:
                            act.wait_ge(down_half, at(down_half, l, g + 1))
                            if not first:
                                act.wait_ge(comb_ps, at(comb_ps, l, 4 * g))
                        copy(yg[:, half * 512:(half + 1) * 512], ps[:, 4 + half, :]).then_inc(yg_sb, 1)
                loop_sets(act, one_set)
                late_tanhs(l)

            act.wait_ge(late_settled, at(late_settled, L - 1, 1))
            for n in range(2):
                square(L, n)

        @block.vector
        def _(dve):
            V = dve

            def copy(out, in_, scale=None):
                if scale is None:
                    return V.tensor_copy(out, in_)
                return V.tensor_scalar(out, in_, scale, None, ALU.mult)

            def route(l):
                V.wait_ge(route_ps, at(route_ps, l))
                V.wait_ge(rbias_in, at(rbias_in, 0, 1))
                V.tensor_tensor(lg, ps[:, 6, 0:2 * (G + E)].rearrange("p (a n) -> p a n", a=TT),
                                rbias[:, l, :].unsqueeze(1).to_broadcast([P, TT, G + E]), ALU.add).then_inc(step, 1)
                V.wait_ge(step, steps(1))
                V.memset(g8[:], REPL).then_inc(step, 1)
                V.wait_ge(step, steps(1))
                V.tensor_copy(g8[:, :, 0:G], lg[:, :, 0:G]).then_inc(step, 1)
                V.wait_ge(step, steps(1))
                for tt in range(TT):
                    V.max(m8[:, tt, :], g8[:, tt, :]).then_inc(step, 1)
                V.wait_ge(step, steps(2))
                for tt in range(TT):
                    V.max_index(i8[:, tt, :], m8[:, tt, :], g8[:, tt, :]).then_inc(step, 1)
                V.wait_ge(step, steps(2))
                V.tensor_copy(fi[:, :, 0:1], i8[:, :, 0:1]).then_inc(step, 1)
                V.tensor_tensor(eg, lg[:, :, 0:G], m8[:, :, 0:1].to_broadcast([P, TT, G]), ALU.subtract).then_inc(step, 1)
                V.wait_ge(step, steps(2))
                V.tensor_tensor(ohg, iota[:, 0:G].unsqueeze(1).to_broadcast([P, TT, G]),
                                fi[:, :, 0:1].to_broadcast([P, TT, G]), ALU.is_equal).then_inc(gdiff_sb, 1)
                V.wait_ge(gdiff_sb, at(gdiff_sb, l, 1))
                for tt in range(TT):
                    V.tensor_tensor(prod[:, tt, :].rearrange("p (g e) -> p g e", g=G),
                                    lg[:, tt, G:G + E].rearrange("p (g e) -> p g e", g=G),
                                    ohg[:, tt, :].unsqueeze(2).to_broadcast([P, G, EPG]), ALU.mult).then_inc(step, 1)
                V.wait_ge(step, steps(2))
                for tt in range(TT):
                    V.tensor_reduce(ein[:, tt, :], prod[:, tt, :].rearrange("p (g e) -> p e g", g=G),
                                    AX_X, ALU.add).then_inc(step, 1)
                V.wait_ge(step, steps(2))
                for tt in range(TT):
                    V.max(e8[:, tt, :], ein[:, tt, :]).then_inc(step, 1)
                V.wait_ge(step, steps(2))
                for tt in range(TT):
                    V.max_index(j8[:, tt, :], e8[:, tt, :], ein[:, tt, :]).then_inc(step, 1)
                V.wait_ge(step, steps(2))
                V.tensor_copy(fi[:, :, 1:3], j8[:, :, 0:2]).then_inc(step, 1)
                V.wait_ge(step, steps(1))
                V.tensor_tensor(rw[:, 0, :], e8[:, :, 1], e8[:, :, 0], ALU.subtract).then_inc(gdiff_sb, 1)
                V.tensor_tensor(oh1, iota[:, 0:EPG].unsqueeze(1).to_broadcast([P, TT, EPG]),
                                fi[:, :, 1:2].to_broadcast([P, TT, EPG]), ALU.is_equal).then_inc(step, 1)
                V.tensor_tensor(oh2, iota[:, 0:EPG].unsqueeze(1).to_broadcast([P, TT, EPG]),
                                fi[:, :, 2:3].to_broadcast([P, TT, EPG]), ALU.is_equal).then_inc(step, 1)
                V.wait_ge(step, steps(2))
                V.tensor_tensor(ce, oh1, oh2, ALU.add).then_inc(step, 1)
                V.wait_ge(step, steps(1))
                for tt in range(TT):
                    last = V.tensor_tensor(asg[:, tt, :].rearrange("p (g e) -> p g e", g=G),
                                           ohg[:, tt, :].unsqueeze(2).to_broadcast([P, G, EPG]),
                                           ce[:, tt, :].unsqueeze(1).to_broadcast([P, G, EPG]), ALU.mult)
                    if tt == 0:
                        last.then_inc(step, 1)
                        V.wait_ge(step, steps(1))
                last.then_inc(asg_sb, 1)
                V.wait_ge(gexp_sb, at(gexp_sb, l, 2))
                V.tensor_reduce(rw[:, 2, :], eg, AX_X, ALU.add).then_inc(step, 1)
                V.tensor_scalar(rw[:, 3, :], rw[:, 1, :], 1.0, None, ALU.add).then_inc(step, 1)
                V.wait_ge(step, steps(2))
                V.tensor_tensor(rw[:, 4, :], rw[:, 2, :], rw[:, 3, :], ALU.mult).then_inc(step, 1)
                V.wait_ge(step, steps(1))
                V.reciprocal(rw[:, 5, :], rw[:, 4, :]).then_inc(step, 1)
                V.wait_ge(step, steps(1))
                V.tensor_scalar(rw[:, 6, :], rw[:, 5, :], 0.5, None, ALU.mult).then_inc(step, 1)
                V.wait_ge(step, steps(1))
                V.tensor_tensor(rw[:, 7, :], rw[:, 6, :], rw[:, 1, :], ALU.mult).then_inc(step, 1)
                V.wait_ge(step, steps(1))
                V.tensor_tensor(oh1, oh1, rw[:, 6, :].unsqueeze(2).to_broadcast([P, TT, EPG]), ALU.mult).then_inc(step, 1)
                V.tensor_tensor(oh2, oh2, rw[:, 7, :].unsqueeze(2).to_broadcast([P, TT, EPG]), ALU.mult).then_inc(step, 1)
                V.wait_ge(step, steps(2))
                V.tensor_tensor(ce, oh1, oh2, ALU.add).then_inc(step, 1)
                V.wait_ge(step, steps(1))
                for tt in range(TT):
                    V.tensor_tensor(comb[:, tt, :].rearrange("p (g e) -> p g e", g=G),
                                    ohg[:, tt, :].unsqueeze(2).to_broadcast([P, G, EPG]),
                                    ce[:, tt, :].unsqueeze(1).to_broadcast([P, G, EPG]), ALU.mult).then_inc(step, 1)
                V.wait_ge(step, steps(2))
                V.wait_ge(rank_ps, at(rank_ps, l))
                V.wait_ge(asg_sb, at(asg_sb, l))
                V.scalar_tensor_tensor(rk, ps[:, 5, 0:2 * E].rearrange("p (a n) -> p a n", a=TT), 1.0,
                                       asg, ALU.add, ALU.mult).then_inc(step, 1)
                V.wait_ge(step, steps(1))
                V.tensor_scalar(rk, rk, -1.0, None, ALU.add).then_inc(step, 1)
                V.wait_ge(step, steps(1))
                for lo, hi in ((0, XG), (XG, E)):
                    for tt in range(TT):
                        V.tensor_tensor(sel[:, tt, lo * SLOTS:hi * SLOTS].rearrange("p (e s) -> p e s", e=hi - lo),
                                        iota.unsqueeze(1).to_broadcast([P, hi - lo, SLOTS]),
                                        rk[:, tt, lo:hi].unsqueeze(2).to_broadcast([P, hi - lo, SLOTS]),
                                        ALU.is_equal).then_inc(sel_sb, 1)
                for tt in range(TT):
                    V.wait_ge(sel_sb, at(sel_sb, l, TT + tt + 1))
                    V.tensor_tensor(selws[tt].rearrange("p (e s) -> p e s", e=E),
                                    sel[:, tt, :].rearrange("p (e s) -> p e s", e=E),
                                    comb[:, tt, :].unsqueeze(2).to_broadcast([P, E, SLOTS]), ALU.mult).then_inc(selw_sb, 1)
                V.tensor_scalar(late, rk, LATE_FROM - 0.5, None, ALU.is_gt).then_inc(step, 1)
                V.wait_ge(count_ps, at(count_ps, l))
                V.tensor_reduce(cnt, ps[:, 4, 0:E], AX_X, ALU.max).then_inc(step, 1)
                V.wait_ge(step, steps(2))
                V.tensor_tensor(late, late, comb, ALU.mult).then_inc(step, 1)
                V.wait_ge(step, steps(1))
                V.tensor_scalar(flag[:], cnt, LATE_FROM + 0.5, None, ALU.is_gt).then_inc(flag_sb, 1)

            def late_sums(l, late_flag):
                with V.If(late_flag > 0):
                    V.wait_ge(late_xnT_ps[l], at(late_xnT_ps[l], 0, 1))
                    for k in range(KC):
                        copy(hT[:, k, :], ps[:, k // 2, (k % 2) * T:(k % 2 + 1) * T],
                             small[:, l, S_GF + k:S_GF + k + 1]).then_inc(late_hT[l], 1)
                    with V.Fori(0, NG) as g:
                        for j in range(XG):
                            for tt in range(TT):
                                n = TT * XG * g + (TT * j + tt + 1)
                                V.wait_ge(late_tanh[l], at(late_tanh[l], 0, n))
                                V.scalar_tensor_tensor(thl[:, tt, :], thl[:, tt, :], 1.0, ps[:, tt, 0:FE],
                                                       ALU.add, ALU.mult).then_inc(late_silu[l], 1)
                                V.wait_ge(late_silu[l], at(late_silu[l], 0, n))
                                w = late[:, tt, bass.ds(XG * g + j, 1)]
                                V.scalar_tensor_tensor(hidl[:, tt, :], thl[:, tt, :], w, ps[:, tt, FE:2 * FE],
                                                       ALU.mult, ALU.mult).then_inc(late_hid[l], 1)
                            V.wait_ge(late_done[l], at(late_done[l], 0, XG * g + (j + 2)))
                            for n in range(4):
                                xs = x[:, n // 2, (n % 2) * 512:(n % 2 + 1) * 512]
                                ins = V.tensor_tensor(xs, xs, ps[:, 4 + n, :], ALU.add)
                                ins.then_inc(late_added[l], 1)
                            V.wait_ge(late_added[l], at(late_added[l], 0, 4 * XG * g + 4 * (j + 1)))

            def mean_square(l):
                for n in (2, 3):
                    xs = x[:, 1, (n - 2) * 512:(n - 1) * 512]
                    V.tensor_tensor_reduce(junk[:, n, :], xs, xs, 1.0 / D, 0.0,
                                           ALU.mult, ALU.add, st[:, 32 + n:33 + n]).then_inc(step, 1)
                V.wait_ge(step, steps(2))
                V.wait_ge(sums_act, at(sums_act, l, 2))
                sums = st[:, 32:36].rearrange("p (a n) -> p n a", a=TT)
                V.scalar_tensor_tensor(st[:, 0:2], sums[:, 0, :], EPS, sums[:, 1, :], ALU.add, ALU.add).then_inc(var_ready, 1)

            def tile_rstd(l, tt):
                V.wait_ge(sums_act, at(sums_act, l, tt + 5))
                s0 = 32 + 2 * tt
                V.scalar_tensor_tensor(st[:, tt:tt + 1], st[:, s0:s0 + 1], EPS, st[:, s0 + 1:s0 + 2],
                                       ALU.add, ALU.add).then_inc(var_ready, 1)
                V.wait_ge(rstd_ready, at(rstd_ready, l, tt + 3))

            def norm(l, half):
                if half:
                    tile_rstd(l, 1)
                    V.tensor_scalar(xe[1][:, 0:D // 2], x[:, 1, 0:D // 2], st[:, 9:10], None, ALU.mult).then_inc(xn_dve, 1)
                else:
                    mean_square(l)
                    V.wait_ge(rstd_ready, at(rstd_ready, l, 1))
                    for tt in range(TT):
                        V.tensor_scalar(xn[:, tt, :], x[:, tt, :], st[:, 8 + tt:9 + tt], None, ALU.mult).then_inc(xn_dve, 1)
                if not l and not half:
                    V.wait_ge(consts_in, at(consts_in, 0, 2))
                for k in (0, 1, 4, 5) if half else range(KC):
                    gain = small[:, l, (S_GF if half else S_GA) + k:(S_GF if half else S_GA) + k + 1]
                    if not half:
                        V.wait_ge(hT_act, at(hT_act, l, 2 * (k // 2) + 2))
                        V.scalar_tensor_tensor(hT_lo[:, k, :], ps[:, k // 2, (k % 2) * T:(k % 2 + 1) * T], gain,
                                               hT_hi[:, k, :].bitcast(F32), ALU.mult, ALU.subtract).then_inc(hT_dve, 1)
                        continue
                    V.wait_ge(xnT_ps, at(xnT_ps, l, 4 + k // 2 + 1))
                    copy(hT[:, k, :], ps[:, k // 2, (k % 2) * T:(k % 2 + 1) * T], gain).then_inc(hT_dve, 1)

            def rope(l, k, view, n, rot, oc, os):
                if k:
                    V.wait_ge(roped, at(roped, l, k))
                size = TT * n * rot
                t1 = rope1[:, 0:size].rearrange("p (a n r) -> p a n r", a=TT, n=n)
                t2 = rope2[:, 0:size].rearrange("p (a n r) -> p a n r", a=TT, n=n)
                cos = cst[:, oc:oc + TT * rot].rearrange("p (a r) -> p a r", a=TT).unsqueeze(2)
                sin = cst[:, os:os + TT * rot].rearrange("p (a r) -> p a r", a=TT).unsqueeze(2)
                hf = rot // 2
                z = view[:, :, :, 0:rot]
                V.tensor_tensor(t1, z, cos.to_broadcast([P, TT, n, rot]), ALU.mult).then_inc(step, 1)
                V.tensor_tensor(t2[:, :, :, 0:hf], z[:, :, :, hf:rot],
                                sin[:, :, :, 0:hf].to_broadcast([P, TT, n, hf]), ALU.mult).then_inc(step, 1)
                V.tensor_tensor(t2[:, :, :, hf:rot], z[:, :, :, 0:hf],
                                sin[:, :, :, hf:rot].to_broadcast([P, TT, n, hf]), ALU.mult).then_inc(step, 1)
                V.wait_ge(step, steps(3))
                V.tensor_tensor(z, t1, t2, ALU.add).then_inc(roped, 1)

            def heads(t, n):
                return t.rearrange("p a (n r) -> p a n r", n=n)

            def index_score(l, qt):
                n = keys(qt)
                out = score[:, qt, 0:n]
                first = True
                for b in (range(2) if qt == 0 else range(2, 6)):
                    V.wait_ge(relu_sb, at(relu_sb, l, b + 1))
                    count = 4 if qt == 0 else 2
                    for m in range(count):
                        pair = m if qt == 0 else 2 * ((b - 2) // 2) + m
                        h = 2 * pair + b % 2
                        r = relu[:, b % 2, m * n:(m + 1) * n]
                        w = ziw[:, qt, h:h + 1]
                        if first:
                            ins = V.tensor_scalar(out, r, w, None, ALU.mult)
                        else:
                            ins = V.scalar_tensor_tensor(out, r, w, out, ALU.mult, ALU.add)
                        first = False
                        if m == count - 1:
                            ins.then_inc(idx_used, 1)
                            V.wait_ge(idx_used, at(idx_used, l, b + 1))
                        else:
                            ins.then_inc(step, 1)
                            V.wait_ge(step, steps(1))
                V.tensor_tensor(out, out, mask_of(qt), ALU.add).then_inc(step, 1)
                V.wait_ge(step, steps(1))

            def top_keys(qt):
                out = score[:, qt, 0:keys(qt)]
                for _ in range(TOPK // 8):
                    V.max(st8[:], out).then_inc(step, 1)
                    V.wait_ge(step, steps(1))
                    V.match_replace(out, st8[:], out, REPL).then_inc(step, 1)
                    V.wait_ge(step, steps(1))
                V.tensor_scalar(out, out, REPL / 2, NEG, ALU.is_gt, ALU.mult).then_inc(step, 1)
                V.wait_ge(step, steps(1))

            def low_output(l, j, o):
                hi, lo = o_parts[PROJ_ORDER[j]]
                V.wait_ge(o_hi_made, at(o_hi_made, l, j + 1))
                V.tensor_tensor(lo[:], o[:], hi[:].bitcast(F32), ALU.subtract).then_inc(o_lo_made, 1)

            def softmax(l, u):
                m, qt = UNITS[u]
                n = keys(qt)
                V.wait_ge(score_ps, at(score_ps, l, u + 1))
                if u:
                    V.wait_ge(exp_sb, at(exp_sb, l, 4 * u))
                src = ps[:, 2:4, :].rearrange("p b (s k) -> p (b s) k", k=T)[:, :, 0:n]
                if m == "c":
                    if u == 0:
                        V.wait_ge(cb_masked, at(cb_masked, l))
                    bias = cbias[:, :, P:2 * P] if qt == 0 else cbias[:]
                elif m == "b":
                    bias = mask_of(qt).unsqueeze(1).to_broadcast([P, H, n])
                else:
                    bias = score[:, qt, 0:n].unsqueeze(1).to_broadcast([P, H, n])
                scale = {"a": HD ** -0.5, "b": (HD + BR) ** -0.5, "c": HD ** -0.5}[m]
                V.scalar_tensor_tensor(logits[:, :, 0:n], src, scale, bias, ALU.mult, ALU.add).then_inc(logit_sb, 1)
                V.wait_ge(logit_sb, at(logit_sb, l, u + 1))
                V.tensor_reduce(st[:, 16:20], logits[:, :, 0:n], AX_X, ALU.max, negate=True).then_inc(nmax_sb, 1)
                V.wait_ge(exp_sb, at(exp_sb, l, 4 * u + 4))
                if u:
                    V.wait_ge(probs_sb, at(probs_sb, l, u))
                V.reciprocal(st[:, 24:28], st[:, 20:24]).then_inc(step, 1)
                V.wait_ge(step, steps(1))
                r = st[:, 24:28].unsqueeze(2).to_broadcast([P, H, n])
                V.tensor_tensor(probs[:, :, 0:n], probs[:, :, 0:n], r, ALU.mult).then_inc(probs_sb, 1)

            V.wait_ge(x_in, at(x_in, 0, 1))
            for l in range(L):
                norm(l, 0)
                if not l:
                    V.wait_ge(hi_made, at(hi_made, 0, 1))
                    V.tensor_tensor(part_of(w_lo, 0), raw_half(0), part_of(w_hi, 0).bitcast(F32),
                                    ALU.subtract).then_inc(lo_made, 1)
                copy_tokens(V, l, 1, z_dve, copy)
                V.wait_ge(z_act, at(z_act, l))
                V.wait_ge(z_dve, at(z_dve, l))
                rope(l, 0, heads(zaq, H), H, A_ROT, C_CA, C_SA)
                rope(l, 1, heads(zkv[:], 2)[:, :, 0:1, :], 1, A_ROT, C_CA, C_SA)
                rope(l, 2, heads(ziq, IH), IH, I_ROT, C_CI, C_SI)
                rope(l, 3, zik, 2, I_ROT, C_CI, C_SI)
                rope(l, 4, zkr, 2, BR, C_CB, C_SB)
                V.tensor_scalar(ziw, ziw, float(IH ** -0.5 * ID ** -0.5), None, ALU.mult).then_inc(step, 1)
                V.wait_ge(step, steps(1))
                squares = rope1[:, 0:BQ]
                V.wait_ge(roped, at(roped, l, 5))
                for n, (o, w) in enumerate(((0, BQ), (BQ, BKV))):
                    for tt in range(TT):
                        V.tensor_tensor_reduce([squares, rope2][tt][:, 0:w], zb[:, tt, o:o + w], zb[:, tt, o:o + w], 1.0,
                                               0.0, ALU.mult, ALU.add, st[:, 28 + 2 * n + tt:29 + 2 * n + tt]).then_inc(step, 1)
                    V.wait_ge(step, steps(2))
                V.tensor_scalar(st[:, 4:6], st[:, 28:30], 1.0 / BQ, EPS, ALU.mult, ALU.add).then_inc(step, 1)
                V.wait_ge(step, steps(1))
                V.tensor_scalar(st[:, 6:8], st[:, 30:32], 1.0 / BKV, EPS, ALU.mult, ALU.add).then_inc(var_ready, 1)
                V.wait_ge(rstd_ready, at(rstd_ready, l, 2))
                for n, (o, w) in enumerate(((0, BQ), (BQ, BKV))):
                    for tt in range(TT):
                        V.tensor_scalar(zb[:, tt, o:o + w], zb[:, tt, o:o + w],
                                        st[:, 12 + 2 * n + tt:13 + 2 * n + tt], None, ALU.mult).then_inc(bn_ready, 1)
                V.wait_ge(turn_ps, at(turn_ps, l, 2))
                copy(aqT[:, :, P:2 * P], ps[:, 3, :].rearrange("p (h t) -> p h t", h=4)).then_inc(turn_dve, 1)
                V.wait_ge(turn_ps, at(turn_ps, l, 4))
                copy(iqT[:, :, P:2 * P], ps[:, 5, :].rearrange("p (h t) -> p h t", h=4)).then_inc(turn_dve, 1)
                V.wait_ge(turn_ps, at(turn_ps, l, 6))
                for k in range(2):
                    copy(bcqT[:, k, :], ps[:, 7, k * T:(k + 1) * T], small[:, l, S_GQ + k:S_GQ + k + 1]).then_inc(turn_dve, 1)
                V.wait_ge(turn_ps, at(turn_ps, l, 7))
                copy(bckvT[:], ps[:, 0, 0:T], small[:, l, S_GKV:S_GKV + 1]).then_inc(turn_dve, 1)
                index_score(l, 0)
                index_score(l, 1)
                V.wait_ge(b_sb, at(b_sb, l, 1))
                rope(l, 5, heads(zqr, H), H, BR, C_CB, C_SB)
                for u in range(len(UNITS)):
                    softmax(l, u)
                    if u < TT:
                        top_keys(u)
                low_output(l, 0, cqT)
                low_output(l, 1, qnT)
                for n in range(12):
                    m, c = PROJ_ORDER[n // 4], 2 * (n % 4)
                    if n % 2:
                        V.wait_ge(half_ps, at(half_ps, l, 2 * B_PROJ + n // 2 + 1))
                    else:
                        V.wait_ge(proj_ps, at(proj_ps, l, n // 2 + 1))
                    if n == 0:
                        V.wait_ge(gate_sb, at(gate_sb, l))
                        V.wait_ge(o_ps, at(o_ps, l))
                    g = gates[:, KC * "abc".index(m) + c:KC * "abc".index(m) + c + 2, :]
                    src = ps[:, n % 4, :].rearrange("p (m t) -> p m t", m=2)
                    dst = mixT[:, c:c + 2, :]
                    if n < 4:
                        V.scalar_tensor_tensor(dst, g, 1.0, src, ALU.add, ALU.mult).then_inc(proj_used, 1)
                    else:
                        V.scalar_tensor_tensor(g, g, 1.0, src, ALU.add, ALU.mult).then_inc(step, 1)
                        V.wait_ge(step, steps(1))
                        if n == 4:
                            V.wait_ge(proj_used, at(proj_used, l, 4))
                        elif n == 8:
                            V.wait_ge(proj_used, at(proj_used, l, 8))
                        V.tensor_tensor(dst, dst, g, ALU.add).then_inc(proj_used, 1)
                    if n == 5:
                        low_output(l, 2, aqT)
                    if n == 9 or n == 11:
                        for p in (n - 9, n - 8):
                            V.wait_ge(mix_hi_made, at(mix_hi_made, l, p + 1))
                            V.tensor_tensor(mix_lo[:, 2 * p:2 * p + 2, :], mixT[:, 2 * p:2 * p + 2, :],
                                            mix_hi[:, 2 * p:2 * p + 2, :].bitcast(F32),
                                            ALU.subtract).then_inc(mix_lo_made, 1)
                for n, part in enumerate(ADDED):
                    tt, half = part // 2, part % 2
                    if tt:
                        V.wait_ge(half_ps, at(half_ps, l, HALVES - 1 + half))
                    else:
                        V.wait_ge(wo_ps, at(wo_ps, l, half + 1))
                    xs = x[:, tt, half * 512:(half + 1) * 512]
                    V.scalar_tensor_tensor(xs, ps[:, 4 + part, :], 0.5, xs, ALU.mult, ALU.add).then_inc(x_added, 1)
                    if n == 2:
                        tile_rstd(l, 0)
                        V.tensor_scalar(xe[0], x[:, 0, :], st[:, 8:9], None, ALU.mult).then_inc(xn_dve, 1)
                norm(l, 1)
                route(l)

                def hidden(g, first):
                    V.wait_ge(tanh_sb, at(tanh_sb, l, g + 1))
                    V.scalar_tensor_tensor(th, th, 1.0, ps[:, 2, 0:FE], ALU.add, ALU.mult).then_inc(silu_sb, 1)
                    if not first:
                        V.wait_ge(hidT_ps, at(hidT_ps, l, g))
                    V.wait_ge(silu_sb, at(silu_sb, l, g + 1))
                    V.tensor_tensor(hid, th, ps[:, 2, FE:2 * FE], ALU.mult).then_inc(hid_sb, 1)

                def gathered(g):
                    for q in range(2):
                        V.wait_ge(gath_ps, at(gath_ps, l, 2 * g + q + 1))
                        gain = small[:, l, S_GF + 4 * q:S_GF + 4 * q + 4].unsqueeze(2).to_broadcast([P, 4, P])
                        V.tensor_tensor(xg[:, 4 * q:4 * q + 4, :],
                                        ps[:, q, :].rearrange("p (k s) -> p k s", k=4), gain, ALU.mult).then_inc(xg_sb, 1)

                def add_back(g, tt, bank):
                    for half in range(2):
                        V.wait_ge(comb_ps, at(comb_ps, l, 4 * g + (2 * tt + half + 1)))
                        xs = x[:, tt, half * 512:(half + 1) * 512]
                        V.wait_ge(x_added, at(x_added, l, 4 * g + (2 * tt + half + 1)))
                        V.tensor_tensor(xs, xs, ps[:, bank + half, :], ALU.add).then_inc(x_added, 1)

                gathered(0)
                V.wait_ge(flag_sb, at(flag_sb, l))
                late_flag = V.value_load(flag[0:1, 0:1], min_val=0, max_val=1)

                def one_set(g, first, last):
                    hidden(g, first)
                    if not first:
                        add_back(g - 1, 0, 6)
                    if not last:
                        V.wait_ge(gu_ps, at(gu_ps, l, g + 1))
                        gathered(g + 1)
                    if not first:
                        add_back(g - 1, 1, 0 if last else 6)
                loop_sets(V, one_set)
                add_back(NG - 1, 0, 6)
                add_back(NG - 1, 1, 4)
                V.wait_ge(x_added, at(x_added, l))
                late_sums(l, late_flag)
                V.sem_inc(late_settled, 1)

            mean_square(L)
            V.wait_ge(rstd_ready, at(rstd_ready, L, 1))
            V.wait_ge(fgain_in, at(fgain_in, 0, 1))
            for tt in range(TT):
                V.scalar_tensor_tensor(outs[tt], x[:, tt, :], st[:, 8 + tt:9 + tt], fgain,
                                       ALU.mult, ALU.mult).then_inc(out_ready, 1)


def blocks(w, k):
    return w.reshape(k, P, -1).transpose(1, 0, 2).reshape(P, -1)


def kernel(**inputs):
    import concourse.bacc as _bacc
    from concourse.bass_utils import run_bass_kernel_spmd as _run

    i = {k: np.asarray(v) for k, v in inputs.items()}
    stream = np.zeros((L * PER_LAYER, P, BLK), np.float32)
    small = np.zeros((L, P, NSMALL), np.float32)
    up = np.zeros((L, P, NUP), np.float32)
    for l in range(L):
        s = stream[l * PER_LAYER:(l + 1) * PER_LAYER]
        win = i["w_in"][l]
        for n, (lo, hi) in enumerate(TOKEN_BLOCKS + [(c, c + 512) for c in range(O_CQ, N_IN, 512)]):
            s[n, :, :KC * (hi - lo)] = blocks(win[:, lo:hi], KC)
        for n, m in enumerate(PROJ_ORDER):
            s[B_PROJ + n] = blocks(i[f"w_proj_{m}"][l], 4)
        for n in range(2):
            s[B_WO + n] = blocks(i["w_out"][l][n * 512:(n + 1) * 512], 4)
        for g in range(NG):
            for n, (kind, j) in enumerate(SET_ORDER):
                e = XG * g + j
                if kind == "gu":
                    w = blocks(np.concatenate([i["w_gate"][l, e], i["w_up"][l, e]], 1), KC)
                else:
                    w = blocks(i["w_down"][l, e:e + 2].reshape(2 * FE, D), 4)
                s[NT + PER_SET * g + n] = w
        small[l, :, S_GA:S_GA + KC] = i["attn_norm_g"][l].reshape(KC, P).T
        small[l, :, S_GF:S_GF + KC] = i["ffn_norm_g"][l].reshape(KC, P).T
        small[l, :, S_GQ:S_GQ + 2] = i["b_q_norm_g"][l].reshape(2, P).T
        small[l, :, S_GKV] = i["b_kv_norm_g"][l]
        small[l, :, S_R:] = blocks(np.concatenate([i["w_group"][l], i["w_router"][l]], 1), KC)
        up[l] = np.concatenate([blocks(i["b_w_uq"][l], 2), i["b_w_ukv"][l]], 1)
    at = np.minimum(P + np.arange(P)[:, None] - np.arange(T)[None, :], REL) + REL
    rel = i["c_rel_bias"][:, :, at].transpose(0, 2, 1, 3).reshape(L, P, H * T)
    arrays = {
        "x": i["x"], "consts": shape_constants(), "stream": stream, "small": small, "up": up,
        "rel": np.ascontiguousarray(rel), "final_gain": i["final_norm_g"],
        "rbias": np.concatenate([i["b_group"], i["b_router"]], 1),
    }
    nc = _bacc.Bacc("TRN2", target_bir_lowering=False, num_devices=1)
    a = {n: nc.dram_tensor(f"in_{n}", v.shape, mybir.dt.from_np(v.dtype), kind="ExternalInput").ap()
         for n, v in arrays.items()}
    a["out"] = nc.dram_tensor("out_dram", (1, T, D), F32, kind="ExternalOutput").ap()
    build(nc, a)
    r = _run(nc, [{f"in_{n}": v for n, v in arrays.items()}], core_ids=[0])
    return r.results[0]["out_dram"]
```
